# Optimizing a Trainium2 kernel written in Bass

```python
import jax
import jax.numpy as jnp
from jax import lax
import numpy as np

D_MODEL = 1024
BATCH = 1
SEQ = 512
DEPTH = 1
DEC_BATCH = 1
DEC_SEQ = 32
PAST_LEN = 256

CHUNK = 64
D_HGRN = D_MODEL
HGRN_EXPAND = 128
HGRN_HEADS = D_HGRN // HGRN_EXPAND
HGRN_DK = HGRN_EXPAND
HGRN_DV = D_HGRN // HGRN_HEADS
HGRN_BLOCK = CHUNK // 4
D_RWKV = D_MODEL
RWKV_HEAD = 64
RWKV_HEADS = D_RWKV // RWKV_HEAD
DECAY_LORA = max(32, int(round(1.8 * D_RWKV ** 0.5 / 32)) * 32)
ICL_LORA = max(32, int(round(1.8 * D_RWKV ** 0.5 / 32)) * 32)
GATE_LORA = max(32, int(round(0.6 * D_RWKV ** 0.8 / 32)) * 32)
RWKV_GN_EPS = 64e-5
N_RWKV_IN = 3 * D_RWKV + DECAY_LORA + ICL_LORA + GATE_LORA
N_IN = 4 * D_HGRN + N_RWKV_IN + 2 * D_MODEL
N_MEM = 256
X_HEADS = 4
X_HEAD_DIM = D_MODEL // X_HEADS
N_GROUPS = 4
EXPERTS_PER_GROUP = 8
N_EXPERTS = N_GROUPS * EXPERTS_PER_GROUP
TOP_K = 2
D_EXPERT = D_MODEL // 4
NORM_EPS = 1e-6

kernel_name = 'hgrn2_rwkv7_memxattn_hmoe_stream_step'

def rmsnorm(x, g):
    xf = x.astype(jnp.float32)
    y = xf * lax.rsqrt(jnp.mean(xf * xf, axis=-1, keepdims=True) + NORM_EPS)
    return (y * g.astype(jnp.float32)).astype(x.dtype)

def hgrn2_blocked(q, k, g, v, s0):
    B, T, H, _ = q.shape
    DV = v.shape[-1]
    L = HGRN_BLOCK
    pad = (-T) % L
    n = (T + pad) // L

    def blocks(t):
        t = jnp.pad(t.astype(jnp.float32), ((0, 0), (0, pad), (0, 0), (0, 0)))
        return t.reshape(B, n, L, H, t.shape[-1]).transpose(1, 0, 3, 2, 4)

    causal = jnp.tril(jnp.ones((L, L), dtype=bool))

    def step(S, blk):
        qb, kb, gb, vb = blk
        b = jnp.cumsum(gb, axis=2)
        b_last = b[:, :, -1:, :]
        q_dec = qb * jnp.exp(b)
        scores = jnp.einsum('bhld,bhmd->bhlm', q_dec, kb * jnp.exp(-b))
        scores = jnp.where(causal, scores, 0.0)
        o = jnp.einsum('bhlm,bhmv->bhlv', scores, vb) + jnp.einsum('bhld,bhdv->bhlv', q_dec, S)
        S = (jnp.exp(b_last[:, :, 0, :])[..., None] * S
             + jnp.einsum('bhld,bhlv->bhdv', kb * jnp.exp(b_last - b), vb))
        return S, o

    S, o = lax.scan(step, s0.astype(jnp.float32), (blocks(q), blocks(k), blocks(g), blocks(v)))
    o = o.transpose(1, 0, 3, 2, 4).reshape(B, n * L, H, DV)[:, :T]
    return o, S

def rwkv7_scan(r, w, k, v, a, b, s0):
    time_major = lambda t: jnp.moveaxis(t.astype(jnp.float32), 1, 0)

    def step(S, inp):
        rt, wt, kt, vt, at, bt = inp
        sa = jnp.einsum('bhvk,bhk->bhv', S, at)
        S = S * wt[:, :, None, :] + sa[..., None] * bt[:, :, None, :] + vt[..., None] * kt[:, :, None, :]
        return S, jnp.einsum('bhvk,bhk->bhv', S, rt)

    S, o = lax.scan(step, s0.astype(jnp.float32), tuple(time_major(t) for t in (r, w, k, v, a, b)))
    return jnp.moveaxis(o, 0, 1), S

def token_shift(p, buf, mu):
    prev = jnp.concatenate([buf.astype(p.dtype), p[:, :-1]], axis=1)
    return p + (prev - p) * mu, p[:, -1:]

def parallel_mixers(u, s_h, s_r, buf, lb, lp):
    B, T, _ = u.shape
    f32 = jnp.float32
    p = u @ lp['w_in']
    cuts = np.cumsum([D_HGRN, D_HGRN, D_HGRN, D_HGRN, N_RWKV_IN, D_MODEL]).tolist()
    hq, hf, hi, hg, pr, gate_a, gate_b = jnp.split(p, cuts, axis=-1)

    hh = lambda t, d: t.reshape(B, T, HGRN_HEADS, d)
    f = lb + (1.0 - lb) * jax.nn.sigmoid(hf.astype(f32))
    o_h, s_h_new = hgrn2_blocked(hh(jax.nn.silu(hq), HGRN_DK), hh(1.0 - f, HGRN_DK),
                                 hh(jnp.log(f), HGRN_DK), hh(hi, HGRN_DV), s_h)
    o_h = o_h * lax.rsqrt(jnp.mean(o_h * o_h, axis=-1, keepdims=True) + NORM_EPS)
    o_h = (o_h * lp['hgrn_norm_g'].astype(f32)
           * jax.nn.silu(hh(hg, HGRN_DV).astype(f32))).reshape(B, T, D_HGRN)

    sp, buf_new = token_shift(pr, buf, lp['rwkv_mu'])
    rcuts = np.cumsum([D_RWKV, D_RWKV, D_RWKV, DECAY_LORA, ICL_LORA]).tolist()
    r, k, v, xw, xa, xg = jnp.split(sp, rcuts, axis=-1)
    rh = lambda t: t.reshape(B, T, RWKV_HEADS, RWKV_HEAD)
    w_log = -jax.nn.softplus(-(lp['rwkv_w0'] + jnp.tanh(xw) @ lp['rwkv_w2']).astype(f32)) - 0.5
    decay = jnp.exp(-jnp.exp(w_log))
    a_icl = jax.nn.sigmoid((lp['rwkv_a0'] + xa @ lp['rwkv_a2']).astype(f32))
    g_out = (jax.nn.sigmoid(xg) @ lp['rwkv_g2']).astype(f32)
    kk = rh(k.astype(f32) * lp['rwkv_k_k'].astype(f32))
    kk = kk / jnp.maximum(jnp.sqrt(jnp.sum(kk * kk, axis=-1, keepdims=True)), 1e-12)
    k_mod = k.astype(f32) * (1.0 + (a_icl - 1.0) * lp['rwkv_k_a'].astype(f32))
    o_r, s_r_new = rwkv7_scan(rh(r), rh(decay), rh(k_mod), rh(v), -kk, kk * rh(a_icl), s_r)
    mean = jnp.mean(o_r, axis=-1, keepdims=True)
    var = jnp.mean(jnp.square(o_r - mean), axis=-1, keepdims=True)
    o_r = (((o_r - mean) * lax.rsqrt(var + RWKV_GN_EPS)).reshape(B, T, D_RWKV)
           * lp['rwkv_ln_g'].astype(f32) + lp['rwkv_ln_b'].astype(f32))
    bonus = jnp.sum(rh(r).astype(f32) * rh(k_mod) * lp['rwkv_r_k'].astype(f32), axis=-1, keepdims=True)
    o_r = (o_r + (bonus * rh(v).astype(f32)).reshape(B, T, D_RWKV)) * g_out

    merged = jax.nn.sigmoid(gate_a.astype(f32)) * o_h + jax.nn.sigmoid(gate_b.astype(f32)) * o_r
    return merged.astype(u.dtype), s_h_new.astype(s_h.dtype), s_r_new.astype(s_r.dtype), buf_new.astype(buf.dtype)

def memory_kv(mem, norm_g, wk, wv):
    B, M, _ = mem.shape
    m = rmsnorm(mem, norm_g)
    return (m @ wk).reshape(B, M, X_HEADS, X_HEAD_DIM), (m @ wv).reshape(B, M, X_HEADS, X_HEAD_DIM)

def memory_cross_attention(u, mem_k, mem_v, wq, wo):
    B, T, _ = u.shape
    q = (u @ wq).reshape(B, T, X_HEADS, X_HEAD_DIM)
    s = jnp.einsum('bthd,bmhd->bhtm', q.astype(jnp.float32), mem_k.astype(jnp.float32)) * (X_HEAD_DIM ** -0.5)
    attn = jax.nn.softmax(s, axis=-1)
    o = jnp.einsum('bhtm,bmhd->bthd', attn, mem_v.astype(jnp.float32)).reshape(B, T, D_MODEL)
    return o.astype(u.dtype) @ wo

def hier_moe(u, lp):
    B, T, D = u.shape
    x = u.reshape(-1, D)
    N = x.shape[0]
    f32 = jnp.float32
    lg = (x @ lp['router_group_w']).astype(f32) + lp['router_group_b'].astype(f32)
    pg = jax.nn.softmax(lg, axis=-1)
    c = jnp.argmax(lg, axis=-1)
    pg_c = jnp.take_along_axis(pg, c[:, None], axis=1)
    le = ((x @ lp['router_expert_w']).astype(f32).reshape(N, N_GROUPS, EXPERTS_PER_GROUP)
          + lp['router_expert_b'].astype(f32))
    le_c = jnp.take_along_axis(le, c[:, None, None], axis=1)[:, 0]
    top_v, top_i = lax.top_k(le_c, TOP_K)
    wt = jax.nn.softmax(top_v, axis=-1) * pg_c
    w_e = jnp.sum(jax.nn.one_hot(top_i, EXPERTS_PER_GROUP, dtype=f32) * wt[..., None], axis=1)
    w_full = jax.nn.one_hot(c, N_GROUPS, dtype=f32)[:, :, None] * w_e[:, None, :]
    out = jnp.zeros_like(x)
    for gi in range(N_GROUPS):
        sl = slice(gi * EXPERTS_PER_GROUP, (gi + 1) * EXPERTS_PER_GROUP)
        h = (jax.nn.silu(jnp.einsum('nd,edf->nef', x, lp['expert_w_gate'][sl]))
             * jnp.einsum('nd,edf->nef', x, lp['expert_w_up'][sl]))
        h = h * w_full[:, gi, :, None].astype(h.dtype)
        out = out + jnp.einsum('nef,efd->nd', h, lp['expert_w_down'][sl]).astype(x.dtype)
    return out.reshape(B, T, D)

def trunk_layer(h, mem_k, mem_v, s_h, s_r, buf, lb, lp):
    m, s_h, s_r, buf = parallel_mixers(rmsnorm(h, lp['norm_mix_g']), s_h, s_r, buf, lb, lp)
    h = h + m @ lp['w_out']
    h = h + memory_cross_attention(rmsnorm(h, lp['norm_x_g']), mem_k, mem_v, lp['wq_x'], lp['wo_x'])
    h = h + hier_moe(rmsnorm(h, lp['norm_ffn_g']), lp)
    return h, s_h, s_r, buf

def setup_inputs(seed: int = 0) -> dict:
    key = jax.random.key(seed)
    ks = iter(jax.random.split(key, 40))
    nrm = lambda shape, scale: scale * jax.random.normal(next(ks), shape, jnp.float32)
    unif = lambda shape, lo, hi: jax.random.uniform(next(ks), shape, jnp.float32, lo, hi)
    L = DEPTH
    sD = D_MODEL ** -0.5
    return {
        'x_prompt': nrm((BATCH, SEQ, D_MODEL), 1.0),
        'x_sample': nrm((DEC_BATCH, DEC_SEQ, D_MODEL), 1.0),
        'mem_prompt': nrm((BATCH, N_MEM, D_MODEL), 1.0),
        'cache_mem_k': nrm((L, DEC_BATCH, N_MEM, X_HEADS, X_HEAD_DIM), 1.0),
        'cache_mem_v': nrm((L, DEC_BATCH, N_MEM, X_HEADS, X_HEAD_DIM), 1.0),
        'state_hgrn': nrm((L, DEC_BATCH, HGRN_HEADS, HGRN_DK, HGRN_DV), 0.5),
        'state_rwkv': nrm((L, DEC_BATCH, RWKV_HEADS, RWKV_HEAD, RWKV_HEAD), 0.5),
        'state_rwkv_shift': nrm((L, DEC_BATCH, 1, N_RWKV_IN), 1.0),
        'norm_mix_g': 1.0 + nrm((L, D_MODEL), 0.02),
        'w_in': nrm((L, D_MODEL, N_IN), sD),
        'hgrn_lower_bounds': nrm((L + 1, D_HGRN), 0.1),
        'hgrn_norm_g': 1.0 + nrm((L, HGRN_DV), 0.02),
        'rwkv_mu': unif((L, N_RWKV_IN), 0.0, 1.0),
        'rwkv_w0': unif((L, D_RWKV), -5.0, -1.0),
        'rwkv_w2': nrm((L, DECAY_LORA, D_RWKV), 0.1),
        'rwkv_a0': nrm((L, D_RWKV), 0.1),
        'rwkv_a2': nrm((L, ICL_LORA, D_RWKV), ICL_LORA ** -0.5),
        'rwkv_g2': nrm((L, GATE_LORA, D_RWKV), GATE_LORA ** -0.5),
        'rwkv_k_k': 0.85 + nrm((L, D_RWKV), 0.05),
        'rwkv_k_a': 1.0 + nrm((L, D_RWKV), 0.05),
        'rwkv_r_k': nrm((L, RWKV_HEADS, RWKV_HEAD), 0.1),
        'rwkv_ln_g': 1.0 + nrm((L, D_RWKV), 0.02),
        'rwkv_ln_b': nrm((L, D_RWKV), 0.02),
        'w_out': nrm((L, D_MODEL, D_MODEL), sD),
        'norm_x_g': 1.0 + nrm((L, D_MODEL), 0.02),
        'norm_mem_g': 1.0 + nrm((L, D_MODEL), 0.02),
        'wq_x': nrm((L, D_MODEL, D_MODEL), sD),
        'wk_x': nrm((L, D_MODEL, D_MODEL), sD),
        'wv_x': nrm((L, D_MODEL, D_MODEL), sD),
        'wo_x': nrm((L, D_MODEL, D_MODEL), sD),
        'norm_ffn_g': 1.0 + nrm((L, D_MODEL), 0.02),
        'router_group_w': nrm((L, D_MODEL, N_GROUPS), sD),
        'router_group_b': nrm((L, N_GROUPS), 0.01),
        'router_expert_w': nrm((L, D_MODEL, N_EXPERTS), sD),
        'router_expert_b': nrm((L, N_GROUPS, EXPERTS_PER_GROUP), 0.01),
        'expert_w_gate': nrm((L, N_EXPERTS, D_MODEL, D_EXPERT), sD),
        'expert_w_up': nrm((L, N_EXPERTS, D_MODEL, D_EXPERT), sD),
        'expert_w_down': nrm((L, N_EXPERTS, D_EXPERT, D_MODEL), D_EXPERT ** -0.5),
        'norm_final_g': 1.0 + nrm((D_MODEL,), 0.02),
    }

def reference(x_prompt, x_sample, mem_prompt, cache_mem_k, cache_mem_v, state_hgrn, state_rwkv,
              state_rwkv_shift, norm_mix_g, w_in, hgrn_lower_bounds, hgrn_norm_g, rwkv_mu, rwkv_w0,
              rwkv_w2, rwkv_a0, rwkv_a2, rwkv_g2, rwkv_k_k, rwkv_k_a, rwkv_r_k, rwkv_ln_g, rwkv_ln_b,
              w_out, norm_x_g, norm_mem_g, wq_x, wk_x, wv_x, wo_x, norm_ffn_g, router_group_w,
              router_group_b, router_expert_w, router_expert_b, expert_w_gate, expert_w_up,
              expert_w_down, norm_final_g):
    lb_all = jnp.cumsum(jax.nn.softmax(hgrn_lower_bounds.astype(jnp.float32), axis=0), axis=0)
    Bp = x_prompt.shape[0]
    dt = x_prompt.dtype
    hp, hs = x_prompt, x_sample
    mk_p, mv_p, sh_p, sh_s, sr_p, sr_s, bf_p, bf_s = [], [], [], [], [], [], [], []
    for l in range(DEPTH):
        lp = {
            'norm_mix_g': norm_mix_g[l], 'w_in': w_in[l], 'hgrn_norm_g': hgrn_norm_g[l],
            'rwkv_mu': rwkv_mu[l], 'rwkv_w0': rwkv_w0[l], 'rwkv_w2': rwkv_w2[l], 'rwkv_a0': rwkv_a0[l],
            'rwkv_a2': rwkv_a2[l], 'rwkv_g2': rwkv_g2[l], 'rwkv_k_k': rwkv_k_k[l], 'rwkv_k_a': rwkv_k_a[l],
            'rwkv_r_k': rwkv_r_k[l], 'rwkv_ln_g': rwkv_ln_g[l], 'rwkv_ln_b': rwkv_ln_b[l],
            'w_out': w_out[l], 'norm_x_g': norm_x_g[l], 'wq_x': wq_x[l], 'wo_x': wo_x[l],
            'norm_ffn_g': norm_ffn_g[l], 'router_group_w': router_group_w[l],
            'router_group_b': router_group_b[l], 'router_expert_w': router_expert_w[l],
            'router_expert_b': router_expert_b[l], 'expert_w_gate': expert_w_gate[l],
            'expert_w_up': expert_w_up[l], 'expert_w_down': expert_w_down[l],
        }
        lb = lb_all[l]
        mem_k, mem_v = memory_kv(mem_prompt, norm_mem_g[l], wk_x[l], wv_x[l])
        hp, s_h, s_r, buf = trunk_layer(
            hp, mem_k, mem_v,
            jnp.zeros((Bp, HGRN_HEADS, HGRN_DK, HGRN_DV), dt),
            jnp.zeros((Bp, RWKV_HEADS, RWKV_HEAD, RWKV_HEAD), dt),
            jnp.zeros((Bp, 1, N_RWKV_IN), dt), lb, lp)
        mk_p.append(mem_k)
        mv_p.append(mem_v)
        sh_p.append(s_h)
        sr_p.append(s_r)
        bf_p.append(buf)
        hs, s_h2, s_r2, buf2 = trunk_layer(
            hs, cache_mem_k[l], cache_mem_v[l], state_hgrn[l], state_rwkv[l], state_rwkv_shift[l], lb, lp)
        sh_s.append(s_h2)
        sr_s.append(s_r2)
        bf_s.append(buf2)
    y_prompt = rmsnorm(hp, norm_final_g)
    y_sample = rmsnorm(hs, norm_final_g)
    return (y_prompt, y_sample, jnp.stack(mk_p), jnp.stack(mv_p), jnp.stack(sh_p), jnp.stack(sh_s),
            jnp.stack(sr_p), jnp.stack(sr_s), jnp.stack(bf_p), jnp.stack(bf_s))


_drawn_inputs = setup_inputs


def setup_inputs(seed=0):
    import zlib

    import numpy as np

    out = dict(_drawn_inputs(seed))
    spreads = {}
    factors = {'rwkv_ln_b': 6.771,
     'norm_x_g': 8.0,
     'norm_mem_g': 2.8,
     'router_group_b': 26.883,
     'router_expert_b': 3.886,
     'norm_final_g': 8.281,
     'norm_ffn_g': 3.704}
    for name, (base, spread) in spreads.items():
        noise = np.random.default_rng([zlib.crc32(name.encode()), seed]).standard_normal(out[name].shape)
        drawn = base * np.exp(spread * noise) if base else spread * noise
        out[name] = jnp.asarray(drawn.astype(out[name].dtype))
    for name, factor in factors.items():
        out[name] = (out[name] * factor).astype(out[name].dtype)
    return out
```

```python
from contextlib import ExitStack

import concourse.bass as bass
from concourse import mybir

F32 = mybir.dt.float32
ALU = mybir.AluOpType
ACT = mybir.ActivationFunctionType
AX_X = mybir.AxisListType.X

P = 128
D = 1024
FT = D // P
SEQ = 512
DEC = 32
N = SEQ + DEC
HALF = N // 2
CH = 64
NCH = SEQ // CH
BW = 1 + (NCH + 1) * CH + 1
HEADS = 8
DECAY_L, ICL_L, GATE_L = 64, 64, 160
LORA = DECAY_L + ICL_L + GATE_L
N_RWKV = 3 * D + LORA
COL_RWKV = 4 * D
COL_GATES = COL_RWKV + N_RWKV
MEM = 256
XH = 4
XSCALE = (D // XH) ** -0.5
GROUPS, PER_GROUP = 4, 8
EXPERTS = GROUPS * PER_GROUP
DE = 256
EPS = 1e-6
GN_EPS = 64e-5
UNIT = 256
TT = 5
DECAY = 0.6065306597126334
LN2 = 0.6931471805599453

H, XN, B2, B3, B4, B5, B6 = (FT * i for i in range(7))


class Sems:

    def __init__(self, nc):
        self.nc, self.by_name, self.kept = nc, {}, {}

    def __getitem__(self, name):
        where = self.kept if name.startswith(("slot", "banks")) else self.by_name
        if name not in where:
            where[name] = self.nc.alloc_semaphore(name)
        return where[name]

    def end_stage(self):
        self.nc.clear_and_free_semaphores(list(self.by_name.values()))
        self.nc.all_engine_barrier()
        self.by_name = {}


def shaped(flat, base, shape):
    n = 1
    for s in shape:
        n *= s
    v = flat[:, base:base + n]
    if len(shape) == 2:
        v = v.rearrange("p (a b) -> p a b", a=shape[0])
    if len(shape) == 3:
        v = v.rearrange("p (a b c) -> p a b c", a=shape[0], b=shape[1])
    return v


class Room:

    def __init__(self, flat, n):
        self.flat, self.n, self.at = flat, n, 0

    def take(self, *shape):
        v = shaped(self.flat, self.at, shape)
        n = 1
        for s in shape:
            n *= s
        self.at += n
        assert self.at <= self.n, (self.at, self.n)
        return v


SCR = 12800


def build(nc, I, O):
    with ExitStack() as ctx:
        def sb(name, shape):
            return ctx.enter_context(nc.sbuf_tensor(name, shape, F32))

        S = Sems(nc)
        arena = sb("arena", [P, 7 * FT, BW])
        flat = arena[:, :, :].rearrange("p f n -> p (f n)")
        ring = sb("ring", [P, 2, FT, UNIT])
        ring_flat = ring[:, :, :, :].rearrange("p s k n -> p (s k n)")
        lora = sb("lora", [P, 3, BW])
        ident = sb("ident", [P, P])
        ones = sb("ones", [P, P])
        head_ones = sb("head_ones", [P, P])
        rows_a = sb("rows_a", [P, P])
        rows_b = sb("rows_b", [P, P])
        ca = sb("ca", [P, P])
        cb = sb("cb", [P, P])
        lbs = sb("lbs", [P, 2, FT])
        tiny = sb("tiny", [P, 4])
        scale_row = sb("scale_row", [P, BW])
        scr = sb("scr", [P, SCR])
        ps = ctx.enter_context(nc.psum_tensor("ps", [P, 8, 512], F32))
        bank = [ps[:, b, :] for b in range(8)]
        eps_c, gn_eps_c, kk_c = tiny[:, 0:1], tiny[:, 1:2], tiny[:, 2:3]

        VEC = ["norm_mix_g", "rwkv_w0", "rwkv_a0", "rwkv_k_k", "rwkv_k_a", "rwkv_r_k", "rwkv_ln_g", "rwkv_ln_b",
               "norm_x_g", "norm_mem_g", "norm_ffn_g", "norm_final_g", "lb0", "lb1"]
        NV = len(VEC) * FT

        def col(name, f=None):
            k = VEC.index(name) * FT
            return ca[:, k:k + FT] if f is None else ca[:, k + f:k + f + 1]

        MU, HG, SHIFT, NSH = 0, 27, 28, 27

        def frames(base, a, n, f0=0, f1=FT):
            return arena[:, base + f0:base + f1, bass.ds(a + 1, n)]

        def whole(base):
            return arena[:, base:base + FT, 1:1 + N]

        def over(c, n):
            return c.unsqueeze(2).to_broadcast([P, c.shape[1], n])

        def split_heads(b):
            return b.rearrange("p (a n) -> p a n", a=8)

        def norm_stage(k, src, dst, gain, n, sq):
            parts = [(0, n)] if n <= 512 else [(0, n // 2), (n // 2, n)]
            rs = scale_row[:, 0:n]

            def on_act(act):
                act.activation(sq, src, ACT.Square).then_inc(S[k + "_squares"], 1)
                act.wait_ge(S[k + "_sums"], 1)
                for h, (a, b) in enumerate(parts):
                    act.activation(rs[:, a:b], ps[:, h, 0:b - a], ACT.Sqrt, bias=eps_c, scale=1.0 / D).then_inc(S[k + "_rms"], 1)

            def on_pe(pe):
                pe.wait_ge(S[k + "_squares"], 1)
                for h, (a, b) in enumerate(parts):
                    for f in range(FT):
                        mm = pe.matmul(ps[:, h, 0:b - a], ones[:, :], sq[:, f, a:b], start=(f == 0), stop=(f == FT - 1))
                mm.then_inc(S[k + "_sums"], 1)

            def on_dve(dve):
                dve.wait_ge(S[k + "_rms"], len(parts))
                dve.reciprocal(rs, rs).then_inc(S[k + "_rrms"], 1)
                dve.wait_ge(S[k + "_rrms"], 1)
                for f in range(FT):
                    dve.scalar_tensor_tensor(out=dst[:, f, :], in0=src[:, f, :], scalar=gain(f), in1=rs,
                                             op0=ALU.mult, op1=ALU.mult).then_inc(S[k + "_normed"], 1)

            return on_act, on_pe, on_dve

        used = [0]

        def linear(jobs):
            spans = []
            for job in jobs:
                spans.append((used[0], job))
                used[0] += job[3] // 2

            def on_sp(sp):
                for b0, (kind, w, c0, units, x, dst) in spans:
                    wv = w.rearrange("(k p) n -> p k n", p=P)
                    with sp.Fori(0, units // 2) as i:
                        n = sp.snap(i + (b0 + 1))
                        for s in range(2):
                            sp.wait_ge(S[f"slot{s}_free"], n)
                            sp.dma_start(ring[:, s], wv[:, :, bass.ds(i * (2 * UNIT) + (c0 + s * UNIT), UNIT)]).then_inc(S[f"slot{s}_loaded"], 16)

            def on_pe(pe):
                for b0, (kind, w, c0, units, x, dst) in spans:
                    with pe.Fori(0, units // 2) as i:
                        n = pe.snap(i + (b0 + 1))
                        n16 = pe.snap(i * 16 + (b0 + 1) * 16)
                        for s in range(2):
                            pe.wait_ge(S[f"banks{s}_free"], n)
                            pe.wait_ge(S[f"slot{s}_loaded"], n16)
                            if kind == "rows":
                                for h in range(MEM // P):
                                    for k in range(FT):
                                        mm = pe.matmul(ps[:, 4 * s + h, 0:UNIT], x[:, k, h * P:(h + 1) * P], ring[:, s, k, :],
                                                       start=(k == 0), stop=(k == FT - 1))
                            else:
                                for o in range(UNIT // P):
                                    for h in range(2):
                                        for k in range(FT):
                                            mm = pe.matmul(ps[:, 4 * s + 2 * o + h, 0:HALF], ring[:, s, k, o * P:(o + 1) * P],
                                                           arena[:, x + k, 1 + h * HALF:1 + (h + 1) * HALF],
                                                           start=(k == 0), stop=(k == FT - 1))
                            mm.then_inc(S[f"slot{s}_free"], 1)

            def leave(eng, on_dve):
                for b0, (kind, w, c0, units, x, dst) in spans:
                    if (kind == "add") != on_dve:
                        continue
                    with eng.Fori(0, units // 2) as i:
                        n = eng.snap(i + (b0 + 2))
                        for s in range(2):
                            eng.wait_ge(S[f"slot{s}_free"], n)
                            if kind == "rows":
                                last = eng.copy(dst[:, :, bass.ds(i * (2 * UNIT) + s * UNIT, UNIT)], ps[:, 4 * s:4 * s + 2, 0:UNIT])
                            else:
                                for o in range(UNIT // P):
                                    src = ps[:, 4 * s + 2 * o:4 * s + 2 * o + 2, 0:HALF]
                                    to = arena[:, bass.ds(i * 4 + (dst + 2 * s + o), 1), 1:1 + N].rearrange("p o (h n) -> p (o h) n", h=2)
                                    if kind == "keep":
                                        last = eng.copy(to, src)
                                    else:
                                        last = eng.tensor_tensor(to, to, src, ALU.add)
                            last.then_inc(S[f"banks{s}_free"], 1)

            return on_sp, on_pe, leave

        x_tok = shaped(flat, B2 * BW, (TT, D))
        x_groups = []
        for t in range(TT):
            n = P if t < TT - 1 else DEC
            for f0 in (0, 4):
                x_groups.append((x_tok[0:n, t, :], n, f0, arena[:, H + f0:H + f0 + 4, 1 + t * P:1 + t * P + n]))

        with nc.Block() as block:
            @block.sync
            def _(sp):
                sp.dma_start(x_tok[:, 0:4, :], I["x_prompt"][0].rearrange("(t p) d -> p t d", p=P)).then_inc(S["x_in"], 16)
                sp.dma_start(x_tok[0:DEC, 4, :], I["x_sample"][0]).then_inc(S["x_in"], 16)

            @block.scalar
            def _(act):
                for s in range(2):
                    act.sem_inc(S[f"banks{s}_free"], 1)
                for v, name in enumerate(VEC):
                    if name == "rwkv_r_k":
                        src = I[name][0].rearrange("(f a) b -> f (a b)", f=FT)
                    elif name == "norm_final_g":
                        src = I[name].rearrange("(f p) -> f p", f=FT)
                    elif name in ("lb0", "lb1"):
                        src = I["hgrn_lower_bounds"][int(name[2])].rearrange("(f p) -> f p", f=FT)
                    else:
                        src = I[name][0].rearrange("(f p) -> f p", f=FT)
                    act.dma_start(rows_a[v * FT:(v + 1) * FT, :], src).then_inc(S["rows_a_in"], 16)
                act.wait_ge(S["rows_b_cleared"], 1)
                full = N_RWKV // P
                rest = N_RWKV - full * P
                for base, src in ((MU, I["rwkv_mu"][0]), (SHIFT, I["state_rwkv_shift"][0, 0, 0])):
                    act.dma_start(rows_b[base:base + full, :], src[0:full * P].rearrange("(f p) -> f p", p=P)).then_inc(S["rows_b_in"], 16)
                    act.dma_start(rows_b[base + full:base + full + 1, 0:rest], src[full * P:N_RWKV].unsqueeze(0)).then_inc(S["rows_b_in"], 16)
                act.dma_start(rows_b[HG:HG + 1, :], I["hgrn_norm_g"]).then_inc(S["rows_b_in"], 16)
                for i, (src, n, f0, dst) in enumerate(x_groups):
                    if i % 2:
                        act.wait_ge(S["x_turned"], i + 1)
                        act.copy(dst, ps[:, i % 8, :].rearrange("p (f n) -> p f n", f=4)[:, :, 0:n]).then_inc(S["x_kept_odd"], 1)

            @block.gpsimd
            def _(pool):
                pool.memset(rows_b[:, :], 0.0).then_inc(S["rows_b_cleared"], 1)
                pool.memset(ident[:, :], 0.0).then_inc(S["ident_zero"], 1)
                pool.memset(ones[:, :], 1.0).then_inc(S["consts"], 1)
                pool.memset(eps_c, EPS).then_inc(S["consts"], 1)
                pool.memset(gn_eps_c, GN_EPS).then_inc(S["consts"], 1)
                pool.memset(kk_c, 15.0 * LN2).then_inc(S["consts"], 1)
                pool.wait_ge(S["ident_zero"], 1)
                pool.affine_select(out=ident[:, :], in_=ident[:, :], compare_op=ALU.not_equal, fill=1.0, base=0,
                                   pattern=[[-1, P]], channel_multiplier=1).then_inc(S["ident_ready"], 1)

            @block.tensor
            def _(pe):
                for s in range(2):
                    pe.sem_inc(S[f"slot{s}_free"], 1)
                pe.wait_ge(S["ident_ready"], 1)
                pe.wait_ge(S["x_in"], 32)
                for i, (src, n, f0, dst) in enumerate(x_groups):
                    if i >= 8:
                        pe.wait_ge(S["x_kept_odd" if i % 2 else "x_kept_even"], (i - 8) // 2 + 1)
                    for f in range(4):
                        mm = pe.transpose(ps[:, i % 8, f * P:f * P + n], src[:, (f0 + f) * P:(f0 + f + 1) * P], ident[0:n, 0:n])
                    mm.then_inc(S["x_turned"], 1)
                pe.wait_ge(S["x_kept_odd"], 2)
                pe.wait_ge(S["rows_a_in"], 16 * len(VEC))
                pe.transpose(ps[:, 3, 0:NV], rows_a[0:NV, :], ident[0:NV, 0:NV]).then_inc(S["vectors_turned"], 1)
                pe.wait_ge(S["rows_b_in"], 80)
                pe.wait_ge(S["x_kept_even"], 3)
                pe.transpose(ps[:, 4, 0:P], rows_b[:, :], ident[:, :]).then_inc(S["vectors_turned"], 1)

            @block.vector
            def _(dve):
                dve.memset(arena[:, 0:B2, 1 + N:BW], 0.0).then_inc(S["pads"], 1)
                dve.memset(arena[:, 0:B2, 0:1], 0.0).then_inc(S["pads"], 1)
                dve.memset(lora[:, :, :], 0.0).then_inc(S["pads"], 1)
                dve.memset(head_ones[:, :], 0.0).then_inc(S["head_zero"], 1)
                dve.wait_ge(S["head_zero"], 1)
                dve.memset(head_ones[0:64, 0:64], 1.0).then_inc(S["consts"], 1)
                dve.memset(head_ones[64:128, 64:128], 1.0).then_inc(S["consts"], 1)
                for i, (src, n, f0, dst) in enumerate(x_groups):
                    if i % 2 == 0:
                        dve.wait_ge(S["x_turned"], i + 1)
                        dve.tensor_copy(dst, ps[:, i % 8, :].rearrange("p (f n) -> p f n", f=4)[:, :, 0:n]).then_inc(S["x_kept_even"], 1)
                dve.wait_ge(S["vectors_turned"], 1)
                dve.tensor_copy(ca[:, 0:NV], ps[:, 3, 0:NV]).then_inc(S["vectors"], 1)
                dve.wait_ge(S["vectors_turned"], 2)
                dve.tensor_copy(cb[:, :], ps[:, 4, 0:P]).then_inc(S["vectors"], 1)

        S.end_stage()

        w_in = I["w_in"][0]
        sq_all = shaped(scr[:, :], 0, (FT, N))
        n_act, n_pe, n_dve = norm_stage("mix", whole(H), whole(XN), lambda f: col("norm_mix_g", f), N, sq_all)
        l_sp, l_pe, l_leave = linear([("keep", w_in, 0, 16, XN, B2), ("keep", w_in, COL_GATES, 4, XN, B6)])
        lb, one_m_lb = lbs[:, 0, :], lbs[:, 1, :]

        with nc.Block() as block:
            @block.sync
            def _(sp):
                l_sp(sp)

            @block.scalar
            def _(act):
                n_act(act)
                l_leave(act, False)
                act.wait_ge(S["lb_diff"], 1)
                act.activation(lb, lb, ACT.Sigmoid).then_inc(S["lb_ready"], 1)
                act.wait_ge(S["banks0_free"], used[0] + 1)
                act.wait_ge(S["banks1_free"], used[0] + 1)
                act.activation(whole(B3), whole(B3), ACT.Sigmoid).then_inc(S["f_sig"], 1)
                act.activation(whole(B6), whole(B6), ACT.Sigmoid).then_inc(S["ga_sig"], 1)
                act.activation(sq_all, whole(B2), ACT.Sigmoid).then_inc(S["q_sig"], 1)
                act.wait_ge(S["q_silu"], 1)
                act.activation(sq_all, whole(B5), ACT.Sigmoid).then_inc(S["g_sig"], 1)

            @block.tensor
            def _(pe):
                n_pe(pe)
                pe.wait_ge(S["mix_normed"], FT)
                pe.wait_ge(S["mix_rms"], 2)
                l_pe(pe)

            @block.vector
            def _(dve):
                n_dve(dve)
                dve.memset(arena[:, B2:B6 + FT, 1 + N:BW], 0.0).then_inc(S["pads2"], 1)
                dve.memset(arena[:, B2:B6 + FT, 0:1], 0.0).then_inc(S["pads2"], 1)
                dve.tensor_tensor(lb, col("lb0"), col("lb1"), ALU.subtract).then_inc(S["lb_diff"], 1)
                dve.wait_ge(S["lb_ready"], 1)
                dve.tensor_scalar(one_m_lb, lb, -1.0, 1.0, ALU.mult, ALU.add).then_inc(S["lb_ready"], 1)
                dve.wait_ge(S["lb_ready"], 2)
                dve.wait_ge(S["pads2"], 2)
                dve.wait_ge(S["f_sig"], 1)
                for f in range(FT):
                    t = arena[:, B3 + f, 1:1 + N]
                    dve.tensor_scalar(t, t, one_m_lb[:, f:f + 1], lb[:, f:f + 1], ALU.mult, ALU.add).then_inc(S["f_ready"], 1)
                dve.memset(arena[:, B3:B3 + FT, 1 + N:BW], 1.0).then_inc(S["f_ready"], 1)
                dve.wait_ge(S["q_sig"], 1)
                dve.tensor_tensor(whole(B2), whole(B2), sq_all, ALU.mult).then_inc(S["q_silu"], 1)
                dve.wait_ge(S["ga_sig"], 1)
                dve.tensor_tensor(whole(B6), whole(B6), whole(B5), ALU.mult).then_inc(S["gates"], 1)
                dve.wait_ge(S["g_sig"], 1)
                dve.wait_ge(S["gates"], 1)
                dve.scalar_tensor_tensor(out=whole(B5), in0=whole(B6), scalar=cb[:, HG:HG + 1], in1=sq_all, op0=ALU.mult, op1=ALU.mult).then_inc(S["gates"], 1)

        S.end_stage()

        room = Room(scr[:, :], SCR)
        g_s, k_s, b_s, eb, enb, q16, kinv, kh16, q32, kh32, v_s = (room.take(FT, CH) for _ in range(11))
        e32 = room.take(FT, 2)
        sc = room.take(2, 4, CH)
        k_tok, v_tok = room.take(4, P), room.take(4, P)
        state = room.take(HEADS, P)
        o_sq, o_rs, o_n = (room.take(2, 4, CH) for _ in range(3))
        h_out = ps[:, 6:8, 0:4 * CH].rearrange("p q (a t) -> p q a t", a=4)

        def by_parity(v):
            return v.rearrange("p (a q) t -> p q a t", q=2)

        h_mask = room.take(2, 4, CH)
        h_scan = room.take(FT * CH)

        def flat2(v):
            return v.rearrange("p a b -> p (a b)")

        def blocks(v):
            return flat2(v).rearrange("p (m e l) -> p m e l", e=2, l=16)

        def block_end(v):
            return blocks(v)[:, :, :, 15:16]

        def hgrn_act(act, c, n):
            act.wait_ge(S["h_chunk_done"], n)
            act.activation(g_s, frames(B3, c * CH, CH), ACT.Ln).then_inc(S["h_g"], 1)
            act.copy(v_s, frames(B4, c * CH, CH)).then_inc(S["h_v"], 1)
            act.wait_ge(S["h_b"], n)
            act.activation(eb, b_s, ACT.Exp).then_inc(S["h_eb"], 1)
            act.activation(enb, b_s, ACT.Exp, scale=-1.0).then_inc(S["h_enb"], 1)
            act.wait_ge(S["h_v_turned"], n)
            act.copy(v_tok, bank[2].rearrange("p (a b) -> p a b", a=4)).then_inc(S["h_v_tok"], 1)
            act.wait_ge(S["h_k_turned"], n)
            act.copy(k_tok, bank[1].rearrange("p (a b) -> p a b", a=4)).then_inc(S["h_k_tok"], 1)
            act.wait_ge(S["h_o"], n)
            act.activation(o_sq, h_out, ACT.Square).then_inc(S["h_o_sq"], 1)
            act.wait_ge(S["h_ms"], n)
            act.activation(o_rs, bank[3].rearrange("p (q a t) -> p q a t", q=2, a=4), ACT.Ln, bias=eps_c, scale=1.0 / P).then_inc(S["h_ln_ms"], 1)
            act.wait_ge(S["h_ln_ms"], n)
            act.activation(o_rs, o_rs, ACT.Exp, scale=-0.5).then_inc(S["h_rs"], 1)

        def hgrn_dve(dve, c, n):
            dve.wait_ge(S["h_chunk_done"], n)
            dve.tensor_scalar(k_s, frames(B3, c * CH, CH), -1.0, 1.0, ALU.mult, ALU.add).then_inc(S["h_k"], 1)
            dve.wait_ge(S["h_g"], n)
            dve.tensor_tensor_scan(flat2(b_s), h_scan, flat2(g_s), 0.0, ALU.mult, ALU.add).then_inc(S["h_b"], 1)
            dve.wait_ge(S["h_eb"], n)
            dve.tensor_tensor(q16, frames(B2, c * CH, CH), eb, ALU.mult).then_inc(S["h_q16"], 1)
            dve.tensor_tensor(flat2(e32).rearrange("p (m o) -> p m o", o=1), block_end(eb)[:, :, 0, :], block_end(eb)[:, :, 1, :], ALU.mult).then_inc(S["h_e32"], 1)
            dve.wait_ge(S["h_enb"], n)
            dve.wait_ge(S["h_k"], n)
            dve.tensor_tensor(kinv, k_s, enb, ALU.mult).then_inc(S["h_kinv"], 1)
            dve.wait_ge(S["h_kinv"], n)
            dve.tensor_tensor(blocks(kh16), blocks(kinv), block_end(eb).to_broadcast([P, 16, 2, 16]), ALU.mult).then_inc(S["h_kh16"], 1)
            dve.wait_ge(S["h_kh16"], n)
            dve.tensor_tensor(blocks(kh32)[:, :, 0, :], blocks(kh16)[:, :, 0, :], block_end(eb)[:, :, 1, :].to_broadcast([P, 16, 16]), ALU.mult)
            dve.tensor_copy(blocks(kh32)[:, :, 1, :], blocks(kh16)[:, :, 1, :]).then_inc(S["h_kh32"], 1)
            dve.wait_ge(S["h_q16"], n)
            dve.tensor_tensor(blocks(q32)[:, :, 1, :], blocks(q16)[:, :, 1, :], block_end(eb)[:, :, 0, :].to_broadcast([P, 16, 16]), ALU.mult)
            dve.tensor_copy(blocks(q32)[:, :, 0, :], blocks(q16)[:, :, 0, :]).then_inc(S["h_q32"], 1)
            dve.wait_ge(S["h_scores"], n)
            dve.tensor_tensor(sc, bank[0].rearrange("p (e a b) -> p e a b", e=2, a=4), h_mask, ALU.mult).then_inc(S["h_masked"], 1)
            dve.wait_ge(S["h_e32"], n)
            for m in range(2):
                dve.wait_ge(S[f"h_ds{m}"], n)
                for h in range(HEADS):
                    up = dve.scalar_tensor_tensor(out=state[:, h, :], in0=state[:, h, :], scalar=e32[:, h, m:m + 1],
                                                  in1=ps[:, 4 + h % 2, (h // 2) * P:(h // 2 + 1) * P], op0=ALU.mult, op1=ALU.add)
                up.then_inc(S[f"h_state{m}"], 1)
            dve.wait_ge(S["h_rs"], n)
            dve.tensor_tensor(o_n, h_out, o_rs, ALU.mult).then_inc(S["h_on"], 1)
            dve.wait_ge(S["h_on"], n)
            dve.wait_ge(S["h_state1"], n)
            gate = by_parity(frames(B5, c * CH, CH))
            dve.tensor_tensor(gate, o_n, gate, ALU.mult).then_inc(S["h_chunk_done"], 1)

        def hgrn_pe(pe, c, n):
            def half(h):
                return slice(64 * (h % 2), 64 * (h % 2) + 64)

            pe.wait_ge(S["h_chunk_done"], n)
            pe.wait_ge(S["h_v"], n)
            for h in range(HEADS):
                mm = pe.matmul(bank[2][half(h), (h // 2) * P:(h // 2 + 1) * P], v_s[:, h, :], ident[:, :], start=True, stop=True)
            mm.then_inc(S["h_v_turned"], 1)
            pe.wait_ge(S["h_kinv"], n)
            pe.wait_ge(S["h_q16"], n)
            for h in range(HEADS):
                pe.matmul(bank[0][half(h), (h // 2) * CH:(h // 2 + 1) * CH], kinv[:, h, :], q16[:, h, :], start=True, stop=True)
            pe.wait_ge(S["h_kh16"], n)
            for h in range(HEADS):
                mm = pe.matmul(bank[0][half(h), 256 + (h // 2) * CH:256 + (h // 2 + 1) * CH], kh16[:, h, :], q16[:, h, :], start=True, stop=True)
            mm.then_inc(S["h_scores"], 1)
            pe.wait_ge(S["h_kh32"], n)
            for h in range(HEADS):
                mm = pe.matmul(bank[1][half(h), (h // 2) * P:(h // 2 + 1) * P], kh32[:, h, :], ident[:, :], start=True, stop=True)
            mm.then_inc(S["h_k_turned"], 1)
            pe.wait_ge(S["h_q32"], n)
            pe.wait_ge(S["h_masked"], n)
            pe.wait_ge(S["h_v_tok"], n)
            for h in range(HEADS):
                for e in range(2):
                    pe.matmul(bank[6 + h % 2][:, (h // 2) * CH:(h // 2 + 1) * CH], v_tok[half(h), h // 2, :], sc[half(h), e, h // 2, :],
                              start=(h < 2 and e == 0), stop=False, skip_group_check=True)
            for m in range(2):
                if m:
                    pe.wait_ge(S["h_state0"], n)
                else:
                    pe.wait_ge(S["h_k_tok"], n)
                for h in range(HEADS):
                    at = (h // 2) * CH + 32 * m
                    mm = pe.matmul(bank[6 + h % 2][:, at:at + 32], state[:, h, :], q32[:, h, 32 * m:32 * m + 32],
                                   start=False, stop=(m == 1 and h >= HEADS - 2), skip_group_check=True)
                if m:
                    mm.then_inc(S["h_o"], 1)
                for h in range(HEADS):
                    part = slice(64 * (h % 2) + 32 * m, 64 * (h % 2) + 32 * m + 32)
                    mm = pe.matmul(ps[:, 4 + h % 2, (h // 2) * P:(h // 2 + 1) * P], k_tok[part, h // 2, :], v_tok[part, h // 2, :],
                                   start=True, stop=True)
                mm.then_inc(S[f"h_ds{m}"], 1)
            pe.wait_ge(S["h_o_sq"], n)
            pe.matmul(bank[3], ones[:, :], o_sq.rearrange("p q a t -> p (q a t)"), start=True, stop=True).then_inc(S["h_ms"], 1)

        with nc.Block() as block:
            @block.gpsimd
            def _(pool):
                pool.memset(h_mask[:, :, :, :], 1.0).then_inc(S["h_mask_ones"], 1)
                pool.memset(h_scan, 1.0).then_inc(S["h_scan_ones"], 1)
                pool.memset(state[:, :, :], 0.0).then_inc(S["h_state_zero"], 1)
                pool.wait_ge(S["h_scan_ones"], 1)
                pool.memset(h_scan.rearrange("p (m l) -> p m l", l=16)[:, :, 0:1], 0.0).then_inc(S["h_masks"], 1)
                pool.wait_ge(S["h_mask_ones"], 1)
                pool.wait_ge(S["h_masks"], 1)
                k = 0
                for q in range(2):
                    r = slice(64 * q, 64 * q + 64)
                    a = h_mask[r, 0, :, :].rearrange("p a (b l) -> p a b l", l=16)
                    z = h_mask[r, 1, :, :].rearrange("p a (b e l) -> p a b e l", e=2, l=16)
                    pool.memset(z[:, :, :, 0, :], 0.0).then_inc(S["h_mask_cut"], 1)
                    k += 1
                    pool.wait_ge(S["h_mask_cut"], k)
                    for view, pattern, base, mult in (
                            (a, [[0, 4], [16, 4], [1, 16]], 0, -1),
                            (a, [[0, 4], [-16, 4], [0, 16]], 0, 1),
                            (z[:, :, :, 1, :], [[0, 4], [-32, 2], [0, 16]], 0, 1),
                            (z[:, :, :, 1, :], [[0, 4], [32, 2], [0, 16]], 15, -1)):
                        k += 1
                        pool.affine_select(out=view, in_=view, compare_op=ALU.is_ge, fill=0.0, base=base,
                                           pattern=pattern, channel_multiplier=mult).then_inc(S["h_mask_cut"], 1)
                        pool.wait_ge(S["h_mask_cut"], k)
                pool.wait_ge(S["h_state_zero"], 1)
                pool.wait_ge(S["h_masks"], 1)
                pool.sem_inc(S["h_chunk_done"], 1)

            @block.sync
            def _(sp):
                heads = "h k v -> k h v"
                sp.wait_ge(S["h_chunk_done"], NCH + 1)
                sp.dma_start(O["hgrn_prompt"][0, 0].rearrange(heads, h=HEADS), state[:, :, :]).then_inc(S["h_state_out"], 16)
                sp.wait_ge(S["h_state_out"], 16)
                sp.dma_start(state[:, :, :], I["state_hgrn"][0, 0].rearrange(heads, h=HEADS)).then_inc(S["h_state_in"], 16)
                sp.wait_ge(S["h_chunk_done"], NCH + 2)
                sp.dma_start(O["hgrn_sample"][0, 0].rearrange(heads, h=HEADS), state[:, :, :]).then_inc(S["h_state_out"], 16)
                sp.wait_ge(S["h_state_out"], 32)

            @block.scalar
            def _(act):
                with act.Fori(0, NCH) as c:
                    hgrn_act(act, c, act.snap(c + 1))
                hgrn_act(act, NCH, NCH + 1)

            @block.vector
            def _(dve):
                with dve.Fori(0, NCH) as c:
                    hgrn_dve(dve, c, dve.snap(c + 1))
                dve.wait_ge(S["h_state_in"], 16)
                hgrn_dve(dve, NCH, NCH + 1)

            @block.tensor
            def _(pe):
                with pe.Fori(0, NCH) as c:
                    hgrn_pe(pe, c, pe.snap(c + 1))
                pe.wait_ge(S["h_state_in"], 16)
                hgrn_pe(pe, NCH, NCH + 1)

        S.end_stage()

        l_sp, l_pe, l_leave = linear([("keep", w_in, COL_RWKV, 12, XN, B2), ("keep", w_in, COL_GATES + D, 4, XN, B6)])
        w_lora = shaped(scr[:, :], 0, (FT, LORA))
        lora_tiles = [(0, P), (P, P), (2 * P, LORA - 2 * P)]

        with nc.Block() as block:
            @block.sync
            def _(sp):
                sp.dma_start(w_lora, w_in.rearrange("(k p) n -> p k n", p=P)[:, :, COL_RWKV + 3 * D:COL_RWKV + N_RWKV]).then_inc(S["w_lora_in"], 16)
                l_sp(sp)

            @block.scalar
            def _(act):
                l_leave(act, False)
                act.wait_ge(S["lora_done"], 1)
                for t, (c0, m) in enumerate(lora_tiles):
                    act.copy(lora[0:m, t, 1:1 + N].rearrange("p (h n) -> p h n", h=2), ps[0:m, 2 * t:2 * t + 2, 0:HALF]).then_inc(S["lora_kept"], 1)
                act.activation(whole(B6), whole(B6), ACT.Sigmoid).then_inc(S["gb_sig"], 1)

            @block.tensor
            def _(pe):
                l_pe(pe)
                pe.wait_ge(S["w_lora_in"], 16)
                pe.wait_ge(S["banks0_free"], used[0] + 1)
                pe.wait_ge(S["banks1_free"], used[0] + 1)
                for t, (c0, m) in enumerate(lora_tiles):
                    for h in range(2):
                        for k in range(FT):
                            mm = pe.matmul(ps[0:m, 2 * t + h, 0:HALF], w_lora[:, k, c0:c0 + m],
                                           arena[:, XN + k, 1 + h * HALF:1 + (h + 1) * HALF], start=(k == 0), stop=(k == FT - 1))
                mm.then_inc(S["lora_done"], 1)

        S.end_stage()

        xroom = Room(flat[:, XN * BW:(XN + FT) * BW], FT * BW)
        rroom = Room(ring_flat, 2 * FT * UNIT)
        room = Room(scr[:, :], SCR)
        wa2, g2a, g2b = room.take(D), room.take(D), room.take(D)
        d16low, d16up, offup, strictup, inclup, eye = (room.take(CH) for _ in range(6))
        r_scan = room.take(FT * CH)
        v_d, l_d, l_s, l_a = room.take(FT, CH), room.take(3, CH), room.take(3, CH), room.take(3, CH)
        sa = room.take(2, FT, CH)
        sg_s, a_s = sa[:, 0], sa[:, 1]
        rb_s = room.take(FT, CH)
        w_dec = room.take(FT, CH + 2)
        iw = room.take(FT, CH)
        ar = room.take(FT, 2, CH)
        bh, kh = room.take(FT, CH), room.take(FT, CH)
        bonus, gg = room.take(FT, CH), room.take(FT, CH)
        t1, a1, nt = room.take(FT, CH), room.take(FT, CH), room.take(FT, CH)
        r_s, k_s2, v_s2 = xroom.take(FT, CH), xroom.take(FT, CH), xroom.take(FT, CH)
        d_r, d_k = xroom.take(FT, CH), xroom.take(FT, CH)
        kk, kmod, bka, rn = (xroom.take(FT, CH) for _ in range(4))
        b_tok, k_tok2, v_tok2 = (rroom.take(FT, CH) for _ in range(3))
        takT, trbT, trkT = (rroom.take(FT, CH) for _ in range(3))
        z_s, u_s = rroom.take(FT, CH), rroom.take(FT, CH)
        st = room.take(FT, CH)
        a2t2, a4, t4, t8, qt = sa, d_r, d_k, v_d, rb_s
        q_inv = kk
        ff = shaped(xroom.flat, 6 * FT * CH, (2, FT, CH))
        f2, y_s, mt = rn, r_s, k_s2
        o_c, o_q, o_r = a1, t1, nt
        st_vk = z_s
        st_in = u_s
        w_last = w_dec[:, :, CH:CH + 1].to_broadcast([P, FT, CH])
        w_prev, w_cur = w_dec[:, :, 0:CH], w_dec[:, :, 1:CH + 1]

        def pairs(m):
            return m.unsqueeze(1).to_broadcast([P, FT, CH])

        def q_half(q):
            return slice(64 * q, 64 * q + 64)

        def b_cols(b, a):
            return bank[b][:, a * CH:(a + 1) * CH]

        mu = cb[:, MU:MU + 27]

        def per_head(pe, b, lhsT, rhs, start=True, stop=True):
            for a in range(FT):
                for q in range(2):
                    r = q_half(q)
                    mm = pe.matmul(bank[b][r, a * CH:(a + 1) * CH], lhsT[r, a, :], rhs[r, a, :], start=start, stop=stop)
            return mm

        eye2 = [ident[q_half(q), q_half(q)] for q in range(2)]

        def turn_heads(pe, b, x):
            for a in range(FT):
                for q in range(2):
                    mm = pe.matmul(bank[b][q_half(q), a * CH:(a + 1) * CH], x[q_half(q), a, :], eye2[q], start=True, stop=True)
            return mm

        def rwkv_pool(pool, c, n, last):
            pool.wait_ge(S["r_chunk_done"], n)
            cur, prev = lora[:, :, bass.ds(c * CH + 1, CH)], lora[:, :, bass.ds(c * CH, CH)]
            pool.tensor_tensor(l_d, prev, cur, ALU.subtract).then_inc(S["r_ld"], 1)
            pool.wait_ge(S["r_ld"], n)
            pool.tensor_tensor(l_d, l_d, over(mu[:, 24:27], CH), ALU.mult).then_inc(S["r_lm"], 1)
            pool.wait_ge(S["r_masks"], 1)
            pool.wait_ge(S["r_lm"], n)
            pool.tensor_tensor(l_s, l_d, cur, ALU.add).then_inc(S["r_l"], 1)
            cur, prev = frames(B4, c * CH, CH), frames(B4, c * CH - 1, CH)
            pool.tensor_tensor(v_d, prev, cur, ALU.subtract).then_inc(S["r_vd"], 1)
            pool.wait_ge(S["r_vd"], n)
            pool.tensor_tensor(v_d, v_d, over(mu[:, 16:24], CH), ALU.mult).then_inc(S["r_vm"], 1)
            pool.wait_ge(S["r_masks"], 1)
            pool.wait_ge(S["r_vm"], n)
            pool.tensor_tensor(v_s2, v_d, cur, ALU.add).then_inc(S["r_v"], 1)
            pool.wait_ge(S["r_kmod"], n)
            pool.wait_ge(S["r_r"], n)
            pool.tensor_tensor(bonus, r_s, kmod, ALU.mult).then_inc(S["r_rk0"], 1)
            pool.wait_ge(S["r_rk0"], n)
            pool.tensor_tensor(bonus, bonus, over(col("rwkv_r_k"), CH), ALU.mult).then_inc(S["r_rk"], 1)
            pool.wait_ge(S["r_g"], n)
            pool.tensor_tensor(gg, gg, frames(B6, c * CH, CH), ALU.mult).then_inc(S["r_gg"], 1)

        def rwkv_act(act, c, n, last):
            act.wait_ge(S["r_l"], n)
            act.activation(l_a[0:64, 0, :], l_s[0:64, 0, :], ACT.Exp, scale=-2.0)
            act.activation(l_a[:, 1:3, :], l_s[:, 1:3, :], ACT.Exp, scale=-1.0).then_inc(S["r_la_exp"], 1)
            act.wait_ge(S["r_kk0"], n)
            act.activation(rn, kk, ACT.Square).then_inc(S["r_kk_sq"], 1)
            act.wait_ge(S["r_ssm"], n)
            act.activation(rn, rn, ACT.Ln, scale=2.0 ** 30).then_inc(S["r_ln_ss"], 1)
            act.wait_ge(S["r_ln_ss"], n)
            act.activation(rn, rn, ACT.Exp, scale=-0.5, bias=kk_c).then_inc(S["r_rn"], 1)
            act.wait_ge(S["r_pre"], n)
            act.activation(sa, sa, ACT.Exp, scale=-1.0).then_inc(S["r_sa_exp"], 1)
            act.wait_ge(S["r_glora"], n)
            act.copy(gg, split_heads(bank[2])).then_inc(S["r_g"], 1)
            act.wait_ge(S["r_b"], n)
            act.activation(w_cur, rb_s, ACT.Exp, scale=-DECAY).then_inc(S["r_w"], 1)
            act.activation(iw, rb_s, ACT.Exp, scale=DECAY).then_inc(S["r_iw"], 1)
            act.wait_ge(S["r_v_turned"], n)
            act.copy(v_tok2, split_heads(bank[7])).then_inc(S["r_v_tok"], 1)
            act.wait_ge(S["r_b_turned"], n)
            act.copy(b_tok, split_heads(bank[5])).then_inc(S["r_b_tok"], 1)
            act.wait_ge(S["r_k_turned"], n)
            act.copy(k_tok2, split_heads(bank[6])).then_inc(S["r_k_tok"], 1)
            act.wait_ge(S["r_sq2"], n)
            act.copy(a2t2, ps[:, 5:7, :].rearrange("p e (a b) -> p e a b", a=8)).then_inc(S["r_a2t2"], 1)
            act.wait_ge(S["r_sq4"], n)
            act.copy(t4, split_heads(bank[6])).then_inc(S["r_t4"], 1)
            act.copy(a4, split_heads(bank[5])).then_inc(S["r_a4"], 1)
            act.wait_ge(S["r_sq8"], n)
            act.copy(t8, split_heads(bank[5])).then_inc(S["r_t8"], 1)
            act.wait_ge(S["r_q_turned"], n)
            act.copy(q_inv, split_heads(bank[5])).then_inc(S["r_q"], 1)
            act.wait_ge(S["r_rk"], n)
            act.wait_ge(S["r_f_done"], n)
            act.copy(ff, ps[:, 6:8, :].rearrange("p e (a b) -> p e a b", a=8)).then_inc(S["r_f"], 1)
            act.wait_ge(S["r_f2_done"], n)
            act.copy(f2, split_heads(bank[5])).then_inc(S["r_f2"], 1)
            act.wait_ge(S["r_z_done"], n)
            act.copy(z_s, split_heads(bank[0])).then_inc(S["r_z"], 1)
            act.wait_ge(S["r_mt_done"], n)
            act.copy(mt, split_heads(bank[7])).then_inc(S["r_mt"], 1)
            act.wait_ge(S["r_u_done"], n)
            act.copy(u_s, split_heads(bank[1])).then_inc(S["r_u"], 1)
            act.wait_ge(S["r_o_done"], n)
            act.copy(o_c, split_heads(bank[2])).then_inc(S["r_o"], 1)
            act.wait_ge(S["r_oc"], n)
            act.activation(o_q, o_c, ACT.Square).then_inc(S["r_o_sq"], 1)
            act.wait_ge(S["r_var"], n)
            act.activation(o_r, split_heads(bank[5]), ACT.Ln, scale=1.0 / 64, bias=gn_eps_c).then_inc(S["r_ln_var"], 1)
            act.wait_ge(S["r_ln_var"], n)
            act.activation(o_r, o_r, ACT.Exp, scale=-0.5).then_inc(S["r_rstd"], 1)

        def rwkv_dve(dve, c, n, last):
            pad = slice(DEC, CH)
            dve.wait_ge(S["r_chunk_done"], n)
            r_cur, k_cur = frames(B2, c * CH, CH), frames(B3, c * CH, CH)
            dve.tensor_tensor(d_k, frames(B3, c * CH - 1, CH), k_cur, ALU.subtract).then_inc(S["r_kd"], 1)
            dve.tensor_tensor(d_r, frames(B2, c * CH - 1, CH), r_cur, ALU.subtract).then_inc(S["r_rd"], 1)
            dve.wait_ge(S["r_kd"], n)
            dve.tensor_tensor(d_k, d_k, over(mu[:, 8:16], CH), ALU.mult).then_inc(S["r_km"], 1)
            dve.wait_ge(S["r_rd"], n)
            dve.tensor_tensor(d_r, d_r, over(mu[:, 0:8], CH), ALU.mult).then_inc(S["r_rm"], 1)
            dve.wait_ge(S["r_km"], n)
            dve.tensor_tensor(k_s2, d_k, k_cur, ALU.add).then_inc(S["r_k"], 1)
            dve.wait_ge(S["r_rm"], n)
            dve.tensor_tensor(r_s, d_r, r_cur, ALU.add).then_inc(S["r_r"], 1)
            dve.wait_ge(S["r_k"], n)
            dve.tensor_tensor(kk, k_s2, over(col("rwkv_k_k"), CH), ALU.mult).then_inc(S["r_kk0"], 1)
            dve.wait_ge(S["r_la_exp"], n)
            dve.tensor_scalar(l_a[0:64, 0, :], l_a[0:64, 0, :], 1.0, None, ALU.add)
            dve.tensor_scalar(l_a[:, 1:3, :], l_a[:, 1:3, :], 1.0, None, ALU.add).then_inc(S["r_la_1"], 1)
            dve.wait_ge(S["r_la_1"], n)
            dve.reciprocal(l_a[0:64, 0, :], l_a[0:64, 0, :]).then_inc(S["r_la_tr"], 1)
            dve.reciprocal(l_a[:, 1:3, :], l_a[:, 1:3, :]).then_inc(S["r_la_sg"], 1)
            dve.wait_ge(S["r_la_tr"], n)
            dve.tensor_scalar(l_a[0:64, 0, :], l_a[0:64, 0, :], 2.0, -1.0, ALU.mult, ALU.add).then_inc(S["r_la_th"], 1)
            dve.wait_ge(S["r_kk_ss"], n)
            dve.wait_ge(S["r_kk_sq"], n)
            dve.tensor_scalar(rn, split_heads(bank[3]), 1e-24, None, ALU.max).then_inc(S["r_ssm"], 1)
            dve.wait_ge(S["r_wlora"], n)
            dve.tensor_tensor(sg_s, split_heads(bank[0]), over(col("rwkv_w0"), CH), ALU.add)
            dve.tensor_tensor(a_s, split_heads(bank[1]), over(col("rwkv_a0"), CH), ALU.add).then_inc(S["r_pre"], 1)
            dve.wait_ge(S["r_sa_exp"], n)
            dve.tensor_scalar(sa, sa, 1.0, None, ALU.add).then_inc(S["r_sa_1"], 1)
            dve.wait_ge(S["r_sa_1"], n)
            dve.reciprocal(sa, sa).then_inc(S["r_sa"], 1)
            dve.wait_ge(S["r_sa"], n)
            if last:
                dve.memset(sg_s[:, :, pad], 0.0).then_inc(S["r_pad"], 1)
                dve.wait_ge(S["r_pad"], 1)
            dve.tensor_tensor_scan(flat2(rb_s), r_scan, flat2(sg_s), 0.0, ALU.mult, ALU.add).then_inc(S["r_b"], 1)
            dve.scalar_tensor_tensor(out=kmod, in0=a_s, scalar=-1.0, in1=over(col("rwkv_k_a"), CH), op0=ALU.add, op1=ALU.mult).then_inc(S["r_ka"], 1)
            dve.wait_ge(S["r_rn"], n)
            dve.tensor_tensor(kk, kk, rn, ALU.mult).then_inc(S["r_kkn"], 1)
            dve.wait_ge(S["r_ka"], n)
            dve.scalar_tensor_tensor(out=kmod, in0=kmod, scalar=1.0, in1=k_s2, op0=ALU.add, op1=ALU.mult).then_inc(S["r_kmod0"], 1)
            dve.wait_ge(S["r_kkn"], n)
            dve.tensor_tensor(bka, kk, a_s, ALU.mult).then_inc(S["r_bka"], 1)
            dve.wait_ge(S["r_bka"], n)
            dve.wait_ge(S["r_kmod0"], n)
            if last:
                dve.memset(kmod[:, :, pad], 0.0).then_inc(S["r_pad"], 1)
                dve.memset(bka[:, :, pad], 0.0).then_inc(S["r_pad"], 1)
                dve.wait_ge(S["r_pad"], 3)
            dve.sem_inc(S["r_kmod"], 1)
            dve.wait_ge(S["r_iw"], n)
            dve.tensor_tensor(bh, bka, iw, ALU.mult).then_inc(S["r_bh"], 1)
            dve.wait_ge(S["r_w"], n)
            dve.scalar_tensor_tensor(out=ar[:, :, 0, :], in0=kk, scalar=-1.0, in1=w_prev, op0=ALU.mult, op1=ALU.mult).then_inc(S["r_ah"], 1)
            dve.tensor_tensor(ar[:, :, 1, :], r_s, w_cur, ALU.mult).then_inc(S["r_rh"], 1)
            dve.tensor_tensor(kh, kmod, iw, ALU.mult).then_inc(S["r_kh"], 1)
            two = lambda b: ps[:, b:b + 2, :].rearrange("p b (a e t) -> p (b a) e t", a=4, e=2)
            dve.wait_ge(S["r_t_done"], n)
            dve.tensor_tensor(t1, split_heads(bank[0]), pairs(d16low), ALU.mult).then_inc(S["r_t1"], 1)
            dve.wait_ge(S["r_tt_done"], n)
            dve.tensor_tensor(a1, two(1)[:, :, 0, :], pairs(d16up), ALU.mult).then_inc(S["r_a1"], 1)
            dve.tensor_tensor(nt, two(1)[:, :, 0, :], pairs(offup), ALU.mult).then_inc(S["r_nt"], 1)
            dve.tensor_tensor(trbT, two(1)[:, :, 1, :], pairs(inclup), ALU.mult).then_inc(S["r_trb"], 1)
            dve.wait_ge(S["r_a1"], n)
            dve.tensor_tensor(qt, a1, pairs(eye), ALU.add).then_inc(S["r_qt1"], 1)
            dve.wait_ge(S["r_rk_ss"], n)
            dve.wait_ge(S["r_v"], n)
            dve.tensor_tensor(bonus, split_heads(bank[4]), v_s2, ALU.mult).then_inc(S["r_bonus"], 1)
            dve.wait_ge(S["r_tk_done"], n)
            dve.tensor_tensor(takT, two(3)[:, :, 0, :], pairs(strictup), ALU.mult).then_inc(S["r_tak"], 1)
            dve.tensor_tensor(trkT, two(3)[:, :, 1, :], pairs(inclup), ALU.mult).then_inc(S["r_trk"], 1)
            dve.wait_ge(S["r_qt1"], n)
            for k, (stage, b) in enumerate((("r_q2_done", 7), ("r_q3_done", 6), ("r_q4_done", 7))):
                dve.wait_ge(S[stage], n)
                if k:
                    dve.wait_ge(S[f"r_qt{k + 1}"], n)
                dve.tensor_tensor(qt, qt, split_heads(bank[b]), ALU.add).then_inc(S[f"r_qt{k + 2}"], 1)
            dve.wait_ge(S["r_f"], n)
            dve.tensor_tensor(y_s, ff[:, 0], pairs(eye), ALU.add).then_inc(S["r_y1"], 1)
            dve.wait_ge(S["r_y1"], n)
            dve.wait_ge(S["r_f2"], n)
            dve.tensor_tensor(y_s, y_s, f2, ALU.add).then_inc(S["r_y2"], 1)
            dve.wait_ge(S["r_y2"], n)
            dve.wait_ge(S["r_f3_done"], n)
            dve.tensor_tensor(y_s, y_s, split_heads(bank[6]), ALU.add).then_inc(S["r_y"], 1)
            dve.wait_ge(S["r_o_done"], n)
            dve.tensor_tensor(st, st, split_heads(bank[3]), ALU.add).then_inc(S["r_st0"], 1)
            dve.wait_ge(S["r_st0"], n)
            dve.tensor_tensor(st, st, w_last, ALU.mult).then_inc(S["r_st"], 1)
            dve.wait_ge(S["r_mean"], n)
            dve.wait_ge(S["r_o"], n)
            dve.scalar_tensor_tensor(out=o_c, in0=split_heads(bank[4]), scalar=-1.0 / 64, in1=o_c, op0=ALU.mult, op1=ALU.add).then_inc(S["r_oc"], 1)
            dve.wait_ge(S["r_rstd"], n)
            dve.tensor_tensor(o_c, o_c, o_r, ALU.mult).then_inc(S["r_e1"], 1)
            dve.wait_ge(S["r_e1"], n)
            dve.tensor_tensor(o_c, o_c, over(col("rwkv_ln_g"), CH), ALU.mult).then_inc(S["r_e2"], 1)
            dve.wait_ge(S["r_e2"], n)
            dve.tensor_tensor(o_c, o_c, over(col("rwkv_ln_b"), CH), ALU.add).then_inc(S["r_e3"], 1)
            dve.wait_ge(S["r_e3"], n)
            dve.wait_ge(S["r_bonus"], n)
            dve.tensor_tensor(o_c, o_c, bonus, ALU.add).then_inc(S["r_e4"], 1)
            dve.wait_ge(S["r_e4"], n)
            dve.wait_ge(S["r_gg"], n)
            dve.tensor_tensor(o_c, o_c, gg, ALU.mult).then_inc(S["r_e5"], 1)
            dve.wait_ge(S["r_e5"], n)
            dve.wait_ge(S["r_st"], n)
            dve.tensor_tensor(frames(B5, c * CH, CH), frames(B5, c * CH, CH), o_c, ALU.add).then_inc(S["r_chunk_done"], 1)

        def rwkv_pe(pe, c, n, last):
            def const():
                pe.wait_ge(S["r_masks"], 1)

            pe.wait_ge(S["r_kk_sq"], n)
            pe.matmul(bank[3], head_ones[:, :], flat2(rn), start=True, stop=True).then_inc(S["r_kk_ss"], 1)
            pe.wait_ge(S["r_l"], n)
            for f in range(FT):
                pe.matmul(b_cols(1, f), wa2[64:128, f * P:(f + 1) * P], l_s[64:128, 0, :], start=True, stop=True)
            pe.wait_ge(S["r_la_th"], n)
            for f in range(FT):
                mm = pe.matmul(b_cols(0, f), wa2[0:64, f * P:(f + 1) * P], l_a[0:64, 0, :], start=True, stop=True)
            mm.then_inc(S["r_wlora"], 1)
            pe.wait_ge(S["r_la_sg"], n)
            for f in range(FT):
                pe.matmul(b_cols(2, f), g2a[:, f * P:(f + 1) * P], l_a[:, 1, :], start=True, stop=False)
                mm = pe.matmul(b_cols(2, f), g2b[0:32, f * P:(f + 1) * P], l_a[0:32, 2, :], start=False, stop=True)
            mm.then_inc(S["r_glora"], 1)
            const()
            pe.wait_ge(S["r_v"], n)
            turn_heads(pe, 7, v_s2).then_inc(S["r_v_turned"], 1)
            pe.wait_ge(S["r_rk"], n)
            pe.matmul(bank[4], head_ones[:, :], flat2(bonus), start=True, stop=True).then_inc(S["r_rk_ss"], 1)
            const()
            pe.wait_ge(S["r_bh"], n)
            turn_heads(pe, 5, bh).then_inc(S["r_b_turned"], 1)
            const()
            pe.wait_ge(S["r_ah"], n)
            per_head(pe, 0, ar[:, :, 0, :], bh).then_inc(S["r_t_done"], 1)

            def both(b, x):
                for a in range(FT):
                    for q in range(2):
                        mm = pe.matmul(bank[b + a // 4][q_half(q), (a % 4) * 2 * CH:(a % 4 + 1) * 2 * CH], x[q_half(q), a, :],
                                       ar[q_half(q), a, :, :], start=True, stop=True)
                return mm

            const()
            pe.wait_ge(S["r_g"], n)
            pe.wait_ge(S["r_rh"], n)
            both(1, bh).then_inc(S["r_tt_done"], 1)
            const()
            pe.wait_ge(S["r_kh"], n)
            turn_heads(pe, 6, kh).then_inc(S["r_k_turned"], 1)
            const()
            pe.wait_ge(S["r_bonus"], n)
            both(3, kh).then_inc(S["r_tk_done"], 1)
            const()
            pe.wait_ge(S["r_b_tok"], n)
            pe.wait_ge(S["r_k_tok"], n)
            pe.wait_ge(S["r_t1"], n)
            pe.wait_ge(S["r_a1"], n)
            per_head(pe, 5, t1, a1)
            per_head(pe, 6, a1, t1).then_inc(S["r_sq2"], 1)
            const()
            pe.wait_ge(S["r_a2t2"], n)
            per_head(pe, 5, a2t2[:, 1], a2t2[:, 0])
            per_head(pe, 6, a2t2[:, 0], a2t2[:, 1]).then_inc(S["r_sq4"], 1)
            const()
            pe.wait_ge(S["r_v_tok"], n)
            pe.wait_ge(S["r_qt1"], n)
            per_head(pe, 7, a2t2[:, 1], qt).then_inc(S["r_q2_done"], 1)
            const()
            pe.wait_ge(S["r_a4"], n)
            per_head(pe, 5, a4, t4).then_inc(S["r_sq8"], 1)
            const()
            pe.wait_ge(S["r_qt2"], n)
            per_head(pe, 6, t4, qt).then_inc(S["r_q3_done"], 1)
            const()
            pe.wait_ge(S["r_tak"], n)
            pe.wait_ge(S["r_t1"], n)
            for a in range(FT):
                for q in range(2):
                    r = q_half(q)
                    pe.matmul(bank[0][r, a * CH:(a + 1) * CH], takT[r, a, :], v_tok2[r, a, :], start=True, stop=False)
                    mm = pe.matmul(bank[0][r, a * CH:(a + 1) * CH], ar[r, a, 0, :], st[r, a, :], start=False, stop=True)
            mm.then_inc(S["r_z_done"], 1)
            const()
            pe.wait_ge(S["r_t8"], n)
            pe.wait_ge(S["r_qt3"], n)
            per_head(pe, 7, t8, qt).then_inc(S["r_q4_done"], 1)
            const()
            pe.wait_ge(S["r_qt4"], n)
            turn_heads(pe, 5, qt).then_inc(S["r_q_turned"], 1)
            const()
            pe.wait_ge(S["r_nt"], n)
            pe.wait_ge(S["r_q"], n)
            per_head(pe, 6, nt, q_inv)
            per_head(pe, 7, q_inv, nt).then_inc(S["r_f_done"], 1)
            const()
            pe.wait_ge(S["r_f"], n)
            per_head(pe, 5, ff[:, 1], ff[:, 0]).then_inc(S["r_f2_done"], 1)
            const()
            pe.wait_ge(S["r_f2"], n)
            per_head(pe, 6, ff[:, 1], f2).then_inc(S["r_f3_done"], 1)
            const()
            pe.wait_ge(S["r_y"], n)
            per_head(pe, 7, y_s, qt).then_inc(S["r_mt_done"], 1)
            const()
            pe.wait_ge(S["r_z"], n)
            pe.wait_ge(S["r_mt"], n)
            pe.wait_ge(S["r_trb"], n)
            per_head(pe, 1, mt, z_s).then_inc(S["r_u_done"], 1)
            const()
            pe.wait_ge(S["r_u"], n)
            pe.wait_ge(S["r_trk"], n)
            for a in range(FT):
                for q in range(2):
                    r = q_half(q)
                    out = bank[3][r, a * CH:(a + 1) * CH]
                    pe.matmul(out, b_tok[r, a, :], u_s[r, a, :], start=True, stop=False)
                    mm = pe.matmul(out, k_tok2[r, a, :], v_tok2[r, a, :], start=False, stop=True)
            for a in range(FT):
                for q in range(2):
                    r = q_half(q)
                    out = bank[2][r, a * CH:(a + 1) * CH]
                    pe.matmul(out, st[r, a, :], ar[r, a, 1, :], start=True, stop=False)
                    pe.matmul(out, u_s[r, a, :], trbT[r, a, :], start=False, stop=False)
                    mm = pe.matmul(out, v_tok2[r, a, :], trkT[r, a, :], start=False, stop=True)
            mm.then_inc(S["r_o_done"], 1)
            pe.wait_ge(S["r_o"], n)
            pe.matmul(bank[4], head_ones[:, :], flat2(o_c), start=True, stop=True).then_inc(S["r_mean"], 1)
            pe.wait_ge(S["r_o_sq"], n)
            pe.matmul(bank[5], head_ones[:, :], flat2(o_q), start=True, stop=True).then_inc(S["r_var"], 1)

        ends = ((0, SEQ), (32, N))
        shift_cols = rows_a
        shift_rows = rows_b
        full = N_RWKV // P
        rest = N_RWKV - full * P

        with nc.Block() as block:
            @block.gpsimd
            def _(pool):
                for m in (d16low, d16up, offup, strictup, inclup, eye):
                    pool.memset(m, 1.0).then_inc(S["r_mask_ones"], 1)
                pool.memset(r_scan, 1.0).then_inc(S["r_mask_ones"], 1)
                pool.memset(st, 0.0).then_inc(S["r_mask_ones"], 1)
                pool.memset(w_dec[:, :, 0:1], 1.0).then_inc(S["r_mask_ones"], 1)
                pool.wait_ge(S["r_mask_ones"], 9)
                pool.memset(r_scan.rearrange("p (m l) -> p m l", l=CH)[:, :, 0:1], 0.0).then_inc(S["r_scan_ready"], 1)
                pool.wait_ge(S["r_scan_ready"], 1)
                k = 0

                def cut(m, pattern, base, mult, op=ALU.is_ge):
                    pool.affine_select(out=m, in_=m, compare_op=op, fill=0.0, base=base, pattern=pattern,
                                       channel_multiplier=mult).then_inc(S["r_mask_cut"], 1)

                for q in range(2):
                    r = q_half(q)
                    b16 = lambda m: m[r].rearrange("p (b l) -> p b l", l=16)
                    steps = [
                        [(d16low[r], [[-1, CH]], -1, 1), (d16up[r], [[1, CH]], -1, -1), (strictup[r], [[1, CH]], -1, -1),
                         (inclup[r], [[1, CH]], 0, -1), (b16(offup), [[16, 4], [0, 16]], -1, -1)],
                        [(b16(d16low), [[16, 4], [0, 16]], 15, -1), (b16(d16up), [[-16, 4], [0, 16]], 0, 1)],
                    ]
                    for step in steps:
                        for m, pattern, base, mult in step:
                            cut(m, pattern, base, mult)
                            k += 1
                            pool.wait_ge(S["r_mask_cut"], k)
                    cut(eye[r], [[1, CH]], 0, -1, ALU.is_equal)
                    k += 1
                    pool.wait_ge(S["r_mask_cut"], k)
                pool.wait_ge(S["r_lora_in"], 64)
                pool.wait_ge(S["r_ends_kept"], 1)
                pool.sem_inc(S["r_masks"], 1)
                pool.sem_inc(S["r_chunk_done"], 1)
                with pool.Fori(0, NCH) as c:
                    rwkv_pool(pool, c, pool.snap(c + 1), False)
                pool.wait_ge(S["r_swapped"], 1)
                rwkv_pool(pool, NCH, NCH + 1, True)

            @block.sync
            def _(sp):
                sp.dma_start(wa2[0:64, :], I["rwkv_w2"][0]).then_inc(S["r_lora_in"], 16)
                sp.dma_start(wa2[64:128, :], I["rwkv_a2"][0]).then_inc(S["r_lora_in"], 16)
                sp.dma_start(g2a, I["rwkv_g2"][0][0:P, :]).then_inc(S["r_lora_in"], 16)
                sp.dma_start(g2b[0:32, :], I["rwkv_g2"][0][P:GATE_L, :]).then_inc(S["r_lora_in"], 16)
                sp.wait_ge(S["r_ends_kept"], 1)
                for (r0, _), name in zip(ends, ("shift_prompt", "shift_sample")):
                    out = O[name][0, 0, 0]
                    sp.dma_start(out[0:full * P].rearrange("(f p) -> f p", p=P), shift_rows[r0:r0 + full, :]).then_inc(S["r_shift_out"], 16)
                    sp.dma_start(out[full * P:N_RWKV].unsqueeze(0), shift_rows[r0 + full:r0 + full + 1, 0:rest]).then_inc(S["r_shift_out"], 16)
                rows = "(a q) v k -> (q v) a k"
                sp.wait_ge(S["r_state_turned"], 1)
                sp.dma_start(O["rwkv_prompt"][0, 0].rearrange(rows, q=2), st_vk).then_inc(S["r_state_out"], 16)
                sp.dma_start(st_in, I["state_rwkv"][0, 0].rearrange(rows, q=2)).then_inc(S["r_state_in"], 16)
                sp.wait_ge(S["r_state_turned"], 2)
                sp.dma_start(O["rwkv_sample"][0, 0].rearrange(rows, q=2), st_vk).then_inc(S["r_state_out"], 16)
                sp.wait_ge(S["r_state_out"], 32)
                sp.wait_ge(S["r_shift_out"], 64)

            @block.scalar
            def _(act):
                with act.Fori(0, NCH) as c:
                    rwkv_act(act, c, act.snap(c + 1), False)
                act.wait_ge(S["r_end_turned"], 1)
                act.copy(st_vk, split_heads(bank[6])).then_inc(S["r_state_turned"], 1)
                act.wait_ge(S["r_state_out"], 16)
                act.wait_ge(S["r_swapped"], 1)
                rwkv_act(act, NCH, NCH + 1, True)
                act.wait_ge(S["r_end_turned"], 2)
                act.copy(st_vk, split_heads(bank[6])).then_inc(S["r_state_turned"], 1)

            @block.vector
            def _(dve):
                dve.memset(shift_cols[:, :], 0.0).then_inc(S["r_ends_zero"], 1)
                dve.wait_ge(S["r_ends_zero"], 1)
                for r0, at in ends:
                    for g, base in enumerate((B2, B3, B4)):
                        dve.tensor_copy(shift_cols[:, r0 + 8 * g:r0 + 8 * g + 8].unsqueeze(2), arena[:, base:base + FT, at:at + 1])
                    cp = dve.tensor_copy(shift_cols[:, r0 + 24:r0 + 27].unsqueeze(2), lora[:, :, at:at + 1])
                cp.then_inc(S["r_ends"], 1)
                dve.wait_ge(S["r_ends_turned"], 1)
                dve.tensor_copy(shift_rows[:, :], bank[0][:, 0:P]).then_inc(S["r_ends_kept"], 1)
                with dve.Fori(0, NCH) as c:
                    rwkv_dve(dve, c, dve.snap(c + 1), False)
                dve.wait_ge(S["r_chunk_done"], NCH + 1)
                for g, base in enumerate((B2, B3, B4)):
                    dve.tensor_copy(arena[:, base:base + FT, SEQ:SEQ + 1], cb[:, SHIFT + 8 * g:SHIFT + 8 * g + 8].unsqueeze(2)).then_inc(S["r_swap"], 1)
                dve.tensor_copy(lora[:, :, SEQ:SEQ + 1], cb[:, SHIFT + 24:SHIFT + 27].unsqueeze(2)).then_inc(S["r_swap"], 1)
                dve.wait_ge(S["r_start_turned"], 1)
                dve.tensor_copy(st, split_heads(bank[7])).then_inc(S["r_swap"], 1)
                dve.wait_ge(S["r_swap"], 5)
                dve.sem_inc(S["r_swapped"], 1)
                rwkv_dve(dve, NCH, NCH + 1, True)

            @block.tensor
            def _(pe):
                pe.wait_ge(S["r_ends"], 1)
                pe.transpose(bank[0][:, 0:P], shift_cols[:, :], ident[:, :]).then_inc(S["r_ends_turned"], 1)
                pe.wait_ge(S["r_ends_kept"], 1)
                pe.wait_ge(S["r_masks"], 1)
                with pe.Fori(0, NCH) as c:
                    rwkv_pe(pe, c, pe.snap(c + 1), False)
                pe.wait_ge(S["r_chunk_done"], NCH + 1)
                turn_heads(pe, 6, st).then_inc(S["r_end_turned"], 1)
                pe.wait_ge(S["r_state_in"], 16)
                turn_heads(pe, 7, st_in).then_inc(S["r_start_turned"], 1)
                pe.wait_ge(S["r_swapped"], 1)
                rwkv_pe(pe, NCH, NCH + 1, True)
                pe.wait_ge(S["r_chunk_done"], NCH + 2)
                turn_heads(pe, 6, st).then_inc(S["r_end_turned"], 1)

        S.end_stage()

        mroom = Room(flat[:, B2 * BW:B5 * BW], 3 * FT * BW)
        memT, mem_n, mem_sq = (mroom.take(FT, MEM) for _ in range(3))
        mem_tok = mroom.take(2, D)
        aroom = Room(scr[:, :], SCR)
        kT = [aroom.take(FT, MEM) for _ in range(2)]
        v_mem = [aroom.take(2, D) for _ in range(2)]
        k_mem = [mroom.take(2, D) for _ in range(2)]
        a_sq_base = aroom.at

        l_sp, l_pe, l_leave = linear([("add", I["w_out"][0], 0, 4, B5, H),
                                      ("rows", I["wk_x"][0], 0, 4, mem_n, k_mem[0]), ("rows", I["wv_x"][0], 0, 4, mem_n, v_mem[0])])
        m_act, m_pe, m_dve = norm_stage("mem", memT, mem_n, lambda f: col("norm_mem_g", f), MEM, mem_sq)

        def turn_rows(pe, src, j, b):
            for f in range(4):
                mm = pe.transpose(bank[b][:, f * P:(f + 1) * P], src[:, j // 2, ((j % 2) * 4 + f) * P:((j % 2) * 4 + f + 1) * P], ident[:, :])
            return mm

        def turned(dst, j):
            return dst[:, (j % 2) * 4:(j % 2) * 4 + 4, (j // 2) * P:(j // 2 + 1) * P]

        def quarters(b):
            return bank[b].rearrange("p (f n) -> p f n", f=4)

        with nc.Block() as block:
            @block.sync
            def _(sp):
                sp.dma_start(mem_tok, I["mem_prompt"][0].rearrange("(t p) d -> p t d", p=P)).then_inc(S["mem_in"], 16)
                sp.dma_start(k_mem[1], I["cache_mem_k"][0, 0].rearrange("(t p) h d -> p t (h d)", p=P)).then_inc(S["cache_in"], 16)
                sp.dma_start(v_mem[1], I["cache_mem_v"][0, 0].rearrange("(t p) h d -> p t (h d)", p=P)).then_inc(S["cache_in"], 16)
                l_sp(sp)
                rows = "(t p) h d -> p t (h d)"
                sp.wait_ge(S["banks0_free"], used[0] + 1)
                sp.wait_ge(S["banks1_free"], used[0] + 1)
                sp.dma_start(O["mem_k"][0, 0].rearrange(rows, p=P), k_mem[0]).then_inc(S["mem_out"], 16)
                sp.dma_start(O["mem_v"][0, 0].rearrange(rows, p=P), v_mem[0]).then_inc(S["mem_out"], 16)
                sp.wait_ge(S["mem_out"], 32)

            @block.scalar
            def _(act):
                act.wait_ge(S["memT"], 4)
                m_act(act)
                l_leave(act, False)

            @block.tensor
            def _(pe):
                pe.wait_ge(S["mem_in"], 16)
                for j in range(4):
                    mm = turn_rows(pe, mem_tok, j, j)
                mm.then_inc(S["mem_turned"], 1)
                pe.wait_ge(S["cache_in"], 32)
                for j in range(4):
                    mm = turn_rows(pe, k_mem[1], j, 4 + j)
                mm.then_inc(S["cache_turned"], 1)
                pe.wait_ge(S["memT"], 4)
                m_pe(pe)
                pe.wait_ge(S["mem_normed"], FT)
                pe.wait_ge(S["cacheT"], 4)
                l_pe(pe)
                pe.wait_ge(S["banks0_free"], used[0] + 1)
                pe.wait_ge(S["banks1_free"], used[0] + 1)
                for j in range(4):
                    mm = turn_rows(pe, k_mem[0], j, j)
                mm.then_inc(S["keys_turned"], 1)

            @block.vector
            def _(dve):
                dve.wait_ge(S["mem_turned"], 1)
                for j in range(4):
                    dve.tensor_copy(turned(memT, j), quarters(j)).then_inc(S["memT"], 1)
                dve.wait_ge(S["cache_turned"], 1)
                for j in range(4):
                    dve.tensor_copy(turned(kT[1], j), quarters(4 + j)).then_inc(S["cacheT"], 1)
                m_dve(dve)
                l_leave(dve, True)
                dve.wait_ge(S["keys_turned"], 1)
                for j in range(4):
                    dve.tensor_copy(turned(kT[0], j), quarters(j)).then_inc(S["keysT"], 1)

        S.end_stage()

        sq_b = shaped(flat, B4 * BW, (FT, N))
        n_act, n_pe, n_dve = norm_stage("x", whole(H), whole(XN), lambda f: col("norm_x_g", f), N, sq_b)
        l_sp, l_pe, l_leave = linear([("keep", I["wq_x"][0], 0, 4, XN, B2)])

        with nc.Block() as block:
            @block.sync
            def _(sp):
                l_sp(sp)

            @block.scalar
            def _(act):
                n_act(act)
                l_leave(act, False)

            @block.tensor
            def _(pe):
                n_pe(pe)
                pe.wait_ge(S["x_normed"], FT)
                pe.wait_ge(S["x_rms"], 2)
                l_pe(pe)

            @block.vector
            def _(dve):
                n_dve(dve)

        S.end_stage()

        q_s, p_s, pT = aroom.take(FT, P), aroom.take(XH, MEM), aroom.take(FT, P)
        mx, sm = aroom.take(XH), aroom.take(XH)

        def attention_act(act, t, n, m):
            act.wait_ge(S["a_tile_done"], n)
            act.copy(q_s[:, :, 0:m], frames(B2, t * P, m)).then_inc(S["a_q"], 1)
            act.wait_ge(S["a_shifted"], n)
            act.activation(p_s[0:m], p_s[0:m], ACT.Exp, scale=XSCALE).then_inc(S["a_exp"], 1)
            act.wait_ge(S["a_turned"], n)
            act.copy(pT[:, :, 0:m], ps[:, 2:4, :].rearrange("p b (f n) -> p (b f) n", f=4)[:, :, 0:m]).then_inc(S["a_pT"], 1)
            act.wait_ge(S["a_o"], n)
            act.copy(frames(B3, t * P, m), ps[:, 4:6, :].rearrange("p b (f n) -> p (b f) n", f=4)[:, :, 0:m]).then_inc(S["a_tile_done"], 1)

        def attention_dve(dve, t, n, m):
            scores = ps[0:m, 0:2, :].rearrange("p b (h k) -> p (b h) k", h=2)
            dve.wait_ge(S["a_scores"], n)
            dve.tensor_reduce(mx[0:m], scores, AX_X, ALU.max).then_inc(S["a_max"], 1)
            dve.wait_ge(S["a_max"], n)
            dve.tensor_tensor(p_s[0:m], scores, mx[0:m].unsqueeze(2).to_broadcast([m, XH, MEM]), ALU.subtract).then_inc(S["a_shifted"], 1)
            dve.wait_ge(S["a_exp"], n)
            dve.tensor_reduce(sm[0:m], p_s[0:m], AX_X, ALU.add).then_inc(S["a_sum"], 1)
            dve.wait_ge(S["a_sum"], n)
            dve.reciprocal(sm[0:m], sm[0:m]).then_inc(S["a_rsum"], 1)
            dve.wait_ge(S["a_rsum"], n)
            dve.tensor_tensor(p_s[0:m], p_s[0:m], sm[0:m].unsqueeze(2).to_broadcast([m, XH, MEM]), ALU.mult).then_inc(S["a_p"], 1)

        def attention_pe(pe, t, n, m, group):
            pe.wait_ge(S["a_q"], n)
            for h in range(XH):
                for k in range(2):
                    mm = pe.matmul(ps[0:m, h // 2, (h % 2) * MEM:(h % 2 + 1) * MEM], q_s[:, 2 * h + k, 0:m], kT[group][:, 2 * h + k, :],
                                   start=(k == 0), stop=(k == 1))
            mm.then_inc(S["a_scores"], 1)
            pe.wait_ge(S["a_p"], n)
            for h in range(XH):
                for j in range(2):
                    b = 2 * h + j
                    mm = pe.transpose(ps[:, 2 + b // 4, (b % 4) * P:(b % 4) * P + m], p_s[0:m, h, j * P:(j + 1) * P], ident[0:m, 0:m])
            mm.then_inc(S["a_turned"], 1)
            pe.wait_ge(S["a_pT"], n)
            for b in range(FT):
                for j in range(2):
                    mm = pe.matmul(ps[:, 4 + b // 4, (b % 4) * P:(b % 4) * P + m], v_mem[group][:, j, b * P:(b + 1) * P], pT[:, 2 * (b // 2) + j, 0:m],
                                   start=(j == 0), stop=(j == 1))
            mm.then_inc(S["a_o"], 1)

        tiles = SEQ // P
        with nc.Block() as block:
            @block.gpsimd
            def _(pool):
                pool.sem_inc(S["a_tile_done"], 1)

            @block.scalar
            def _(act):
                with act.Fori(0, tiles) as t:
                    attention_act(act, t, act.snap(t + 1), P)
                attention_act(act, tiles, tiles + 1, DEC)

            @block.vector
            def _(dve):
                with dve.Fori(0, tiles) as t:
                    attention_dve(dve, t, dve.snap(t + 1), P)
                attention_dve(dve, tiles, tiles + 1, DEC)

            @block.tensor
            def _(pe):
                with pe.Fori(0, tiles) as t:
                    attention_pe(pe, t, pe.snap(t + 1), P, 0)
                attention_pe(pe, tiles, tiles + 1, DEC, 1)

        S.end_stage()

        l_sp, l_pe, l_leave = linear([("add", I["wo_x"][0], 0, 4, B3, H)])
        n_act, n_pe, n_dve = norm_stage("ffn", whole(H), whole(XN), lambda f: col("norm_ffn_g", f), N, sq_b)
        eroom = Room(scr[:, :], SCR)
        NR = GROUPS + EXPERTS
        w_route = eroom.take(FT, NR)
        b_route = eroom.take(NR)
        lg = eroom.take(TT, NR)
        gmax, gsum, m1, m2, e2, wsum, w1, w2 = (eroom.take(TT) for _ in range(8))
        ge, oh_g, seen_g, one_g = (eroom.take(TT, GROUPS) for _ in range(4))
        le4 = eroom.take(TT * GROUPS, PER_GROUP)
        lec, o1, o2, seen = (eroom.take(TT, PER_GROUP) for _ in range(4))
        one_e = eroom.take(TT, PER_GROUP)
        w_tok = eroom.take(TT * GROUPS, PER_GROUP)
        wT = eroom.take(N)
        exp_l = lg[:, :, GROUPS:NR]

        def wide(v, n):
            return v.unsqueeze(2).to_broadcast([P, v.shape[1], n])

        def first_of(dve, name, eq, scan_mask, seen_):
            dve.wait_ge(S[name + "_eq"], 1)
            dve.tensor_tensor_scan(flat2(seen_), flat2(scan_mask), flat2(eq), 0.0, ALU.mult, ALU.add).then_inc(S[name + "_seen"], 1)
            dve.wait_ge(S[name + "_seen"], 1)
            dve.scalar_tensor_tensor(out=eq, in0=seen_, scalar=1.0, in1=eq, op0=ALU.is_equal, op1=ALU.mult).then_inc(S[name], 1)
            dve.wait_ge(S[name], 1)

        with nc.Block() as block:
            @block.sync
            def _(sp):
                sp.dma_start(w_route[:, :, 0:GROUPS], I["router_group_w"][0].rearrange("(k p) n -> p k n", p=P)).then_inc(S["route_in"], 16)
                sp.dma_start(w_route[:, :, GROUPS:NR], I["router_expert_w"][0].rearrange("(k p) n -> p k n", p=P)).then_inc(S["route_in"], 16)
                sp.dma_start(b_route[0:1, 0:GROUPS], I["router_group_b"]).then_inc(S["route_in"], 16)
                sp.dma_start(b_route[0:1, GROUPS:NR], I["router_expert_b"].rearrange("a g e -> a (g e)")).then_inc(S["route_in"], 16)
                l_sp(sp)

            @block.scalar
            def _(act):
                act.wait_ge(S["banks0_free"], used[0] + 1)
                act.wait_ge(S["banks1_free"], used[0] + 1)
                n_act(act)
                act.wait_ge(S["g_shifted"], 1)
                act.activation(ge, ge, ACT.Exp).then_inc(S["g_exp"], 1)
                act.wait_ge(S["e_shifted"], 1)
                act.activation(e2, e2, ACT.Exp).then_inc(S["e_exp"], 1)

            @block.gpsimd
            def _(pool):
                pool.memset(one_g, 1.0).then_inc(S["scan_ones"], 1)
                pool.memset(one_e, 1.0).then_inc(S["scan_ones"], 1)
                pool.memset(lg, 0.0).then_inc(S["lg_zero"], 1)
                pool.wait_ge(S["scan_ones"], 2)
                pool.memset(one_g[:, :, 0:1], 0.0).then_inc(S["scan_masks"], 1)
                pool.memset(one_e[:, :, 0:1], 0.0).then_inc(S["scan_masks"], 1)

            @block.tensor
            def _(pe):
                l_pe(pe)
                n_pe(pe)
                pe.wait_ge(S["ffn_normed"], FT)
                pe.wait_ge(S["route_in"], 64)
                for t in range(TT):
                    m = P if t < TT - 1 else DEC
                    out = bank[2][0:m, t * NR:(t + 1) * NR]
                    for k in range(FT):
                        pe.matmul(out, arena[:, XN + k, 1 + t * P:1 + t * P + m], w_route[:, k, :], start=(k == 0), stop=False)
                    mm = pe.matmul(out, ones[0:1, 0:m], b_route[0:1, :], start=False, stop=True)
                mm.then_inc(S["logits"], 1)
                pe.wait_ge(S["w_tok"], 1)
                for t in range(TT):
                    m = P if t < TT - 1 else DEC
                    mm = pe.transpose(ps[0:EXPERTS, 3 + t // 4, (t % 4) * P:(t % 4) * P + m],
                                      flat2(w_tok)[0:m, t * EXPERTS:(t + 1) * EXPERTS], ident[0:m, 0:m])
                mm.then_inc(S["w_turned"], 1)

            @block.vector
            def _(dve):
                l_leave(dve, True)
                n_dve(dve)
                dve.wait_ge(S["logits"], 1)
                dve.wait_ge(S["lg_zero"], 1)
                dve.tensor_copy(lg[:, 0:TT - 1, :], bank[2][:, 0:(TT - 1) * NR].rearrange("p (t n) -> p t n", t=TT - 1)).then_inc(S["lg"], 1)
                dve.tensor_copy(lg[0:DEC, TT - 1, :], bank[2][0:DEC, (TT - 1) * NR:TT * NR]).then_inc(S["lg"], 1)
                dve.wait_ge(S["lg"], 2)
                dve.tensor_reduce(gmax, lg[:, :, 0:GROUPS], AX_X, ALU.max).then_inc(S["gmax"], 1)
                dve.wait_ge(S["gmax"], 1)
                dve.tensor_tensor(ge, lg[:, :, 0:GROUPS], wide(gmax, GROUPS), ALU.subtract).then_inc(S["g_shifted"], 1)
                dve.tensor_tensor(oh_g, lg[:, :, 0:GROUPS], wide(gmax, GROUPS), ALU.is_equal).then_inc(S["group_eq"], 1)
                dve.wait_ge(S["scan_masks"], 2)
                first_of(dve, "group", oh_g, one_g, seen_g)
                dve.wait_ge(S["g_exp"], 1)
                dve.tensor_reduce(gsum, ge, AX_X, ALU.add).then_inc(S["gsum"], 1)
                oh_ge = flat2(oh_g).unsqueeze(2).to_broadcast([P, TT * GROUPS, PER_GROUP])
                dve.tensor_tensor(le4.rearrange("p (t g) e -> p t g e", t=TT), exp_l.rearrange("p t (g e) -> p t g e", g=GROUPS),
                                  oh_ge.rearrange("p (t g) e -> p t g e", t=TT), ALU.mult).then_inc(S["le4"], 1)
                dve.wait_ge(S["le4"], 1)
                dve.tensor_reduce(lec, le4.rearrange("p (t g) e -> p t e g", t=TT), AX_X, ALU.add).then_inc(S["lec"], 1)
                dve.wait_ge(S["lec"], 1)
                dve.tensor_reduce(m1, lec, AX_X, ALU.max).then_inc(S["m1"], 1)
                dve.wait_ge(S["m1"], 1)
                dve.tensor_tensor(o1, lec, wide(m1, PER_GROUP), ALU.is_equal).then_inc(S["top1_eq"], 1)
                first_of(dve, "top1", o1, one_e, seen)
                dve.scalar_tensor_tensor(out=lec, in0=o1, scalar=-1e30, in1=lec, op0=ALU.mult, op1=ALU.add).then_inc(S["lec2"], 1)
                dve.wait_ge(S["lec2"], 1)
                dve.tensor_reduce(m2, lec, AX_X, ALU.max).then_inc(S["m2"], 1)
                dve.wait_ge(S["m2"], 1)
                dve.tensor_tensor(e2, m2, m1, ALU.subtract).then_inc(S["e_shifted"], 1)
                dve.tensor_tensor(o2, lec, wide(m2, PER_GROUP), ALU.is_equal).then_inc(S["top2_eq"], 1)
                first_of(dve, "top2", o2, one_e, seen)
                dve.wait_ge(S["e_exp"], 1)
                dve.wait_ge(S["gsum"], 1)
                dve.scalar_tensor_tensor(out=wsum, in0=e2, scalar=1.0, in1=gsum, op0=ALU.add, op1=ALU.mult).then_inc(S["wsum"], 1)
                dve.wait_ge(S["wsum"], 1)
                dve.reciprocal(w1, wsum).then_inc(S["w1"], 1)
                dve.wait_ge(S["w1"], 1)
                dve.tensor_tensor(w2, w1, e2, ALU.mult).then_inc(S["w2"], 1)
                dve.tensor_tensor(o1, o1, wide(w1, PER_GROUP), ALU.mult).then_inc(S["o1w"], 1)
                dve.wait_ge(S["w2"], 1)
                dve.tensor_tensor(o2, o2, wide(w2, PER_GROUP), ALU.mult).then_inc(S["o2w"], 1)
                dve.wait_ge(S["o1w"], 1)
                dve.wait_ge(S["o2w"], 1)
                dve.tensor_tensor(o1, o1, o2, ALU.add).then_inc(S["w_e"], 1)
                dve.wait_ge(S["w_e"], 1)
                dve.tensor_tensor(w_tok.rearrange("p (t g) e -> p t g e", t=TT), oh_ge.rearrange("p (t g) e -> p t g e", t=TT),
                                  o1.unsqueeze(2).to_broadcast([P, TT, GROUPS, PER_GROUP]), ALU.mult).then_inc(S["w_tok"], 1)
                dve.wait_ge(S["w_turned"], 1)
                dve.tensor_copy(wT[0:EXPERTS, 0:SEQ], ps[0:EXPERTS, 3, :]).then_inc(S["wT"], 1)
                dve.tensor_copy(wT[0:EXPERTS, SEQ:N], ps[0:EXPERTS, 4, 0:DEC]).then_inc(S["wT"], 1)

        S.end_stage()

        wroom = Room(flat[:, B2 * BW:7 * FT * BW], 5 * FT * BW)
        wg, wu, wd = [], [], []
        for s in range(2):
            wg.append(wroom.take(FT, DE))
            wu.append(wroom.take(FT, DE))
            wd.append(wroom.take(2, D))
        hid = [eroom.take(2, HALF) for _ in range(2)]
        gate_s = eroom.take(2, HALF)
        sel = [eroom.take(P) for _ in range(2)]
        ITER = EXPERTS // 2

        def gate_up(pe, i, k):
            i, k = (i + 1, 0) if k == 4 else (i, k)
            s, h = k // 2, k % 2
            if h == 0:
                pe.wait_ge(S[f"e_w{s}_in"], i * 48 + 48)
                pe.wait_ge(S[f"e_sel{s}"], i + 1)
            pe.wait_ge(S["e_hid"], i * 4 + (k + 1))
            for o in range(2):
                for w, b in ((wg[s], o), (wu[s], 2 + o)):
                    for f in range(FT):
                        pe.matmul(bank[b][:, 0:HALF], w[:, f, o * P:(o + 1) * P], arena[:, XN + f, 1 + h * HALF:1 + (h + 1) * HALF],
                                  start=(f == 0), stop=(f == FT - 1))
            pe.matmul(bank[5][:, 0:HALF], sel[s][0:EXPERTS, :], wT[0:EXPERTS, h * HALF:(h + 1) * HALF],
                      start=True, stop=True).then_inc(S["e_gate_up"], 1)

        def down(pe, i, k):
            s = k // 2
            pe.wait_ge(S["e_hid"], i * 4 + (k + 2))
            for d in range(FT):
                pe.wait_ge(S["e_added"], i * (4 * FT) + (k * FT + d + 1))
                for f in range(2):
                    mm = pe.matmul(bank[6 + d % 2][:, 0:HALF], wd[s][:, f, d * P:(d + 1) * P], hid[k % 2][:, f, :],
                                   start=(f == 0), stop=(f == 1))
                mm.then_inc(S["e_down"], 1)
            if k % 2:
                pe.wait_ge(S["e_down"], i * (4 * FT) + (k + 1) * FT)
                pe.sem_inc(S[f"e_slot{s}_free"], 1)

        def silu(act, i, k):
            act.wait_ge(S["e_gate_up"], i * 4 + (k + 1))
            act.activation(gate_s, ps[:, 0:2, 0:HALF], ACT.Silu).then_inc(S["e_silu"], 1)

        def hidden(dve, i, k):
            dve.wait_ge(S["e_silu"], i * 4 + (k + 1))
            dve.tensor_tensor(hid[k % 2], gate_s, ps[:, 2:4, 0:HALF], ALU.mult).then_inc(S["e_product"], 1)
            dve.wait_ge(S["e_product"], i * 4 + (k + 1))
            dve.tensor_tensor(hid[k % 2], hid[k % 2], bank[5][:, 0:HALF].unsqueeze(1).to_broadcast([P, 2, HALF]), ALU.mult).then_inc(S["e_hid"], 1)

        def add_down(dve, i, k):
            h = k % 2
            for d in range(FT):
                to = arena[:, H + d, 1 + h * HALF:1 + (h + 1) * HALF]
                dve.wait_ge(S["e_down"], i * (4 * FT) + (k * FT + d + 1))
                dve.tensor_tensor(to, to, bank[6 + d % 2][:, 0:HALF], ALU.add).then_inc(S["e_added"], 1)

        with nc.Block() as block:
            @block.sync
            def _(sp):
                with sp.Fori(0, ITER) as i:
                    for s in range(2):
                        sp.wait_ge(S[f"e_slot{s}_free"], i + 1)
                        for dst, w in ((wg[s], I["expert_w_gate"]), (wu[s], I["expert_w_up"]), (wd[s], I["expert_w_down"])):
                            src = w[0][bass.ds(i * 2 + s, 1)].rearrange("e (k p) n -> p (e k) n", p=P)
                            sp.dma_start(dst, src).then_inc(S[f"e_w{s}_in"], 16)

            @block.gpsimd
            def _(pool):
                with pool.Fori(0, ITER) as i:
                    for s in range(2):
                        pool.wait_ge(S[f"e_slot{s}_free"], i + 1)
                        pool.tensor_copy(sel[s][0:EXPERTS, :], ident[0:EXPERTS, bass.ds(i * 2 + s, 1)].to_broadcast([EXPERTS, P])).then_inc(S[f"e_sel{s}"], 1)

            @block.scalar
            def _(act):
                silu(act, 0, 0)
                with act.Fori(0, ITER - 1) as i:
                    for k in range(4):
                        silu(act, i, k + 1)
                for k in range(3):
                    silu(act, ITER - 1, k + 1)

            @block.tensor
            def _(pe):
                for name, n in (("e_slot0_free", 1), ("e_slot1_free", 1), ("e_hid", 1), ("e_added", 2)):
                    pe.sem_inc(S[name], n)
                gate_up(pe, 0, 0)
                with pe.Fori(0, ITER - 1) as i:
                    for k in range(4):
                        gate_up(pe, i, k + 1)
                        down(pe, i, k)
                for k in range(4):
                    if k < 3:
                        gate_up(pe, ITER - 1, k + 1)
                    down(pe, ITER - 1, k)

            @block.vector
            def _(dve):
                hidden(dve, 0, 0)
                with dve.Fori(0, ITER - 1) as i:
                    for k in range(4):
                        if k < 3:
                            hidden(dve, i, k + 1)
                        else:
                            hidden(dve, i + 1, 0)
                        add_down(dve, i, k)
                for k in range(4):
                    if k < 3:
                        hidden(dve, ITER - 1, k + 1)
                    add_down(dve, ITER - 1, k)

        S.end_stage()

        y_tok = shaped(flat, B2 * BW, (TT, D))
        n_act, n_pe, n_dve = norm_stage("final", whole(H), whole(XN), lambda f: col("norm_final_g", f), N, sq_all)

        with nc.Block() as block:
            @block.scalar
            def _(act):
                n_act(act)
                for j in range(2 * TT):
                    if j % 2:
                        m = P if j // 2 < TT - 1 else DEC
                        act.wait_ge(S["y_turned"], j + 1)
                        act.copy(y_tok[0:m, j // 2, 512:1024], ps[0:m, j % 8, :]).then_inc(S["y_odd"], 1)

            @block.tensor
            def _(pe):
                n_pe(pe)
                pe.wait_ge(S["final_normed"], FT)
                pe.wait_ge(S["final_rms"], 2)
                for j in range(2 * TT):
                    m = P if j // 2 < TT - 1 else DEC
                    if j >= 8:
                        pe.wait_ge(S["y_odd" if j % 2 else "y_even"], (j - 8) // 2 + 1)
                    for f in range(4):
                        mm = pe.transpose(ps[0:m, j % 8, f * P:(f + 1) * P], arena[:, XN + (j % 2) * 4 + f, 1 + (j // 2) * P:1 + (j // 2) * P + m], ident[:, :])
                    mm.then_inc(S["y_turned"], 1)

            @block.vector
            def _(dve):
                n_dve(dve)
                for j in range(0, 2 * TT, 2):
                    m = P if j // 2 < TT - 1 else DEC
                    dve.wait_ge(S["y_turned"], j + 1)
                    dve.tensor_copy(y_tok[0:m, j // 2, 0:512], ps[0:m, j % 8, :]).then_inc(S["y_even"], 1)

            @block.sync
            def _(sp):
                for t in range(TT):
                    sp.wait_ge(S["y_even"], t + 1)
                    sp.wait_ge(S["y_odd"], t + 1)
                    if t < TT - 1:
                        sp.dma_start(O["y_prompt"][0, t * P:(t + 1) * P, :], y_tok[:, t, :]).then_inc(S["y_out"], 16)
                    else:
                        sp.dma_start(O["y_sample"][0], y_tok[0:DEC, t, :]).then_inc(S["y_out"], 16)
                sp.wait_ge(S["y_out"], 16 * TT)


_INS = ["x_prompt", "x_sample", "mem_prompt", "cache_mem_k", "cache_mem_v", "state_hgrn", "state_rwkv", "state_rwkv_shift",
        "norm_mix_g", "w_in", "hgrn_lower_bounds", "hgrn_norm_g", "rwkv_mu", "rwkv_w0", "rwkv_w2", "rwkv_a0", "rwkv_a2",
        "rwkv_g2", "rwkv_k_k", "rwkv_k_a", "rwkv_r_k", "rwkv_ln_g", "rwkv_ln_b", "w_out", "norm_x_g", "norm_mem_g",
        "wq_x", "wk_x", "wv_x", "wo_x", "norm_ffn_g", "router_group_w", "router_group_b", "router_expert_w",
        "router_expert_b", "expert_w_gate", "expert_w_up", "expert_w_down", "norm_final_g"]
_OUTS = [("y_prompt", (1, SEQ, D)), ("y_sample", (1, DEC, D)),
         ("mem_k", (1, 1, MEM, XH, D // XH)), ("mem_v", (1, 1, MEM, XH, D // XH)),
         ("hgrn_prompt", (1, 1, HEADS, P, P)), ("hgrn_sample", (1, 1, HEADS, P, P)),
         ("rwkv_prompt", (1, 1, 16, 64, 64)), ("rwkv_sample", (1, 1, 16, 64, 64)),
         ("shift_prompt", (1, 1, 1, N_RWKV)), ("shift_sample", (1, 1, 1, N_RWKV))]


def kernel(**inputs):
    import numpy as _np
    import concourse.bacc as _bacc
    from concourse.bass_utils import run_bass_kernel_spmd as _run

    nc = _bacc.Bacc("TRN2", target_bir_lowering=False, num_devices=1)
    arrays, ins, outs = {}, {}, {}
    for name in _INS:
        a = _np.ascontiguousarray(inputs[name])
        arrays[f"in_{name}"] = a
        ins[name] = nc.dram_tensor(f"in_{name}", a.shape, F32, kind="ExternalInput").ap()
    for name, shape in _OUTS:
        outs[name] = nc.dram_tensor(f"out_{name}", shape, F32, kind="ExternalOutput").ap()
    build(nc, ins, outs)
    r = _run(nc, [arrays], core_ids=[0])
    return tuple(r.results[0][f"out_{name}"] for name, _ in _OUTS)
```

```python
from contextlib import ExitStack

import concourse.bass as bass
from concourse import mybir

F32 = mybir.dt.float32
ALU = mybir.AluOpType
ACT = mybir.ActivationFunctionType
AX_X = mybir.AxisListType.X

P = 128
D = 1024
FT = D // P
SEQ = 512
DEC = 32
N = SEQ + DEC
HALF = N // 2
CH = 64
NCH = SEQ // CH
BW = 1 + (NCH + 1) * CH + 1
HEADS = 8
DECAY_L, ICL_L, GATE_L = 64, 64, 160
LORA = DECAY_L + ICL_L + GATE_L
N_RWKV = 3 * D + LORA
COL_RWKV = 4 * D
COL_GATES = COL_RWKV + N_RWKV
MEM = 256
XH = 4
XSCALE = (D // XH) ** -0.5
GROUPS, PER_GROUP = 4, 8
EXPERTS = GROUPS * PER_GROUP
DE = 256
EPS = 1e-6
GN_EPS = 64e-5
UNIT = 256
TT = 5
BLK = 96
TOP_K = 2
NBLK = -(-((TOP_K * N - EXPERTS) // BLK + EXPERTS) // 2) * 2
NSLOT = NBLK * BLK
MAXB = -(-N // BLK)
U32 = mybir.dt.uint32
I32 = mybir.dt.int32
DECAY = 0.6065306597126334
LN2 = 0.6931471805599453

H, XN, B2, B3, B4, B5, B6 = (FT * i for i in range(7))


class Sems:

    def __init__(self, nc):
        self.nc, self.by_name, self.kept = nc, {}, {}

    def __getitem__(self, name):
        where = self.kept if name.startswith(("slot", "banks")) else self.by_name
        if name not in where:
            where[name] = self.nc.alloc_semaphore(name)
        return where[name]

    def end_stage(self):
        self.nc.clear_and_free_semaphores(list(self.by_name.values()))
        self.nc.all_engine_barrier()
        self.by_name = {}


def shaped(flat, base, shape):
    n = 1
    for s in shape:
        n *= s
    v = flat[:, base:base + n]
    if len(shape) == 2:
        v = v.rearrange("p (a b) -> p a b", a=shape[0])
    if len(shape) == 3:
        v = v.rearrange("p (a b c) -> p a b c", a=shape[0], b=shape[1])
    return v


class Room:

    def __init__(self, flat, n):
        self.flat, self.n, self.at = flat, n, 0

    def take(self, *shape):
        v = shaped(self.flat, self.at, shape)
        n = 1
        for s in shape:
            n *= s
        self.at += n
        assert self.at <= self.n, (self.at, self.n)
        return v


SCR = 12800


def build(nc, I, O):
    with ExitStack() as ctx:
        def sb(name, shape):
            return ctx.enter_context(nc.sbuf_tensor(name, shape, F32))

        S = Sems(nc)
        x_slots = nc.dram_tensor("x_slots", (NSLOT, D), F32, kind="Internal").ap()
        y_slots = nc.dram_tensor("y_slots", (NSLOT, D), F32, kind="Internal").ap()
        h_kept = nc.dram_tensor("h_kept", (P, FT * BW), F32, kind="Internal").ap()
        arena = sb("arena", [P, 7 * FT, BW])
        flat = arena[:, :, :].rearrange("p f n -> p (f n)")
        ring = sb("ring", [P, 2, FT, UNIT])
        ring_flat = ring[:, :, :, :].rearrange("p s k n -> p (s k n)")
        lora = sb("lora", [P, 3, BW])
        ident = sb("ident", [P, P])
        ones = sb("ones", [P, P])
        head_ones = sb("head_ones", [P, P])
        rows_a = sb("rows_a", [P, P])
        rows_b = sb("rows_b", [P, P])
        ca = sb("ca", [P, P])
        cb = sb("cb", [P, P])
        lbs = sb("lbs", [P, 2, FT])
        tiny = sb("tiny", [P, 4])
        scale_row = sb("scale_row", [P, BW])
        scr = sb("scr", [P, SCR])
        ps = ctx.enter_context(nc.psum_tensor("ps", [P, 8, 512], F32))
        bank = [ps[:, b, :] for b in range(8)]
        eps_c, gn_eps_c, kk_c = tiny[:, 0:1], tiny[:, 1:2], tiny[:, 2:3]

        VEC = ["norm_mix_g", "rwkv_w0", "rwkv_a0", "rwkv_k_k", "rwkv_k_a", "rwkv_r_k", "rwkv_ln_g", "rwkv_ln_b",
               "norm_x_g", "norm_mem_g", "norm_ffn_g", "norm_final_g", "lb0", "lb1"]
        NV = len(VEC) * FT

        def col(name, f=None):
            k = VEC.index(name) * FT
            return ca[:, k:k + FT] if f is None else ca[:, k + f:k + f + 1]

        MU, HG, SHIFT, NSH = 0, 27, 28, 27

        def frames(base, a, n, f0=0, f1=FT):
            return arena[:, base + f0:base + f1, bass.ds(a + 1, n)]

        def whole(base):
            return arena[:, base:base + FT, 1:1 + N]

        def over(c, n):
            return c.unsqueeze(2).to_broadcast([P, c.shape[1], n])

        def split_heads(b):
            return b.rearrange("p (a n) -> p a n", a=8)

        def norm_stage(k, src, dst, gain, n, sq):
            parts = [(0, n)] if n <= 512 else [(0, n // 2), (n // 2, n)]
            rs = scale_row[:, 0:n]

            def on_act(act):
                act.activation(sq, src, ACT.Square).then_inc(S[k + "_squares"], 1)
                act.wait_ge(S[k + "_sums"], 1)
                for h, (a, b) in enumerate(parts):
                    act.activation(rs[:, a:b], ps[:, h, 0:b - a], ACT.Sqrt, bias=eps_c, scale=1.0 / D).then_inc(S[k + "_rms"], 1)

            def on_pe(pe):
                pe.wait_ge(S[k + "_squares"], 1)
                for h, (a, b) in enumerate(parts):
                    for f in range(FT):
                        mm = pe.matmul(ps[:, h, 0:b - a], ones[:, :], sq[:, f, a:b], start=(f == 0), stop=(f == FT - 1))
                mm.then_inc(S[k + "_sums"], 1)

            def on_dve(dve):
                dve.wait_ge(S[k + "_rms"], len(parts))
                dve.reciprocal(rs, rs).then_inc(S[k + "_rrms"], 1)
                dve.wait_ge(S[k + "_rrms"], 1)
                for f in range(FT):
                    dve.scalar_tensor_tensor(out=dst[:, f, :], in0=src[:, f, :], scalar=gain(f), in1=rs,
                                             op0=ALU.mult, op1=ALU.mult).then_inc(S[k + "_normed"], 1)

            return on_act, on_pe, on_dve

        used = [0]

        def linear(jobs):
            spans = []
            for job in jobs:
                spans.append((used[0], job))
                used[0] += job[3] // 2

            def on_sp(sp):
                for b0, (kind, w, c0, units, x, dst) in spans:
                    wv = w.rearrange("(k p) n -> p k n", p=P)
                    with sp.Fori(0, units // 2) as i:
                        n = sp.snap(i + (b0 + 1))
                        for s in range(2):
                            sp.wait_ge(S[f"slot{s}_free"], n)
                            sp.dma_start(ring[:, s], wv[:, :, bass.ds(i * (2 * UNIT) + (c0 + s * UNIT), UNIT)]).then_inc(S[f"slot{s}_loaded"], 16)

            def on_pe(pe):
                for b0, (kind, w, c0, units, x, dst) in spans:
                    with pe.Fori(0, units // 2) as i:
                        n = pe.snap(i + (b0 + 1))
                        n16 = pe.snap(i * 16 + (b0 + 1) * 16)
                        for s in range(2):
                            pe.wait_ge(S[f"banks{s}_free"], n)
                            pe.wait_ge(S[f"slot{s}_loaded"], n16)
                            if kind == "rows":
                                for h in range(MEM // P):
                                    for k in range(FT):
                                        mm = pe.matmul(ps[:, 4 * s + h, 0:UNIT], x[:, k, h * P:(h + 1) * P], ring[:, s, k, :],
                                                       start=(k == 0), stop=(k == FT - 1))
                            else:
                                for o in range(UNIT // P):
                                    for h in range(2):
                                        for k in range(FT):
                                            mm = pe.matmul(ps[:, 4 * s + 2 * o + h, 0:HALF], ring[:, s, k, o * P:(o + 1) * P],
                                                           arena[:, x + k, 1 + h * HALF:1 + (h + 1) * HALF],
                                                           start=(k == 0), stop=(k == FT - 1))
                            mm.then_inc(S[f"slot{s}_free"], 1)

            def leave(eng, on_dve):
                for b0, (kind, w, c0, units, x, dst) in spans:
                    if (kind == "add") != on_dve:
                        continue
                    with eng.Fori(0, units // 2) as i:
                        n = eng.snap(i + (b0 + 2))
                        for s in range(2):
                            eng.wait_ge(S[f"slot{s}_free"], n)
                            if kind == "rows":
                                last = eng.copy(dst[:, :, bass.ds(i * (2 * UNIT) + s * UNIT, UNIT)], ps[:, 4 * s:4 * s + 2, 0:UNIT])
                            else:
                                for o in range(UNIT // P):
                                    src = ps[:, 4 * s + 2 * o:4 * s + 2 * o + 2, 0:HALF]
                                    to = arena[:, bass.ds(i * 4 + (dst + 2 * s + o), 1), 1:1 + N].rearrange("p o (h n) -> p (o h) n", h=2)
                                    if kind == "keep":
                                        last = eng.copy(to, src)
                                    else:
                                        last = eng.tensor_tensor(to, to, src, ALU.add)
                            last.then_inc(S[f"banks{s}_free"], 1)

            return on_sp, on_pe, leave

        x_tok = shaped(flat, B2 * BW, (TT, D))
        x_groups = []
        for t in range(TT):
            n = P if t < TT - 1 else DEC
            for f0 in (0, 4):
                x_groups.append((x_tok[0:n, t, :], n, f0, arena[:, H + f0:H + f0 + 4, 1 + t * P:1 + t * P + n]))

        with nc.Block() as block:
            @block.sync
            def _(sp):
                sp.dma_start(x_tok[:, 0:4, :], I["x_prompt"][0].rearrange("(t p) d -> p t d", p=P)).then_inc(S["x_in"], 16)
                sp.dma_start(x_tok[0:DEC, 4, :], I["x_sample"][0]).then_inc(S["x_in"], 16)

            @block.scalar
            def _(act):
                for s in range(2):
                    act.sem_inc(S[f"banks{s}_free"], 1)
                for v, name in enumerate(VEC):
                    if name == "rwkv_r_k":
                        src = I[name][0].rearrange("(f a) b -> f (a b)", f=FT)
                    elif name == "norm_final_g":
                        src = I[name].rearrange("(f p) -> f p", f=FT)
                    elif name in ("lb0", "lb1"):
                        src = I["hgrn_lower_bounds"][int(name[2])].rearrange("(f p) -> f p", f=FT)
                    else:
                        src = I[name][0].rearrange("(f p) -> f p", f=FT)
                    act.dma_start(rows_a[v * FT:(v + 1) * FT, :], src).then_inc(S["rows_a_in"], 16)
                act.wait_ge(S["rows_b_cleared"], 1)
                full = N_RWKV // P
                rest = N_RWKV - full * P
                for base, src in ((MU, I["rwkv_mu"][0]), (SHIFT, I["state_rwkv_shift"][0, 0, 0])):
                    act.dma_start(rows_b[base:base + full, :], src[0:full * P].rearrange("(f p) -> f p", p=P)).then_inc(S["rows_b_in"], 16)
                    act.dma_start(rows_b[base + full:base + full + 1, 0:rest], src[full * P:N_RWKV].unsqueeze(0)).then_inc(S["rows_b_in"], 16)
                act.dma_start(rows_b[HG:HG + 1, :], I["hgrn_norm_g"]).then_inc(S["rows_b_in"], 16)
                for i, (src, n, f0, dst) in enumerate(x_groups):
                    if i % 2:
                        act.wait_ge(S["x_turned"], i + 1)
                        act.copy(dst, ps[:, i % 8, :].rearrange("p (f n) -> p f n", f=4)[:, :, 0:n]).then_inc(S["x_kept_odd"], 1)

            @block.gpsimd
            def _(pool):
                pool.memset(rows_b[:, :], 0.0).then_inc(S["rows_b_cleared"], 1)
                pool.memset(ident[:, :], 0.0).then_inc(S["ident_zero"], 1)
                pool.memset(ones[:, :], 1.0).then_inc(S["consts"], 1)
                pool.memset(eps_c, EPS).then_inc(S["consts"], 1)
                pool.memset(gn_eps_c, GN_EPS).then_inc(S["consts"], 1)
                pool.memset(kk_c, 15.0 * LN2).then_inc(S["consts"], 1)
                pool.wait_ge(S["ident_zero"], 1)
                pool.affine_select(out=ident[:, :], in_=ident[:, :], compare_op=ALU.not_equal, fill=1.0, base=0,
                                   pattern=[[-1, P]], channel_multiplier=1).then_inc(S["ident_ready"], 1)

            @block.tensor
            def _(pe):
                for s in range(2):
                    pe.sem_inc(S[f"slot{s}_free"], 1)
                pe.wait_ge(S["ident_ready"], 1)
                pe.wait_ge(S["x_in"], 32)
                for i, (src, n, f0, dst) in enumerate(x_groups):
                    if i >= 8:
                        pe.wait_ge(S["x_kept_odd" if i % 2 else "x_kept_even"], (i - 8) // 2 + 1)
                    for f in range(4):
                        mm = pe.transpose(ps[:, i % 8, f * P:f * P + n], src[:, (f0 + f) * P:(f0 + f + 1) * P], ident[0:n, 0:n])
                    mm.then_inc(S["x_turned"], 1)
                pe.wait_ge(S["x_kept_odd"], 2)
                pe.wait_ge(S["rows_a_in"], 16 * len(VEC))
                pe.transpose(ps[:, 3, 0:NV], rows_a[0:NV, :], ident[0:NV, 0:NV]).then_inc(S["vectors_turned"], 1)
                pe.wait_ge(S["rows_b_in"], 80)
                pe.wait_ge(S["x_kept_even"], 3)
                pe.transpose(ps[:, 4, 0:P], rows_b[:, :], ident[:, :]).then_inc(S["vectors_turned"], 1)

            @block.vector
            def _(dve):
                dve.memset(arena[:, 0:B2, 1 + N:BW], 0.0).then_inc(S["pads"], 1)
                dve.memset(arena[:, 0:B2, 0:1], 0.0).then_inc(S["pads"], 1)
                dve.memset(lora[:, :, :], 0.0).then_inc(S["pads"], 1)
                dve.memset(head_ones[:, :], 0.0).then_inc(S["head_zero"], 1)
                dve.wait_ge(S["head_zero"], 1)
                dve.memset(head_ones[0:64, 0:64], 1.0).then_inc(S["consts"], 1)
                dve.memset(head_ones[64:128, 64:128], 1.0).then_inc(S["consts"], 1)
                for i, (src, n, f0, dst) in enumerate(x_groups):
                    if i % 2 == 0:
                        dve.wait_ge(S["x_turned"], i + 1)
                        dve.tensor_copy(dst, ps[:, i % 8, :].rearrange("p (f n) -> p f n", f=4)[:, :, 0:n]).then_inc(S["x_kept_even"], 1)
                dve.wait_ge(S["vectors_turned"], 1)
                dve.tensor_copy(ca[:, 0:NV], ps[:, 3, 0:NV]).then_inc(S["vectors"], 1)
                dve.wait_ge(S["vectors_turned"], 2)
                dve.tensor_copy(cb[:, :], ps[:, 4, 0:P]).then_inc(S["vectors"], 1)

        S.end_stage()

        w_in = I["w_in"][0]
        sq_all = shaped(scr[:, :], 0, (FT, N))
        n_act, n_pe, n_dve = norm_stage("mix", whole(H), whole(XN), lambda f: col("norm_mix_g", f), N, sq_all)
        l_sp, l_pe, l_leave = linear([("keep", w_in, 0, 16, XN, B2), ("keep", w_in, COL_GATES, 4, XN, B6)])
        lb, one_m_lb = lbs[:, 0, :], lbs[:, 1, :]
        zeros = lora[:, :, :].rearrange("p t n -> p (t n)")[:, 0:1536]

        with nc.Block() as block:
            @block.gpsimd
            def _(pool):
                pool.dma_start(h_kept, flat[:, H * BW:(H + FT) * BW]).then_inc(S["slots_zeroed"], 16)
                rows = NSLOT * D // P // 1536
                pool.dma_start(x_slots.rearrange("(p a) d -> p (a d)", p=P).rearrange("p (r c) -> p r c", r=rows),
                               zeros.unsqueeze(1).to_broadcast([P, rows, 1536])).then_inc(S["slots_zeroed"], 16)

            @block.sync
            def _(sp):
                l_sp(sp)

            @block.scalar
            def _(act):
                n_act(act)
                l_leave(act, False)
                act.wait_ge(S["lb_diff"], 1)
                act.activation(lb, lb, ACT.Sigmoid).then_inc(S["lb_ready"], 1)
                act.wait_ge(S["banks0_free"], used[0] + 1)
                act.wait_ge(S["banks1_free"], used[0] + 1)
                act.activation(whole(B3), whole(B3), ACT.Sigmoid).then_inc(S["f_sig"], 1)
                act.activation(whole(B6), whole(B6), ACT.Sigmoid).then_inc(S["ga_sig"], 1)
                act.activation(sq_all, whole(B2), ACT.Sigmoid).then_inc(S["q_sig"], 1)
                act.wait_ge(S["q_silu"], 1)
                act.activation(sq_all, whole(B5), ACT.Sigmoid).then_inc(S["g_sig"], 1)

            @block.tensor
            def _(pe):
                n_pe(pe)
                pe.wait_ge(S["mix_normed"], FT)
                pe.wait_ge(S["mix_rms"], 2)
                l_pe(pe)

            @block.vector
            def _(dve):
                n_dve(dve)
                dve.memset(arena[:, B2:B6 + FT, 1 + N:BW], 0.0).then_inc(S["pads2"], 1)
                dve.memset(arena[:, B2:B6 + FT, 0:1], 0.0).then_inc(S["pads2"], 1)
                dve.tensor_tensor(lb, col("lb0"), col("lb1"), ALU.subtract).then_inc(S["lb_diff"], 1)
                dve.wait_ge(S["lb_ready"], 1)
                dve.tensor_scalar(one_m_lb, lb, -1.0, 1.0, ALU.mult, ALU.add).then_inc(S["lb_ready"], 1)
                dve.wait_ge(S["lb_ready"], 2)
                dve.wait_ge(S["pads2"], 2)
                dve.wait_ge(S["f_sig"], 1)
                for f in range(FT):
                    t = arena[:, B3 + f, 1:1 + N]
                    dve.tensor_scalar(t, t, one_m_lb[:, f:f + 1], lb[:, f:f + 1], ALU.mult, ALU.add).then_inc(S["f_ready"], 1)
                dve.memset(arena[:, B3:B3 + FT, 1 + N:BW], 1.0).then_inc(S["f_ready"], 1)
                dve.wait_ge(S["q_sig"], 1)
                dve.tensor_tensor(whole(B2), whole(B2), sq_all, ALU.mult).then_inc(S["q_silu"], 1)
                dve.wait_ge(S["ga_sig"], 1)
                dve.tensor_tensor(whole(B6), whole(B6), whole(B5), ALU.mult).then_inc(S["gates"], 1)
                dve.wait_ge(S["g_sig"], 1)
                dve.wait_ge(S["gates"], 1)
                dve.scalar_tensor_tensor(out=whole(B5), in0=whole(B6), scalar=cb[:, HG:HG + 1], in1=sq_all, op0=ALU.mult, op1=ALU.mult).then_inc(S["gates"], 1)

        S.end_stage()

        room = Room(scr[:, :], SCR)
        g_s, k_s, b_s, eb, enb, q16, kinv, kh16, q32, kh32, v_s = (room.take(FT, CH) for _ in range(11))
        e32 = room.take(FT, 2)
        sc = room.take(2, 4, CH)
        k_tok, v_tok = room.take(4, P), room.take(4, P)
        state = room.take(HEADS, P)
        o_sq, o_rs, o_n = (room.take(2, 4, CH) for _ in range(3))
        h_out = ps[:, 6:8, 0:4 * CH].rearrange("p q (a t) -> p q a t", a=4)

        def by_parity(v):
            return v.rearrange("p (a q) t -> p q a t", q=2)

        h_mask = room.take(2, 4, CH)
        h_scan = room.take(FT * CH)

        def flat2(v):
            return v.rearrange("p a b -> p (a b)")

        def blocks(v):
            return flat2(v).rearrange("p (m e l) -> p m e l", e=2, l=16)

        def block_end(v):
            return blocks(v)[:, :, :, 15:16]

        def hgrn_act(act, c, n):
            act.wait_ge(S["h_chunk_done"], n)
            act.activation(g_s, frames(B3, c * CH, CH), ACT.Ln).then_inc(S["h_g"], 1)
            act.copy(v_s, frames(B4, c * CH, CH)).then_inc(S["h_v"], 1)
            act.wait_ge(S["h_b"], n)
            act.activation(eb, b_s, ACT.Exp).then_inc(S["h_eb"], 1)
            act.activation(enb, b_s, ACT.Exp, scale=-1.0).then_inc(S["h_enb"], 1)
            act.wait_ge(S["h_v_turned"], n)
            act.copy(v_tok, bank[2].rearrange("p (a b) -> p a b", a=4)).then_inc(S["h_v_tok"], 1)
            act.wait_ge(S["h_k_turned"], n)
            act.copy(k_tok, bank[1].rearrange("p (a b) -> p a b", a=4)).then_inc(S["h_k_tok"], 1)
            act.wait_ge(S["h_o"], n)
            act.activation(o_sq, h_out, ACT.Square).then_inc(S["h_o_sq"], 1)
            act.wait_ge(S["h_ms"], n)
            act.activation(o_rs, bank[3].rearrange("p (q a t) -> p q a t", q=2, a=4), ACT.Ln, bias=eps_c, scale=1.0 / P).then_inc(S["h_ln_ms"], 1)
            act.wait_ge(S["h_ln_ms"], n)
            act.activation(o_rs, o_rs, ACT.Exp, scale=-0.5).then_inc(S["h_rs"], 1)

        def hgrn_dve(dve, c, n):
            dve.wait_ge(S["h_chunk_done"], n)
            dve.tensor_scalar(k_s, frames(B3, c * CH, CH), -1.0, 1.0, ALU.mult, ALU.add).then_inc(S["h_k"], 1)
            dve.wait_ge(S["h_g"], n)
            dve.tensor_tensor_scan(flat2(b_s), h_scan, flat2(g_s), 0.0, ALU.mult, ALU.add).then_inc(S["h_b"], 1)
            dve.wait_ge(S["h_eb"], n)
            dve.tensor_tensor(q16, frames(B2, c * CH, CH), eb, ALU.mult).then_inc(S["h_q16"], 1)
            dve.tensor_tensor(flat2(e32).rearrange("p (m o) -> p m o", o=1), block_end(eb)[:, :, 0, :], block_end(eb)[:, :, 1, :], ALU.mult).then_inc(S["h_e32"], 1)
            dve.wait_ge(S["h_enb"], n)
            dve.wait_ge(S["h_k"], n)
            dve.tensor_tensor(kinv, k_s, enb, ALU.mult).then_inc(S["h_kinv"], 1)
            dve.wait_ge(S["h_kinv"], n)
            dve.tensor_tensor(blocks(kh16), blocks(kinv), block_end(eb).to_broadcast([P, 16, 2, 16]), ALU.mult).then_inc(S["h_kh16"], 1)
            dve.wait_ge(S["h_kh16"], n)
            dve.tensor_tensor(blocks(kh32)[:, :, 0, :], blocks(kh16)[:, :, 0, :], block_end(eb)[:, :, 1, :].to_broadcast([P, 16, 16]), ALU.mult)
            dve.tensor_copy(blocks(kh32)[:, :, 1, :], blocks(kh16)[:, :, 1, :]).then_inc(S["h_kh32"], 1)
            dve.wait_ge(S["h_q16"], n)
            dve.tensor_tensor(blocks(q32)[:, :, 1, :], blocks(q16)[:, :, 1, :], block_end(eb)[:, :, 0, :].to_broadcast([P, 16, 16]), ALU.mult)
            dve.tensor_copy(blocks(q32)[:, :, 0, :], blocks(q16)[:, :, 0, :]).then_inc(S["h_q32"], 1)
            dve.wait_ge(S["h_scores"], n)
            dve.tensor_tensor(sc, bank[0].rearrange("p (e a b) -> p e a b", e=2, a=4), h_mask, ALU.mult).then_inc(S["h_masked"], 1)
            dve.wait_ge(S["h_e32"], n)
            for m in range(2):
                dve.wait_ge(S[f"h_ds{m}"], n)
                for h in range(HEADS):
                    up = dve.scalar_tensor_tensor(out=state[:, h, :], in0=state[:, h, :], scalar=e32[:, h, m:m + 1],
                                                  in1=ps[:, 4 + h % 2, (h // 2) * P:(h // 2 + 1) * P], op0=ALU.mult, op1=ALU.add)
                up.then_inc(S[f"h_state{m}"], 1)
            dve.wait_ge(S["h_rs"], n)
            dve.tensor_tensor(o_n, h_out, o_rs, ALU.mult).then_inc(S["h_on"], 1)
            dve.wait_ge(S["h_on"], n)
            dve.wait_ge(S["h_state1"], n)
            gate = by_parity(frames(B5, c * CH, CH))
            dve.tensor_tensor(gate, o_n, gate, ALU.mult).then_inc(S["h_chunk_done"], 1)

        def hgrn_pe(pe, c, n):
            def half(h):
                return slice(64 * (h % 2), 64 * (h % 2) + 64)

            pe.wait_ge(S["h_chunk_done"], n)
            pe.wait_ge(S["h_v"], n)
            for h in range(HEADS):
                mm = pe.matmul(bank[2][half(h), (h // 2) * P:(h // 2 + 1) * P], v_s[:, h, :], ident[:, :], start=True, stop=True)
            mm.then_inc(S["h_v_turned"], 1)
            pe.wait_ge(S["h_kinv"], n)
            pe.wait_ge(S["h_q16"], n)
            for h in range(HEADS):
                pe.matmul(bank[0][half(h), (h // 2) * CH:(h // 2 + 1) * CH], kinv[:, h, :], q16[:, h, :], start=True, stop=True)
            pe.wait_ge(S["h_kh16"], n)
            for h in range(HEADS):
                mm = pe.matmul(bank[0][half(h), 256 + (h // 2) * CH:256 + (h // 2 + 1) * CH], kh16[:, h, :], q16[:, h, :], start=True, stop=True)
            mm.then_inc(S["h_scores"], 1)
            pe.wait_ge(S["h_kh32"], n)
            for h in range(HEADS):
                mm = pe.matmul(bank[1][half(h), (h // 2) * P:(h // 2 + 1) * P], kh32[:, h, :], ident[:, :], start=True, stop=True)
            mm.then_inc(S["h_k_turned"], 1)
            pe.wait_ge(S["h_q32"], n)
            pe.wait_ge(S["h_masked"], n)
            pe.wait_ge(S["h_v_tok"], n)
            for h in range(HEADS):
                for e in range(2):
                    pe.matmul(bank[6 + h % 2][:, (h // 2) * CH:(h // 2 + 1) * CH], v_tok[half(h), h // 2, :], sc[half(h), e, h // 2, :],
                              start=(h < 2 and e == 0), stop=False, skip_group_check=True)
            for m in range(2):
                if m:
                    pe.wait_ge(S["h_state0"], n)
                else:
                    pe.wait_ge(S["h_k_tok"], n)
                for h in range(HEADS):
                    at = (h // 2) * CH + 32 * m
                    mm = pe.matmul(bank[6 + h % 2][:, at:at + 32], state[:, h, :], q32[:, h, 32 * m:32 * m + 32],
                                   start=False, stop=(m == 1 and h >= HEADS - 2), skip_group_check=True)
                if m:
                    mm.then_inc(S["h_o"], 1)
                for h in range(HEADS):
                    part = slice(64 * (h % 2) + 32 * m, 64 * (h % 2) + 32 * m + 32)
                    mm = pe.matmul(ps[:, 4 + h % 2, (h // 2) * P:(h // 2 + 1) * P], k_tok[part, h // 2, :], v_tok[part, h // 2, :],
                                   start=True, stop=True)
                mm.then_inc(S[f"h_ds{m}"], 1)
            pe.wait_ge(S["h_o_sq"], n)
            pe.matmul(bank[3], ones[:, :], o_sq.rearrange("p q a t -> p (q a t)"), start=True, stop=True).then_inc(S["h_ms"], 1)

        with nc.Block() as block:
            @block.gpsimd
            def _(pool):
                pool.memset(h_mask[:, :, :, :], 1.0).then_inc(S["h_mask_ones"], 1)
                pool.memset(h_scan, 1.0).then_inc(S["h_scan_ones"], 1)
                pool.memset(state[:, :, :], 0.0).then_inc(S["h_state_zero"], 1)
                pool.wait_ge(S["h_scan_ones"], 1)
                pool.memset(h_scan.rearrange("p (m l) -> p m l", l=16)[:, :, 0:1], 0.0).then_inc(S["h_masks"], 1)
                pool.wait_ge(S["h_mask_ones"], 1)
                pool.wait_ge(S["h_masks"], 1)
                k = 0
                for q in range(2):
                    r = slice(64 * q, 64 * q + 64)
                    a = h_mask[r, 0, :, :].rearrange("p a (b l) -> p a b l", l=16)
                    z = h_mask[r, 1, :, :].rearrange("p a (b e l) -> p a b e l", e=2, l=16)
                    pool.memset(z[:, :, :, 0, :], 0.0).then_inc(S["h_mask_cut"], 1)
                    k += 1
                    pool.wait_ge(S["h_mask_cut"], k)
                    for view, pattern, base, mult in (
                            (a, [[0, 4], [16, 4], [1, 16]], 0, -1),
                            (a, [[0, 4], [-16, 4], [0, 16]], 0, 1),
                            (z[:, :, :, 1, :], [[0, 4], [-32, 2], [0, 16]], 0, 1),
                            (z[:, :, :, 1, :], [[0, 4], [32, 2], [0, 16]], 15, -1)):
                        k += 1
                        pool.affine_select(out=view, in_=view, compare_op=ALU.is_ge, fill=0.0, base=base,
                                           pattern=pattern, channel_multiplier=mult).then_inc(S["h_mask_cut"], 1)
                        pool.wait_ge(S["h_mask_cut"], k)
                pool.wait_ge(S["h_state_zero"], 1)
                pool.wait_ge(S["h_masks"], 1)
                pool.sem_inc(S["h_chunk_done"], 1)

            @block.sync
            def _(sp):
                heads = "h k v -> k h v"
                sp.wait_ge(S["h_chunk_done"], NCH + 1)
                sp.dma_start(O["hgrn_prompt"][0, 0].rearrange(heads, h=HEADS), state[:, :, :]).then_inc(S["h_state_out"], 16)
                sp.wait_ge(S["h_state_out"], 16)
                sp.dma_start(state[:, :, :], I["state_hgrn"][0, 0].rearrange(heads, h=HEADS)).then_inc(S["h_state_in"], 16)
                sp.wait_ge(S["h_chunk_done"], NCH + 2)
                sp.dma_start(O["hgrn_sample"][0, 0].rearrange(heads, h=HEADS), state[:, :, :]).then_inc(S["h_state_out"], 16)
                sp.wait_ge(S["h_state_out"], 32)
                sp.wait_ge(S["slots_zeroed"], 32)

            @block.scalar
            def _(act):
                with act.Fori(0, NCH) as c:
                    hgrn_act(act, c, act.snap(c + 1))
                hgrn_act(act, NCH, NCH + 1)

            @block.vector
            def _(dve):
                with dve.Fori(0, NCH) as c:
                    hgrn_dve(dve, c, dve.snap(c + 1))
                dve.wait_ge(S["h_state_in"], 16)
                hgrn_dve(dve, NCH, NCH + 1)

            @block.tensor
            def _(pe):
                with pe.Fori(0, NCH) as c:
                    hgrn_pe(pe, c, pe.snap(c + 1))
                pe.wait_ge(S["h_state_in"], 16)
                hgrn_pe(pe, NCH, NCH + 1)

        S.end_stage()

        l_sp, l_pe, l_leave = linear([("keep", w_in, COL_RWKV, 12, XN, B2), ("keep", w_in, COL_GATES + D, 4, XN, B6)])
        w_lora = shaped(scr[:, :], 0, (FT, LORA))
        lora_tiles = [(0, P), (P, P), (2 * P, LORA - 2 * P)]

        with nc.Block() as block:
            @block.sync
            def _(sp):
                sp.dma_start(w_lora, w_in.rearrange("(k p) n -> p k n", p=P)[:, :, COL_RWKV + 3 * D:COL_RWKV + N_RWKV]).then_inc(S["w_lora_in"], 16)
                l_sp(sp)

            @block.scalar
            def _(act):
                l_leave(act, False)
                act.wait_ge(S["lora_done"], 1)
                for t, (c0, m) in enumerate(lora_tiles):
                    act.copy(lora[0:m, t, 1:1 + N].rearrange("p (h n) -> p h n", h=2), ps[0:m, 2 * t:2 * t + 2, 0:HALF]).then_inc(S["lora_kept"], 1)
                act.activation(whole(B6), whole(B6), ACT.Sigmoid).then_inc(S["gb_sig"], 1)

            @block.tensor
            def _(pe):
                l_pe(pe)
                pe.wait_ge(S["w_lora_in"], 16)
                pe.wait_ge(S["banks0_free"], used[0] + 1)
                pe.wait_ge(S["banks1_free"], used[0] + 1)
                for t, (c0, m) in enumerate(lora_tiles):
                    for h in range(2):
                        for k in range(FT):
                            mm = pe.matmul(ps[0:m, 2 * t + h, 0:HALF], w_lora[:, k, c0:c0 + m],
                                           arena[:, XN + k, 1 + h * HALF:1 + (h + 1) * HALF], start=(k == 0), stop=(k == FT - 1))
                mm.then_inc(S["lora_done"], 1)

        S.end_stage()

        hroom = Room(flat[:, H * BW:(H + FT) * BW], FT * BW)
        xroom = Room(flat[:, XN * BW:(XN + FT) * BW], FT * BW)
        rroom = Room(ring_flat, 2 * FT * UNIT)
        room = Room(scr[:, :], SCR)
        wa2, g2a, g2b = room.take(D), room.take(D), room.take(D)
        d16low, d16up, offup, strictup, inclup, eye = (room.take(CH) for _ in range(6))
        r_scan = room.take(FT * CH)
        v_d, l_d, l_s, l_a = room.take(FT, CH), room.take(3, CH), room.take(3, CH), room.take(3, CH)
        sa = room.take(2, FT, CH)
        sg_s, a_s = sa[:, 0], sa[:, 1]
        rb_s = room.take(FT, CH)
        w_dec = room.take(FT, CH + 2)
        iw = room.take(FT, CH)
        bh, kh = room.take(FT, CH), room.take(FT, CH)
        r_s, k_s2, v_s2 = xroom.take(FT, CH), xroom.take(FT, CH), xroom.take(FT, CH)
        d_r, d_k = xroom.take(FT, CH), xroom.take(FT, CH)
        kk, kmod, bka, rn = (xroom.take(FT, CH) for _ in range(4))
        rk_s = v_d
        g_raw = hroom.take(FT, CH)
        ar = room.take(FT, 2, CH)
        bonus, gg = room.take(FT, CH), room.take(FT, CH)
        t1, a1, nt = room.take(FT, CH), room.take(FT, CH), room.take(FT, CH)
        st = room.take(FT, CH)
        b_tok, k_tok2, v_tok2 = (rroom.take(FT, CH) for _ in range(3))
        takT, trbT, trkT = (rroom.take(FT, CH) for _ in range(3))
        z_s, u_s = rroom.take(FT, CH), rroom.take(FT, CH)
        a2t2 = hroom.take(2, FT, CH)
        a4, t4, t8, qt, q_inv = (hroom.take(FT, CH) for _ in range(5))
        o_c = hroom.take(FT, CH)
        w_end = hroom.take(FT)
        ff, f2, y_s, mt = a2t2, a4, t4, t8
        o_q, o_r = bka, iw
        st_vk = z_s
        st_in = u_s
        w_prev, w_cur = w_dec[:, :, 0:CH], w_dec[:, :, 1:CH + 1]

        def pairs(m):
            return m.unsqueeze(1).to_broadcast([P, FT, CH])

        def q_half(q):
            return slice(64 * q, 64 * q + 64)

        def b_cols(b, a):
            return bank[b][:, a * CH:(a + 1) * CH]

        mu = cb[:, MU:MU + 27]

        def per_head(pe, b, lhsT, rhs, start=True, stop=True):
            for a in range(FT):
                for q in range(2):
                    r = q_half(q)
                    mm = pe.matmul(bank[b][r, a * CH:(a + 1) * CH], lhsT[r, a, :], rhs[r, a, :], start=start, stop=stop)
            return mm

        eye2 = [ident[q_half(q), q_half(q)] for q in range(2)]

        def turn_heads(pe, b, x):
            for a in range(FT):
                for q in range(2):
                    mm = pe.matmul(bank[b][q_half(q), a * CH:(a + 1) * CH], x[q_half(q), a, :], eye2[q], start=True, stop=True)
            return mm

        def counts(eng, c):
            if isinstance(c, int):
                return c + 1, c + 2
            return eng.snap(c + 1), eng.snap(c + 2)

        def frames_of_next(base, c, back=0):
            return frames(base, (c + 1) * CH - back, CH)

        def rwkv_pool(pool, c, cur, nxt):
            n, m = counts(pool, c)

            def const():
                pool.wait_ge(S["r_masks"], 1)

            if nxt:
                const()
                if cur:
                    pool.wait_ge(S["r_trk"], n)
                now, prev = lora[:, :, bass.ds((c + 1) * CH + 1, CH)], lora[:, :, bass.ds((c + 1) * CH, CH)]
                pool.tensor_tensor(l_d, prev, now, ALU.subtract).then_inc(S["r_ld"], 1)
                pool.wait_ge(S["r_ld"], m)
                pool.tensor_tensor(l_d, l_d, over(mu[:, 24:27], CH), ALU.mult).then_inc(S["r_lm"], 1)
                const()
                pool.wait_ge(S["r_lm"], m)
                pool.tensor_tensor(l_s, l_d, now, ALU.add).then_inc(S["r_l"], 1)
            if cur:
                const()
                pool.wait_ge(S["r_rks"], n)
                pool.wait_ge(S["r_chunk_done"], n)
                pool.tensor_tensor(bonus, rk_s, v_s2, ALU.mult).then_inc(S["r_bonus"], 1)
                const()
                pool.wait_ge(S["r_g"], n)
                pool.tensor_tensor(gg, g_raw, frames(B6, c * CH, CH), ALU.mult).then_inc(S["r_gg"], 1)
            if nxt:
                now, prev = frames_of_next(B4, c), frames_of_next(B4, c, 1)
                const()
                if cur:
                    pool.wait_ge(S["r_bonus"], n)
                    pool.wait_ge(S["r_v_turned"], n)
                pool.tensor_tensor(v_d, prev, now, ALU.subtract).then_inc(S["r_vd"], 1)
                pool.wait_ge(S["r_vd"], m)
                pool.tensor_tensor(v_d, v_d, over(mu[:, 16:24], CH), ALU.mult).then_inc(S["r_vm"], 1)
                const()
                pool.wait_ge(S["r_vm"], m)
                pool.tensor_tensor(v_s2, v_d, now, ALU.add).then_inc(S["r_v"], 1)
                pool.wait_ge(S["r_v"], m)
                pool.wait_ge(S["r_kmod"], m)
                pool.tensor_tensor(rk_s, r_s, kmod, ALU.mult).then_inc(S["r_rk0"], 1)
                pool.wait_ge(S["r_rk0"], m)
                pool.tensor_tensor(rk_s, rk_s, over(col("rwkv_r_k"), CH), ALU.mult).then_inc(S["r_rk"], 1)

        def rwkv_act(act, c, cur, nxt):
            n, m = counts(act, c)

            def keep_bank(cond, done, k, b, to, sem):
                if cond:
                    act.wait_ge(S[done], k)
                    act.copy(to, split_heads(bank[b])).then_inc(S[sem], 1)

            if cur:
                act.wait_ge(S["r_sq2"], n)
                act.copy(a2t2, ps[:, 5:7, :].rearrange("p e (a b) -> p e a b", a=8)).then_inc(S["r_a2t2"], 1)
            if nxt:
                act.wait_ge(S["r_l"], m)
                act.activation(l_a[0:64, 0, :], l_s[0:64, 0, :], ACT.Exp, scale=-2.0)
                act.activation(l_a[:, 1:3, :], l_s[:, 1:3, :], ACT.Exp, scale=-1.0).then_inc(S["r_la_exp"], 1)
                act.wait_ge(S["r_kk0"], m)
                act.activation(rn, kk, ACT.Square).then_inc(S["r_kk_sq"], 1)
            keep_bank(cur, "r_sq4", n, 6, t4, "r_t4")
            keep_bank(cur, "r_sq4", n, 5, a4, "r_a4")
            keep_bank(cur, "r_sq8", n, 5, t8, "r_t8")
            if nxt:
                act.wait_ge(S["r_ssm"], m)
                act.activation(rn, rn, ACT.Ln, scale=2.0 ** 30).then_inc(S["r_ln_ss"], 1)
                act.wait_ge(S["r_ln_ss"], m)
                act.activation(rn, rn, ACT.Exp, scale=-0.5, bias=kk_c).then_inc(S["r_rn"], 1)
            keep_bank(cur, "r_z_done", n, 0, z_s, "r_z")
            if nxt:
                act.wait_ge(S["r_pre"], m)
                act.activation(sa, sa, ACT.Exp, scale=-1.0).then_inc(S["r_sa_exp"], 1)
            keep_bank(cur, "r_q_turned", n, 5, q_inv, "r_q")
            if nxt:
                if cur:
                    act.wait_ge(S["r_gg"], n)
                act.wait_ge(S["r_glora"], m)
                act.copy(g_raw, split_heads(bank[2])).then_inc(S["r_g"], 1)
            if cur:
                act.wait_ge(S["r_f_done"], n)
                act.copy(ff, ps[:, 6:8, :].rearrange("p e (a b) -> p e a b", a=8)).then_inc(S["r_f"], 1)
            keep_bank(cur, "r_f2_done", n, 5, f2, "r_f2")
            if nxt:
                act.wait_ge(S["r_b"], m)
                act.activation(iw, rb_s, ACT.Exp, scale=DECAY).then_inc(S["r_iw"], 1)
                if cur:
                    act.wait_ge(S["r_wend"], n)
                act.activation(w_cur, rb_s, ACT.Exp, scale=-DECAY).then_inc(S["r_w"], 1)
            keep_bank(cur, "r_mt_done", n, 7, mt, "r_mt")
            keep_bank(cur, "r_u_done", n, 1, u_s, "r_u")
            keep_bank(cur, "r_o_done", n, 2, o_c, "r_o")
            keep_bank(nxt, "r_rk_ss", m, 7, rk_s, "r_rks")
            if cur:
                act.wait_ge(S["r_oc"], n)
                act.activation(o_q, o_c, ACT.Square).then_inc(S["r_o_sq"], 1)
            keep_bank(nxt, "r_b_turned", m, 6, b_tok, "r_b_tok")
            if cur:
                act.wait_ge(S["r_var"], n)
                act.activation(o_r, split_heads(bank[5]), ACT.Ln, scale=1.0 / 64, bias=gn_eps_c).then_inc(S["r_ln_var"], 1)
                act.wait_ge(S["r_ln_var"], n)
                act.activation(o_r, o_r, ACT.Exp, scale=-0.5).then_inc(S["r_rstd"], 1)
            keep_bank(nxt, "r_k_turned", m, 7, k_tok2, "r_k_tok")
            keep_bank(nxt, "r_v_turned", m, 5, v_tok2, "r_v_tok")

        def rwkv_dve(dve, c, cur, nxt, last):
            n, m = counts(dve, c)
            pad = slice(DEC, CH)
            two = lambda b: ps[:, b:b + 2, :].rearrange("p b (a e t) -> p (b a) e t", a=4, e=2)

            def add_power(k, b):
                dve.wait_ge(S[f"r_q{k}_done"], n)
                dve.wait_ge(S[f"r_qt{k - 1}"], n)
                dve.tensor_tensor(qt, qt, split_heads(bank[b]), ALU.add).then_inc(S[f"r_qt{k}"], 1)

            if nxt:
                r_cur, k_cur = frames_of_next(B2, c), frames_of_next(B3, c)
                dve.tensor_tensor(d_k, frames_of_next(B3, c, 1), k_cur, ALU.subtract).then_inc(S["r_kd"], 1)
                dve.tensor_tensor(d_r, frames_of_next(B2, c, 1), r_cur, ALU.subtract).then_inc(S["r_rd"], 1)
                dve.wait_ge(S["r_kd"], m)
                dve.tensor_tensor(d_k, d_k, over(mu[:, 8:16], CH), ALU.mult).then_inc(S["r_km"], 1)
                dve.wait_ge(S["r_rd"], m)
                dve.tensor_tensor(d_r, d_r, over(mu[:, 0:8], CH), ALU.mult).then_inc(S["r_rm"], 1)
                dve.wait_ge(S["r_km"], m)
                dve.tensor_tensor(k_s2, d_k, k_cur, ALU.add).then_inc(S["r_k"], 1)
                dve.wait_ge(S["r_rm"], m)
                dve.tensor_tensor(r_s, d_r, r_cur, ALU.add).then_inc(S["r_r"], 1)
                dve.wait_ge(S["r_k"], m)
                dve.tensor_tensor(kk, k_s2, over(col("rwkv_k_k"), CH), ALU.mult).then_inc(S["r_kk0"], 1)
            if cur:
                add_power(2, 7)
            if nxt:
                dve.wait_ge(S["r_la_exp"], m)
                dve.tensor_scalar(l_a[0:64, 0, :], l_a[0:64, 0, :], 1.0, None, ALU.add)
                dve.tensor_scalar(l_a[:, 1:3, :], l_a[:, 1:3, :], 1.0, None, ALU.add).then_inc(S["r_la_1"], 1)
                dve.wait_ge(S["r_la_1"], m)
                dve.reciprocal(l_a[0:64, 0, :], l_a[0:64, 0, :]).then_inc(S["r_la_tr"], 1)
                dve.reciprocal(l_a[:, 1:3, :], l_a[:, 1:3, :]).then_inc(S["r_la_sg"], 1)
                dve.wait_ge(S["r_la_tr"], m)
                dve.tensor_scalar(l_a[0:64, 0, :], l_a[0:64, 0, :], 2.0, -1.0, ALU.mult, ALU.add).then_inc(S["r_la_th"], 1)
                dve.wait_ge(S["r_kk_ss"], m)
                dve.wait_ge(S["r_kk_sq"], m)
                dve.tensor_scalar(rn, split_heads(bank[3]), 1e-24, None, ALU.max).then_inc(S["r_ssm"], 1)
            if cur:
                add_power(3, 6)
            if nxt:
                dve.wait_ge(S["r_wlora"], m)
                dve.tensor_tensor(sg_s, split_heads(bank[1]), over(col("rwkv_w0"), CH), ALU.add)
                dve.tensor_tensor(a_s, split_heads(bank[4]), over(col("rwkv_a0"), CH), ALU.add).then_inc(S["r_pre"], 1)
            if cur:
                add_power(4, 7)
            if nxt:
                dve.wait_ge(S["r_sa_exp"], m)
                dve.tensor_scalar(sa, sa, 1.0, None, ALU.add).then_inc(S["r_sa_1"], 1)
                dve.wait_ge(S["r_sa_1"], m)
                dve.reciprocal(sa, sa).then_inc(S["r_sa"], 1)
                dve.wait_ge(S["r_sa"], m)
                if last:
                    dve.memset(sg_s[:, :, pad], 0.0).then_inc(S["r_pad"], 1)
                    dve.wait_ge(S["r_pad"], 1)
                dve.tensor_tensor_scan(flat2(rb_s), r_scan, flat2(sg_s), 0.0, ALU.mult, ALU.add).then_inc(S["r_b"], 1)
            if cur:
                dve.wait_ge(S["r_f"], n)
                dve.tensor_tensor(y_s, ff[:, 0], pairs(eye), ALU.add).then_inc(S["r_y1"], 1)
            if nxt:
                dve.scalar_tensor_tensor(out=kmod, in0=a_s, scalar=-1.0, in1=over(col("rwkv_k_a"), CH), op0=ALU.add, op1=ALU.mult).then_inc(S["r_ka"], 1)
                dve.wait_ge(S["r_rn"], m)
                dve.tensor_tensor(kk, kk, rn, ALU.mult).then_inc(S["r_kkn"], 1)
            if cur:
                dve.wait_ge(S["r_y1"], n)
                dve.wait_ge(S["r_f2"], n)
                dve.tensor_tensor(y_s, y_s, f2, ALU.add).then_inc(S["r_y2"], 1)
            if nxt:
                dve.wait_ge(S["r_ka"], m)
                dve.scalar_tensor_tensor(out=kmod, in0=kmod, scalar=1.0, in1=k_s2, op0=ALU.add, op1=ALU.mult).then_inc(S["r_kmod0"], 1)
                dve.wait_ge(S["r_kkn"], m)
                dve.tensor_tensor(bka, kk, a_s, ALU.mult).then_inc(S["r_bka"], 1)
            if cur:
                dve.wait_ge(S["r_y2"], n)
                dve.wait_ge(S["r_f3_done"], n)
                dve.tensor_tensor(y_s, y_s, split_heads(bank[6]), ALU.add).then_inc(S["r_y"], 1)
            if nxt:
                dve.wait_ge(S["r_bka"], m)
                dve.wait_ge(S["r_kmod0"], m)
                if last:
                    dve.memset(kmod[:, :, pad], 0.0).then_inc(S["r_pad"], 1)
                    dve.memset(bka[:, :, pad], 0.0).then_inc(S["r_pad"], 1)
                    dve.wait_ge(S["r_pad"], 3)
                dve.sem_inc(S["r_kmod"], 1)
                dve.wait_ge(S["r_iw"], m)
                dve.tensor_tensor(bh, bka, iw, ALU.mult).then_inc(S["r_bh"], 1)
                dve.tensor_tensor(kh, kmod, iw, ALU.mult).then_inc(S["r_kh"], 1)
            if cur:
                dve.wait_ge(S["r_o_done"], n)
                dve.tensor_tensor(st, st, split_heads(bank[3]), ALU.add).then_inc(S["r_st0"], 1)
                dve.wait_ge(S["r_st0"], n)
                dve.tensor_tensor(st, st, over(w_end, CH), ALU.mult).then_inc(S["r_st"], 1)
            if nxt:
                dve.wait_ge(S["r_w"], m)
                dve.scalar_tensor_tensor(out=ar[:, :, 0, :], in0=kk, scalar=-1.0, in1=w_prev, op0=ALU.mult, op1=ALU.mult).then_inc(S["r_ah"], 1)
                dve.tensor_tensor(ar[:, :, 1, :], r_s, w_cur, ALU.mult).then_inc(S["r_rh"], 1)
            if cur:
                dve.wait_ge(S["r_mean"], n)
                dve.wait_ge(S["r_o"], n)
                dve.scalar_tensor_tensor(out=o_c, in0=split_heads(bank[4]), scalar=-1.0 / 64, in1=o_c, op0=ALU.mult, op1=ALU.add).then_inc(S["r_oc"], 1)
            if nxt:
                dve.wait_ge(S["r_t_done"], m)
                dve.tensor_tensor(t1, split_heads(bank[0]), pairs(d16low), ALU.mult).then_inc(S["r_t1"], 1)
                dve.wait_ge(S["r_tt_done"], m)
                dve.tensor_tensor(a1, two(1)[:, :, 0, :], pairs(d16up), ALU.mult).then_inc(S["r_a1"], 1)
                dve.tensor_tensor(nt, two(1)[:, :, 0, :], pairs(offup), ALU.mult).then_inc(S["r_nt"], 1)
                dve.tensor_tensor(trbT, two(1)[:, :, 1, :], pairs(inclup), ALU.mult).then_inc(S["r_trb"], 1)
                dve.wait_ge(S["r_a1"], m)
                dve.tensor_tensor(qt, a1, pairs(eye), ALU.add).then_inc(S["r_qt1"], 1)
                if cur:
                    dve.wait_ge(S["r_st"], n)
                dve.tensor_copy(w_end, w_dec[:, :, CH:CH + 1].rearrange("p f o -> p (f o)")).then_inc(S["r_wend"], 1)
            if cur:
                dve.wait_ge(S["r_rstd"], n)
                dve.tensor_tensor(o_c, o_c, o_r, ALU.mult).then_inc(S["r_e1"], 1)
            if nxt:
                dve.wait_ge(S["r_tk_done"], m)
                dve.tensor_tensor(takT, two(3)[:, :, 0, :], pairs(strictup), ALU.mult).then_inc(S["r_tak"], 1)
                dve.tensor_tensor(trkT, two(3)[:, :, 1, :], pairs(inclup), ALU.mult).then_inc(S["r_trk"], 1)
            if cur:
                dve.wait_ge(S["r_e1"], n)
                dve.tensor_tensor(o_c, o_c, over(col("rwkv_ln_g"), CH), ALU.mult).then_inc(S["r_e2"], 1)
                dve.wait_ge(S["r_e2"], n)
                dve.tensor_tensor(o_c, o_c, over(col("rwkv_ln_b"), CH), ALU.add).then_inc(S["r_e3"], 1)
                dve.wait_ge(S["r_e3"], n)
                dve.wait_ge(S["r_bonus"], n)
                dve.tensor_tensor(o_c, o_c, bonus, ALU.add).then_inc(S["r_e4"], 1)
                dve.wait_ge(S["r_e4"], n)
                dve.wait_ge(S["r_gg"], n)
                dve.tensor_tensor(o_c, o_c, gg, ALU.mult).then_inc(S["r_e5"], 1)
                dve.wait_ge(S["r_e5"], n)
                dve.tensor_tensor(frames(B5, c * CH, CH), frames(B5, c * CH, CH), o_c, ALU.add).then_inc(S["r_chunk_done"], 1)

        def rwkv_pe(pe, c, cur, nxt):
            n, m = counts(pe, c)

            def const():
                pe.wait_ge(S["r_masks"], 1)

            def both(b, x):
                for a in range(FT):
                    for q in range(2):
                        mm = pe.matmul(bank[b + a // 4][q_half(q), (a % 4) * 2 * CH:(a % 4 + 1) * 2 * CH], x[q_half(q), a, :],
                                       ar[q_half(q), a, :, :], start=True, stop=True)
                return mm

            if cur:
                pe.wait_ge(S["r_v_tok"], n)
                pe.sem_inc(S["r_core_begun"], 1)
                const()
                pe.wait_ge(S["r_b_tok"], n)
                pe.wait_ge(S["r_t1"], n)
                pe.wait_ge(S["r_a1"], n)
                per_head(pe, 5, t1, a1)
                per_head(pe, 6, a1, t1).then_inc(S["r_sq2"], 1)
                const()
                pe.wait_ge(S["r_a2t2"], n)
                per_head(pe, 5, a2t2[:, 1], a2t2[:, 0])
                per_head(pe, 6, a2t2[:, 0], a2t2[:, 1]).then_inc(S["r_sq4"], 1)
                const()
                pe.wait_ge(S["r_k_tok"], n)
                pe.wait_ge(S["r_qt1"], n)
                per_head(pe, 7, a2t2[:, 1], qt).then_inc(S["r_q2_done"], 1)
            if nxt:
                if cur:
                    pe.wait_ge(S["r_trk"], n)
                pe.wait_ge(S["r_kk_sq"], m)
                pe.matmul(bank[3], head_ones[:, :], flat2(rn), start=True, stop=True).then_inc(S["r_kk_ss"], 1)
            if cur:
                const()
                pe.wait_ge(S["r_a4"], n)
                per_head(pe, 5, a4, t4).then_inc(S["r_sq8"], 1)
                const()
                pe.wait_ge(S["r_qt2"], n)
                per_head(pe, 6, t4, qt).then_inc(S["r_q3_done"], 1)
            if nxt:
                const()
                pe.wait_ge(S["r_l"], m)
                for f in range(FT):
                    pe.matmul(b_cols(4, f), wa2[64:128, f * P:(f + 1) * P], l_s[64:128, 0, :], start=True, stop=True)
                pe.wait_ge(S["r_la_th"], m)
                for f in range(FT):
                    mm = pe.matmul(b_cols(1, f), wa2[0:64, f * P:(f + 1) * P], l_a[0:64, 0, :], start=True, stop=True)
                mm.then_inc(S["r_wlora"], 1)
            if cur:
                const()
                pe.wait_ge(S["r_tak"], n)
                for a in range(FT):
                    for q in range(2):
                        r = q_half(q)
                        pe.matmul(bank[0][r, a * CH:(a + 1) * CH], takT[r, a, :], v_tok2[r, a, :], start=True, stop=False)
                        mm = pe.matmul(bank[0][r, a * CH:(a + 1) * CH], ar[r, a, 0, :], st[r, a, :], start=False, stop=True)
                mm.then_inc(S["r_z_done"], 1)
                const()
                pe.wait_ge(S["r_t8"], n)
                pe.wait_ge(S["r_qt3"], n)
                per_head(pe, 7, t8, qt).then_inc(S["r_q4_done"], 1)
            if nxt:
                pe.wait_ge(S["r_la_sg"], m)
                for f in range(FT):
                    pe.matmul(b_cols(2, f), g2a[:, f * P:(f + 1) * P], l_a[:, 1, :], start=True, stop=False)
                    mm = pe.matmul(b_cols(2, f), g2b[0:32, f * P:(f + 1) * P], l_a[0:32, 2, :], start=False, stop=True)
                mm.then_inc(S["r_glora"], 1)
            if cur:
                const()
                pe.wait_ge(S["r_qt4"], n)
                turn_heads(pe, 5, qt).then_inc(S["r_q_turned"], 1)
                const()
                pe.wait_ge(S["r_nt"], n)
                pe.wait_ge(S["r_q"], n)
                per_head(pe, 6, nt, q_inv)
                per_head(pe, 7, q_inv, nt).then_inc(S["r_f_done"], 1)
                const()
                pe.wait_ge(S["r_f"], n)
                per_head(pe, 5, ff[:, 1], ff[:, 0]).then_inc(S["r_f2_done"], 1)
                const()
                pe.wait_ge(S["r_f2"], n)
                per_head(pe, 6, ff[:, 1], f2).then_inc(S["r_f3_done"], 1)
                const()
                pe.wait_ge(S["r_y"], n)
                per_head(pe, 7, y_s, qt).then_inc(S["r_mt_done"], 1)
                const()
                pe.wait_ge(S["r_z"], n)
                if nxt:
                    pe.wait_ge(S["r_pre"], m)
                pe.wait_ge(S["r_mt"], n)
                per_head(pe, 1, mt, z_s).then_inc(S["r_u_done"], 1)
                const()
                pe.wait_ge(S["r_u"], n)
                for a in range(FT):
                    for q in range(2):
                        r = q_half(q)
                        out = bank[3][r, a * CH:(a + 1) * CH]
                        pe.matmul(out, b_tok[r, a, :], u_s[r, a, :], start=True, stop=False)
                        pe.matmul(out, k_tok2[r, a, :], v_tok2[r, a, :], start=False, stop=True)
                if nxt:
                    const()
                    pe.wait_ge(S["r_g"], m)
                const()
                pe.wait_ge(S["r_trk"], n)
                for a in range(FT):
                    for q in range(2):
                        r = q_half(q)
                        out = bank[2][r, a * CH:(a + 1) * CH]
                        pe.matmul(out, st[r, a, :], ar[r, a, 1, :], start=True, stop=False)
                        pe.matmul(out, u_s[r, a, :], trbT[r, a, :], start=False, stop=False)
                        mm = pe.matmul(out, v_tok2[r, a, :], trkT[r, a, :], start=False, stop=True)
                mm.then_inc(S["r_o_done"], 1)
            if nxt:
                pe.wait_ge(S["r_rk"], m)
                pe.matmul(bank[7], head_ones[:, :], flat2(rk_s), start=True, stop=True).then_inc(S["r_rk_ss"], 1)
                const()
                pe.wait_ge(S["r_bh"], m)
                pe.wait_ge(S["r_ah"], m)
                per_head(pe, 0, ar[:, :, 0, :], bh).then_inc(S["r_t_done"], 1)
            if cur:
                pe.wait_ge(S["r_o"], n)
                pe.matmul(bank[4], head_ones[:, :], flat2(o_c), start=True, stop=True).then_inc(S["r_mean"], 1)
            if nxt:
                const()
                pe.wait_ge(S["r_rh"], m)
                both(1, bh).then_inc(S["r_tt_done"], 1)
                turn_heads(pe, 6, bh).then_inc(S["r_b_turned"], 1)
            if cur:
                pe.wait_ge(S["r_o_sq"], n)
                pe.matmul(bank[5], head_ones[:, :], flat2(o_q), start=True, stop=True).then_inc(S["r_var"], 1)
            if nxt:
                const()
                pe.wait_ge(S["r_rks"], m)
                pe.wait_ge(S["r_kh"], m)
                turn_heads(pe, 7, kh).then_inc(S["r_k_turned"], 1)
                const()
                if cur:
                    pe.wait_ge(S["r_oc"], n)
                    pe.wait_ge(S["r_st0"], n)
                both(3, kh).then_inc(S["r_tk_done"], 1)
                const()
                pe.wait_ge(S["r_v"], m)
                if cur:
                    pe.wait_ge(S["r_ln_var"], n)
                turn_heads(pe, 5, v_s2).then_inc(S["r_v_turned"], 1)

        ends = ((0, SEQ), (32, N))
        shift_cols = rows_a
        shift_rows = rows_b
        full = N_RWKV // P
        rest = N_RWKV - full * P

        with nc.Block() as block:
            @block.gpsimd
            def _(pool):
                for m in (d16low, d16up, offup, strictup, inclup, eye):
                    pool.memset(m, 1.0).then_inc(S["r_mask_ones"], 1)
                pool.memset(r_scan, 1.0).then_inc(S["r_mask_ones"], 1)
                pool.memset(st, 0.0).then_inc(S["r_mask_ones"], 1)
                pool.memset(w_dec[:, :, 0:1], 1.0).then_inc(S["r_mask_ones"], 1)
                pool.wait_ge(S["r_mask_ones"], 9)
                pool.memset(r_scan.rearrange("p (m l) -> p m l", l=CH)[:, :, 0:1], 0.0).then_inc(S["r_scan_ready"], 1)
                pool.wait_ge(S["r_scan_ready"], 1)
                k = 0

                def cut(m, pattern, base, mult, op=ALU.is_ge):
                    pool.affine_select(out=m, in_=m, compare_op=op, fill=0.0, base=base, pattern=pattern,
                                       channel_multiplier=mult).then_inc(S["r_mask_cut"], 1)

                for q in range(2):
                    r = q_half(q)
                    b16 = lambda m: m[r].rearrange("p (b l) -> p b l", l=16)
                    steps = [
                        [(d16low[r], [[-1, CH]], -1, 1), (d16up[r], [[1, CH]], -1, -1), (strictup[r], [[1, CH]], -1, -1),
                         (inclup[r], [[1, CH]], 0, -1), (b16(offup), [[16, 4], [0, 16]], -1, -1)],
                        [(b16(d16low), [[16, 4], [0, 16]], 15, -1), (b16(d16up), [[-16, 4], [0, 16]], 0, 1)],
                    ]
                    for step in steps:
                        for m, pattern, base, mult in step:
                            cut(m, pattern, base, mult)
                            k += 1
                            pool.wait_ge(S["r_mask_cut"], k)
                    cut(eye[r], [[1, CH]], 0, -1, ALU.is_equal)
                    k += 1
                    pool.wait_ge(S["r_mask_cut"], k)
                pool.wait_ge(S["r_lora_in"], 64)
                pool.wait_ge(S["r_ends_kept"], 1)
                pool.sem_inc(S["r_masks"], 1)
                pool.sem_inc(S["r_chunk_done"], 1)
                rwkv_pool(pool, -1, False, True)
                with pool.Fori(0, NCH - 1) as c:
                    rwkv_pool(pool, c, True, True)
                pool.wait_ge(S["r_shift_swapped"], 4)
                rwkv_pool(pool, NCH - 1, True, True)
                rwkv_pool(pool, NCH, True, False)

            @block.sync
            def _(sp):
                sp.dma_start(wa2[0:64, :], I["rwkv_w2"][0]).then_inc(S["r_lora_in"], 16)
                sp.dma_start(wa2[64:128, :], I["rwkv_a2"][0]).then_inc(S["r_lora_in"], 16)
                sp.dma_start(g2a, I["rwkv_g2"][0][0:P, :]).then_inc(S["r_lora_in"], 16)
                sp.dma_start(g2b[0:32, :], I["rwkv_g2"][0][P:GATE_L, :]).then_inc(S["r_lora_in"], 16)
                sp.wait_ge(S["r_ends_kept"], 1)
                for (r0, _), name in zip(ends, ("shift_prompt", "shift_sample")):
                    out = O[name][0, 0, 0]
                    sp.dma_start(out[0:full * P].rearrange("(f p) -> f p", p=P), shift_rows[r0:r0 + full, :]).then_inc(S["r_shift_out"], 16)
                    sp.dma_start(out[full * P:N_RWKV].unsqueeze(0), shift_rows[r0 + full:r0 + full + 1, 0:rest]).then_inc(S["r_shift_out"], 16)
                rows = "(a q) v k -> (q v) a k"
                sp.wait_ge(S["r_state_turned"], 1)
                sp.dma_start(O["rwkv_prompt"][0, 0].rearrange(rows, q=2), st_vk).then_inc(S["r_state_out"], 16)
                sp.dma_start(st_in, I["state_rwkv"][0, 0].rearrange(rows, q=2)).then_inc(S["r_state_in"], 16)
                sp.wait_ge(S["r_state_turned"], 2)
                sp.dma_start(O["rwkv_sample"][0, 0].rearrange(rows, q=2), st_vk).then_inc(S["r_state_out"], 16)
                sp.wait_ge(S["r_state_out"], 32)
                sp.wait_ge(S["r_shift_out"], 64)

            @block.scalar
            def _(act):
                rwkv_act(act, -1, False, True)
                with act.Fori(0, NCH - 1) as c:
                    rwkv_act(act, c, True, True)
                rwkv_act(act, NCH - 1, True, True)
                act.wait_ge(S["r_end_turned"], 1)
                act.copy(st_vk, split_heads(bank[6])).then_inc(S["r_state_turned"], 1)
                act.wait_ge(S["r_state_out"], 16)
                rwkv_act(act, NCH, True, False)
                act.wait_ge(S["r_end_turned"], 2)
                act.copy(st_vk, split_heads(bank[6])).then_inc(S["r_state_turned"], 1)

            @block.vector
            def _(dve):
                dve.memset(shift_cols[:, :], 0.0).then_inc(S["r_ends_zero"], 1)
                dve.wait_ge(S["r_ends_zero"], 1)
                for r0, at in ends:
                    for g, base in enumerate((B2, B3, B4)):
                        dve.tensor_copy(shift_cols[:, r0 + 8 * g:r0 + 8 * g + 8].unsqueeze(2), arena[:, base:base + FT, at:at + 1])
                    cp = dve.tensor_copy(shift_cols[:, r0 + 24:r0 + 27].unsqueeze(2), lora[:, :, at:at + 1])
                cp.then_inc(S["r_ends"], 1)
                dve.wait_ge(S["r_ends_turned"], 1)
                dve.tensor_copy(shift_rows[:, :], bank[0][:, 0:P]).then_inc(S["r_ends_kept"], 1)
                dve.wait_ge(S["r_masks"], 1)
                rwkv_dve(dve, -1, False, True, False)
                with dve.Fori(0, NCH - 1) as c:
                    rwkv_dve(dve, c, True, True, False)
                dve.wait_ge(S["r_l"], NCH)
                dve.wait_ge(S["r_v"], NCH)
                for g, base in enumerate((B2, B3, B4)):
                    dve.tensor_copy(arena[:, base:base + FT, SEQ:SEQ + 1], cb[:, SHIFT + 8 * g:SHIFT + 8 * g + 8].unsqueeze(2)).then_inc(S["r_shift_swapped"], 1)
                dve.tensor_copy(lora[:, :, SEQ:SEQ + 1], cb[:, SHIFT + 24:SHIFT + 27].unsqueeze(2)).then_inc(S["r_shift_swapped"], 1)
                dve.wait_ge(S["r_shift_swapped"], 4)
                rwkv_dve(dve, NCH - 1, True, True, True)
                dve.wait_ge(S["r_start_turned"], 1)
                dve.tensor_copy(st, split_heads(bank[7])).then_inc(S["r_swapped"], 1)
                rwkv_dve(dve, NCH, True, False, False)

            @block.tensor
            def _(pe):
                pe.wait_ge(S["r_ends"], 1)
                pe.transpose(bank[0][:, 0:P], shift_cols[:, :], ident[:, :]).then_inc(S["r_ends_turned"], 1)
                pe.wait_ge(S["r_ends_kept"], 1)
                pe.wait_ge(S["r_masks"], 1)
                rwkv_pe(pe, -1, False, True)
                with pe.Fori(0, NCH - 1) as c:
                    rwkv_pe(pe, c, True, True)
                rwkv_pe(pe, NCH - 1, True, True)
                pe.wait_ge(S["r_st"], NCH)
                pe.wait_ge(S["r_b_tok"], NCH + 1)
                pe.wait_ge(S["r_k_tok"], NCH + 1)
                turn_heads(pe, 6, st).then_inc(S["r_end_turned"], 1)
                pe.wait_ge(S["r_state_in"], 16)
                turn_heads(pe, 7, st_in).then_inc(S["r_start_turned"], 1)
                pe.wait_ge(S["r_swapped"], 1)
                rwkv_pe(pe, NCH, True, False)
                pe.wait_ge(S["r_chunk_done"], NCH + 2)
                turn_heads(pe, 6, st).then_inc(S["r_end_turned"], 1)

        S.end_stage()

        mroom = Room(flat[:, B2 * BW:B5 * BW], 3 * FT * BW)
        memT, mem_n, mem_sq = (mroom.take(FT, MEM) for _ in range(3))
        mem_tok = mroom.take(2, D)
        aroom = Room(scr[:, :], SCR)
        kT = [aroom.take(FT, MEM) for _ in range(2)]
        v_mem = [aroom.take(2, D) for _ in range(2)]
        k_mem = [mroom.take(2, D) for _ in range(2)]
        a_sq_base = aroom.at

        l_sp, l_pe, l_leave = linear([("add", I["w_out"][0], 0, 4, B5, H),
                                      ("rows", I["wk_x"][0], 0, 4, mem_n, k_mem[0]), ("rows", I["wv_x"][0], 0, 4, mem_n, v_mem[0])])
        m_act, m_pe, m_dve = norm_stage("mem", memT, mem_n, lambda f: col("norm_mem_g", f), MEM, mem_sq)

        def turn_rows(pe, src, j, b):
            for f in range(4):
                mm = pe.transpose(bank[b][:, f * P:(f + 1) * P], src[:, j // 2, ((j % 2) * 4 + f) * P:((j % 2) * 4 + f + 1) * P], ident[:, :])
            return mm

        def turned(dst, j):
            return dst[:, (j % 2) * 4:(j % 2) * 4 + 4, (j // 2) * P:(j // 2 + 1) * P]

        def quarters(b):
            return bank[b].rearrange("p (f n) -> p f n", f=4)

        with nc.Block() as block:
            @block.sync
            def _(sp):
                sp.dma_start(flat[:, H * BW:(H + FT) * BW], h_kept).then_inc(S["h_back"], 16)
                sp.dma_start(mem_tok, I["mem_prompt"][0].rearrange("(t p) d -> p t d", p=P)).then_inc(S["mem_in"], 16)
                sp.dma_start(k_mem[1], I["cache_mem_k"][0, 0].rearrange("(t p) h d -> p t (h d)", p=P)).then_inc(S["cache_in"], 16)
                sp.dma_start(v_mem[1], I["cache_mem_v"][0, 0].rearrange("(t p) h d -> p t (h d)", p=P)).then_inc(S["cache_in"], 16)
                l_sp(sp)
                rows = "(t p) h d -> p t (h d)"
                sp.wait_ge(S["banks0_free"], used[0] + 1)
                sp.wait_ge(S["banks1_free"], used[0] + 1)
                sp.dma_start(O["mem_k"][0, 0].rearrange(rows, p=P), k_mem[0]).then_inc(S["mem_out"], 16)
                sp.dma_start(O["mem_v"][0, 0].rearrange(rows, p=P), v_mem[0]).then_inc(S["mem_out"], 16)
                sp.wait_ge(S["mem_out"], 32)

            @block.scalar
            def _(act):
                act.wait_ge(S["memT"], 4)
                m_act(act)
                l_leave(act, False)

            @block.tensor
            def _(pe):
                pe.wait_ge(S["mem_in"], 16)
                for j in range(4):
                    mm = turn_rows(pe, mem_tok, j, j)
                mm.then_inc(S["mem_turned"], 1)
                pe.wait_ge(S["cache_in"], 32)
                for j in range(4):
                    mm = turn_rows(pe, k_mem[1], j, 4 + j)
                mm.then_inc(S["cache_turned"], 1)
                pe.wait_ge(S["memT"], 4)
                m_pe(pe)
                pe.wait_ge(S["mem_normed"], FT)
                pe.wait_ge(S["cacheT"], 4)
                l_pe(pe)
                pe.wait_ge(S["banks0_free"], used[0] + 1)
                pe.wait_ge(S["banks1_free"], used[0] + 1)
                for j in range(4):
                    mm = turn_rows(pe, k_mem[0], j, j)
                mm.then_inc(S["keys_turned"], 1)

            @block.vector
            def _(dve):
                dve.wait_ge(S["mem_turned"], 1)
                for j in range(4):
                    dve.tensor_copy(turned(memT, j), quarters(j)).then_inc(S["memT"], 1)
                dve.wait_ge(S["cache_turned"], 1)
                for j in range(4):
                    dve.tensor_copy(turned(kT[1], j), quarters(4 + j)).then_inc(S["cacheT"], 1)
                m_dve(dve)
                dve.wait_ge(S["h_back"], 16)
                l_leave(dve, True)
                dve.wait_ge(S["keys_turned"], 1)
                for j in range(4):
                    dve.tensor_copy(turned(kT[0], j), quarters(j)).then_inc(S["keysT"], 1)

        S.end_stage()

        sq_b = shaped(flat, B4 * BW, (FT, N))
        n_act, n_pe, n_dve = norm_stage("x", whole(H), whole(XN), lambda f: col("norm_x_g", f), N, sq_b)
        l_sp, l_pe, l_leave = linear([("keep", I["wq_x"][0], 0, 4, XN, B2)])

        with nc.Block() as block:
            @block.sync
            def _(sp):
                l_sp(sp)

            @block.scalar
            def _(act):
                n_act(act)
                l_leave(act, False)

            @block.tensor
            def _(pe):
                n_pe(pe)
                pe.wait_ge(S["x_normed"], FT)
                pe.wait_ge(S["x_rms"], 2)
                l_pe(pe)

            @block.vector
            def _(dve):
                n_dve(dve)

        S.end_stage()

        q_s, p_s, pT = aroom.take(FT, P), aroom.take(XH, MEM), aroom.take(FT, P)
        mx, sm = aroom.take(XH), aroom.take(XH)

        def attention_act(act, t, n, m):
            act.wait_ge(S["a_tile_done"], n)
            act.copy(q_s[:, :, 0:m], frames(B2, t * P, m)).then_inc(S["a_q"], 1)
            act.wait_ge(S["a_shifted"], n)
            act.activation(p_s[0:m], p_s[0:m], ACT.Exp, scale=XSCALE).then_inc(S["a_exp"], 1)
            act.wait_ge(S["a_turned"], n)
            act.copy(pT[:, :, 0:m], ps[:, 2:4, :].rearrange("p b (f n) -> p (b f) n", f=4)[:, :, 0:m]).then_inc(S["a_pT"], 1)
            act.wait_ge(S["a_o"], n)
            act.copy(frames(B3, t * P, m), ps[:, 4:6, :].rearrange("p b (f n) -> p (b f) n", f=4)[:, :, 0:m]).then_inc(S["a_tile_done"], 1)

        def attention_dve(dve, t, n, m):
            scores = ps[0:m, 0:2, :].rearrange("p b (h k) -> p (b h) k", h=2)
            dve.wait_ge(S["a_scores"], n)
            dve.tensor_reduce(mx[0:m], scores, AX_X, ALU.max).then_inc(S["a_max"], 1)
            dve.wait_ge(S["a_max"], n)
            dve.tensor_tensor(p_s[0:m], scores, mx[0:m].unsqueeze(2).to_broadcast([m, XH, MEM]), ALU.subtract).then_inc(S["a_shifted"], 1)
            dve.wait_ge(S["a_exp"], n)
            dve.tensor_reduce(sm[0:m], p_s[0:m], AX_X, ALU.add).then_inc(S["a_sum"], 1)
            dve.wait_ge(S["a_sum"], n)
            dve.reciprocal(sm[0:m], sm[0:m]).then_inc(S["a_rsum"], 1)
            dve.wait_ge(S["a_rsum"], n)
            dve.tensor_tensor(p_s[0:m], p_s[0:m], sm[0:m].unsqueeze(2).to_broadcast([m, XH, MEM]), ALU.mult).then_inc(S["a_p"], 1)

        def attention_pe(pe, t, n, m, group):
            pe.wait_ge(S["a_q"], n)
            for h in range(XH):
                for k in range(2):
                    mm = pe.matmul(ps[0:m, h // 2, (h % 2) * MEM:(h % 2 + 1) * MEM], q_s[:, 2 * h + k, 0:m], kT[group][:, 2 * h + k, :],
                                   start=(k == 0), stop=(k == 1))
            mm.then_inc(S["a_scores"], 1)
            pe.wait_ge(S["a_p"], n)
            for h in range(XH):
                for j in range(2):
                    b = 2 * h + j
                    mm = pe.transpose(ps[:, 2 + b // 4, (b % 4) * P:(b % 4) * P + m], p_s[0:m, h, j * P:(j + 1) * P], ident[0:m, 0:m])
            mm.then_inc(S["a_turned"], 1)
            pe.wait_ge(S["a_pT"], n)
            for b in range(FT):
                for j in range(2):
                    mm = pe.matmul(ps[:, 4 + b // 4, (b % 4) * P:(b % 4) * P + m], v_mem[group][:, j, b * P:(b + 1) * P], pT[:, 2 * (b // 2) + j, 0:m],
                                   start=(j == 0), stop=(j == 1))
            mm.then_inc(S["a_o"], 1)

        tiles = SEQ // P
        with nc.Block() as block:
            @block.gpsimd
            def _(pool):
                pool.sem_inc(S["a_tile_done"], 1)

            @block.scalar
            def _(act):
                with act.Fori(0, tiles) as t:
                    attention_act(act, t, act.snap(t + 1), P)
                attention_act(act, tiles, tiles + 1, DEC)

            @block.vector
            def _(dve):
                with dve.Fori(0, tiles) as t:
                    attention_dve(dve, t, dve.snap(t + 1), P)
                attention_dve(dve, tiles, tiles + 1, DEC)

            @block.tensor
            def _(pe):
                with pe.Fori(0, tiles) as t:
                    attention_pe(pe, t, pe.snap(t + 1), P, 0)
                attention_pe(pe, tiles, tiles + 1, DEC, 1)

        S.end_stage()

        l_sp, l_pe, l_leave = linear([("add", I["wo_x"][0], 0, 4, B3, H)])
        n_act, n_pe, n_dve = norm_stage("ffn", whole(H), whole(XN), lambda f: col("norm_ffn_g", f), N, sq_b)
        eroom = Room(scr[:, :], SCR)
        NR = GROUPS + EXPERTS
        h_tok = eroom.take(TT, D)
        w_route = eroom.take(FT, NR)
        b_route = eroom.take(NR)
        lg = eroom.take(TT, NR)
        gmax, gsum, m1, m2, e2, wsum, w1, w2 = (eroom.take(TT) for _ in range(8))
        slot_f = [eroom.take(TT) for _ in range(TOP_K)]
        ge, oh_g, seen_g, one_g = (eroom.take(TT, GROUPS) for _ in range(4))
        le4 = eroom.take(TT * GROUPS, PER_GROUP)
        lec, o1, o2, seen = (eroom.take(TT, PER_GROUP) for _ in range(4))
        one_e = eroom.take(TT, PER_GROUP)
        pick = [eroom.take(TT, EXPERTS) for _ in range(TOP_K)]
        both, slot_e = eroom.take(TT, EXPERTS), eroom.take(TT, EXPERTS)
        count, blocks_e, ends_e, base_e = (eroom.take(EXPERTS) for _ in range(4))
        before = eroom.take(P)
        blk_no = eroom.take(NBLK)
        over_e = eroom.take(NBLK, EXPERTS)
        owner_f = eroom.take(NBLK)
        x_rows = shaped(flat, B4 * BW, (TT, D))
        slot_i = [ctx.enter_context(nc.sbuf_tensor(f"slot_i{k}", [P, TT], U32)) for k in range(TOP_K)]
        owner = ctx.enter_context(nc.sbuf_tensor("owner", [1, NBLK], I32))
        blk_int = ctx.enter_context(nc.sbuf_tensor("blk_int", [1, NBLK], I32))
        exp_l = lg[:, :, GROUPS:NR]

        def wide(v, n):
            return v.unsqueeze(2).to_broadcast([P, v.shape[1], n])

        def first_of(dve, name, eq, scan_mask, seen_):
            dve.wait_ge(S[name + "_eq"], 1)
            dve.tensor_tensor_scan(flat2(seen_), flat2(scan_mask), flat2(eq), 0.0, ALU.mult, ALU.add).then_inc(S[name + "_seen"], 1)
            dve.wait_ge(S[name + "_seen"], 1)
            dve.scalar_tensor_tensor(out=eq, in0=seen_, scalar=1.0, in1=eq, op0=ALU.is_equal, op1=ALU.mult).then_inc(S[name], 1)
            dve.wait_ge(S[name], 1)

        def tokens(t):
            return P if t < TT - 1 else DEC

        def count_tokens(pe):
            pe.wait_ge(S["picks"], 1)
            pe.wait_ge(S["before"], 1)
            for t in range(TT):
                m = tokens(t)
                pe.matmul(bank[3][:, 0:EXPERTS], ones[0:m, :], both[0:m, t, :], start=(t == 0), stop=(t == TT - 1))
            for t in range(TT):
                m = tokens(t)
                out = bank[3][0:m, (t + 1) * EXPERTS:(t + 2) * EXPERTS]
                for u in range(t):
                    pe.matmul(out, ones[:, 0:m], both[:, u, :], start=(u == 0), stop=False)
                mm = pe.matmul(out, before[0:m, 0:m], both[0:m, t, :], start=(t == 0), stop=True)
            mm.then_inc(S["counted"], 1)

        turns = [(XN, x_rows, j) for j in range(2 * TT)] + [(H, h_tok, j) for j in range(2 * TT)]

        with nc.Block() as block:
            @block.sync
            def _(sp):
                sp.dma_start(w_route[:, :, 0:GROUPS], I["router_group_w"][0].rearrange("(k p) n -> p k n", p=P)).then_inc(S["route_in"], 16)
                sp.dma_start(w_route[:, :, GROUPS:NR], I["router_expert_w"][0].rearrange("(k p) n -> p k n", p=P)).then_inc(S["route_in"], 16)
                sp.dma_start(b_route[0:1, 0:GROUPS], I["router_group_b"]).then_inc(S["route_in"], 16)
                sp.dma_start(b_route[0:1, GROUPS:NR], I["router_expert_b"].rearrange("a g e -> a (g e)")).then_inc(S["route_in"], 16)
                l_sp(sp)

            @block.scalar
            def _(act):
                act.wait_ge(S["banks0_free"], used[0] + 1)
                act.wait_ge(S["banks1_free"], used[0] + 1)
                n_act(act)
                for i, (base, dst, j) in enumerate(turns):
                    act.wait_ge(S["rows_turned"], i + 1)
                    m = tokens(j // 2)
                    act.copy(dst[0:m, j // 2, (j % 2) * 512:(j % 2 + 1) * 512], ps[0:m, 4 + i % 4, :]).then_inc(S["rows_kept"], 1)
                    if i == 9:
                        act.wait_ge(S["g_shifted"], 1)
                        act.activation(ge, ge, ACT.Exp).then_inc(S["g_exp"], 1)
                    if i == 12:
                        act.wait_ge(S["e_shifted"], 1)
                        act.activation(e2, e2, ACT.Exp).then_inc(S["e_exp"], 1)

            @block.gpsimd
            def _(pool):
                pool.memset(one_g, 1.0).then_inc(S["scan_ones"], 1)
                pool.memset(one_e, 1.0).then_inc(S["scan_ones"], 1)
                pool.memset(lg, 0.0).then_inc(S["lg_zero"], 1)
                pool.memset(before, 1.0).then_inc(S["scan_ones"], 1)
                pool.iota(blk_int[:, :], pattern=[[1, NBLK]], base=0, channel_multiplier=0).then_inc(S["blk_int"], 1)
                pool.wait_ge(S["scan_ones"], 3)
                pool.memset(one_g[:, :, 0:1], 0.0).then_inc(S["scan_masks"], 1)
                pool.memset(one_e[:, :, 0:1], 0.0).then_inc(S["scan_masks"], 1)
                pool.affine_select(out=before, in_=before, compare_op=ALU.is_ge, fill=0.0, base=-1,
                                   pattern=[[1, P]], channel_multiplier=-1).then_inc(S["before"], 1)
                pool.wait_ge(S["rows_kept"], 2 * TT)
                pool.wait_ge(S["slots_known"], TOP_K)
                for t in range(TT):
                    for k in range(TOP_K):
                        m = tokens(t)
                        pool.indirect_dma_start(x_slots, bass.IndirectOffsetOnAxis(slot_i[k][0:m, t:t + 1], 0), x_rows[0:m, t, :], None).then_inc(S["scattered"], 16)
                pool.wait_ge(S["scattered"], 16 * TT * TOP_K)

            @block.tensor
            def _(pe):
                l_pe(pe)
                n_pe(pe)
                pe.wait_ge(S["ffn_normed"], FT)
                pe.wait_ge(S["route_in"], 64)
                for t in range(TT):
                    m = tokens(t)
                    out = bank[2][0:m, t * NR:(t + 1) * NR]
                    for k in range(FT):
                        pe.matmul(out, arena[:, XN + k, 1 + t * P:1 + t * P + m], w_route[:, k, :], start=(k == 0), stop=False)
                    mm = pe.matmul(out, ones[0:1, 0:m], b_route[0:1, :], start=False, stop=True)
                mm.then_inc(S["logits"], 1)
                for i, (base, dst, j) in enumerate(turns):
                    m = tokens(j // 2)
                    if i >= 4:
                        pe.wait_ge(S["rows_kept"], i - 3)
                    if i == 2 * TT:
                        count_tokens(pe)
                    for f in range(4):
                        mm = pe.transpose(ps[0:m, 4 + i % 4, f * P:(f + 1) * P],
                                          arena[:, base + (j % 2) * 4 + f, 1 + (j // 2) * P:1 + (j // 2) * P + m], ident[:, :])
                    mm.then_inc(S["rows_turned"], 1)

            @block.vector
            def _(dve):
                l_leave(dve, True)
                n_dve(dve)
                dve.wait_ge(S["logits"], 1)
                dve.wait_ge(S["lg_zero"], 1)
                dve.tensor_copy(lg[:, 0:TT - 1, :], bank[2][:, 0:(TT - 1) * NR].rearrange("p (t n) -> p t n", t=TT - 1)).then_inc(S["lg"], 1)
                dve.tensor_copy(lg[0:DEC, TT - 1, :], bank[2][0:DEC, (TT - 1) * NR:TT * NR]).then_inc(S["lg"], 1)
                dve.wait_ge(S["lg"], 2)
                dve.tensor_reduce(gmax, lg[:, :, 0:GROUPS], AX_X, ALU.max).then_inc(S["gmax"], 1)
                dve.wait_ge(S["gmax"], 1)
                dve.tensor_tensor(ge, lg[:, :, 0:GROUPS], wide(gmax, GROUPS), ALU.subtract).then_inc(S["g_shifted"], 1)
                dve.tensor_tensor(oh_g, lg[:, :, 0:GROUPS], wide(gmax, GROUPS), ALU.is_equal).then_inc(S["group_eq"], 1)
                dve.wait_ge(S["scan_masks"], 2)
                first_of(dve, "group", oh_g, one_g, seen_g)
                oh_ge = flat2(oh_g).unsqueeze(2).to_broadcast([P, TT * GROUPS, PER_GROUP])
                by_group = "p (t g) e -> p t g e"
                dve.tensor_tensor(le4.rearrange(by_group, t=TT), exp_l.rearrange("p t (g e) -> p t g e", g=GROUPS),
                                  oh_ge.rearrange(by_group, t=TT), ALU.mult).then_inc(S["le4"], 1)
                dve.wait_ge(S["le4"], 1)
                dve.tensor_reduce(lec, le4.rearrange("p (t g) e -> p t e g", t=TT), AX_X, ALU.add).then_inc(S["lec"], 1)
                dve.wait_ge(S["lec"], 1)
                dve.tensor_reduce(m1, lec, AX_X, ALU.max).then_inc(S["m1"], 1)
                dve.wait_ge(S["m1"], 1)
                dve.tensor_tensor(o1, lec, wide(m1, PER_GROUP), ALU.is_equal).then_inc(S["top1_eq"], 1)
                first_of(dve, "top1", o1, one_e, seen)
                dve.scalar_tensor_tensor(out=lec, in0=o1, scalar=-1e30, in1=lec, op0=ALU.mult, op1=ALU.add).then_inc(S["lec2"], 1)
                dve.wait_ge(S["lec2"], 1)
                dve.tensor_reduce(m2, lec, AX_X, ALU.max).then_inc(S["m2"], 1)
                dve.wait_ge(S["m2"], 1)
                dve.tensor_tensor(e2, m2, m1, ALU.subtract).then_inc(S["e_shifted"], 1)
                dve.tensor_tensor(o2, lec, wide(m2, PER_GROUP), ALU.is_equal).then_inc(S["top2_eq"], 1)
                first_of(dve, "top2", o2, one_e, seen)
                for k, o in enumerate((o1, o2)):
                    dve.tensor_tensor(pick[k].rearrange("p t (g e) -> p t g e", g=GROUPS), oh_ge.rearrange(by_group, t=TT),
                                      o.unsqueeze(2).to_broadcast([P, TT, GROUPS, PER_GROUP]), ALU.mult).then_inc(S["pick"], 1)
                dve.wait_ge(S["pick"], TOP_K)
                dve.tensor_tensor(both, pick[0], pick[1], ALU.add).then_inc(S["picks"], 1)
                dve.memset(blocks_e, 0.0).then_inc(S["blocks"], 1)
                dve.wait_ge(S["counted"], 1)
                dve.tensor_copy(count, bank[3][:, 0:EXPERTS]).then_inc(S["count"], 1)
                dve.wait_ge(S["count"], 1)
                for b in range(MAXB):
                    dve.wait_ge(S["blocks"], b + 1)
                    dve.scalar_tensor_tensor(out=blocks_e, in0=count, scalar=float(b * BLK), in1=blocks_e, op0=ALU.is_gt, op1=ALU.add).then_inc(S["blocks"], 1)
                dve.wait_ge(S["blocks"], MAXB + 1)
                dve.tensor_tensor_scan(ends_e, ones[:, 0:EXPERTS], blocks_e, 0.0, ALU.mult, ALU.add).then_inc(S["ends"], 1)
                dve.wait_ge(S["ends"], 1)
                dve.tensor_tensor(base_e, ends_e, blocks_e, ALU.subtract).then_inc(S["base"], 1)
                dve.wait_ge(S["base"], 1)
                for t in range(TT):
                    m = tokens(t)
                    dve.scalar_tensor_tensor(out=slot_e[0:m, t, :], in0=base_e[0:m], scalar=float(BLK), in1=bank[3][0:m, (t + 1) * EXPERTS:(t + 2) * EXPERTS],
                                             op0=ALU.mult, op1=ALU.add).then_inc(S["slot_e"], 1)
                dve.memset(slot_e[DEC:2 * DEC, TT - 1, :], 0.0).then_inc(S["slot_e"], 1)
                dve.memset(slot_e[2 * DEC:P, TT - 1, :], 0.0).then_inc(S["slot_e"], 1)
                dve.wait_ge(S["slot_e"], TT + 2)
                for k in range(TOP_K):
                    dve.tensor_tensor(pick[k], pick[k], slot_e, ALU.mult).then_inc(S["slot_k"], 1)
                    dve.wait_ge(S["slot_k"], 2 * k + 1)
                    dve.tensor_reduce(slot_f[k], pick[k], AX_X, ALU.add).then_inc(S["slot_k"], 1)
                    dve.wait_ge(S["slot_k"], 2 * k + 2)
                    dve.tensor_copy(slot_i[k][:, :], slot_f[k]).then_inc(S["slots_known"], 1)
                dve.wait_ge(S["blk_int"], 1)
                dve.tensor_copy(blk_no[0:1], blk_int[:, :]).then_inc(S["blk_no"], 1)
                dve.wait_ge(S["blk_no"], 1)
                dve.tensor_tensor(over_e[0:1], ends_e[0:1].unsqueeze(1).to_broadcast([1, NBLK, EXPERTS]),
                                  blk_no[0:1].unsqueeze(2).to_broadcast([1, NBLK, EXPERTS]), ALU.is_le).then_inc(S["over_e"], 1)
                dve.wait_ge(S["over_e"], 1)
                dve.tensor_reduce(owner_f[0:1], over_e[0:1], AX_X, ALU.add).then_inc(S["owner_f"], 1)
                dve.wait_ge(S["owner_f"], 1)
                dve.tensor_scalar(owner[:, :], owner_f[0:1], float(EXPERTS - 1), None, ALU.min).then_inc(S["owner"], 1)
                dve.wait_ge(S["g_exp"], 1)
                dve.tensor_reduce(gsum, ge, AX_X, ALU.add).then_inc(S["gsum"], 1)
                dve.wait_ge(S["e_exp"], 1)
                dve.wait_ge(S["gsum"], 1)
                dve.scalar_tensor_tensor(out=wsum, in0=e2, scalar=1.0, in1=gsum, op0=ALU.add, op1=ALU.mult).then_inc(S["wsum"], 1)
                dve.wait_ge(S["wsum"], 1)
                dve.reciprocal(w1, wsum).then_inc(S["w1"], 1)
                dve.wait_ge(S["w1"], 1)
                dve.tensor_tensor(w2, w1, e2, ALU.mult).then_inc(S["w2"], 1)

        S.end_stage()

        wroom = Room(flat[:, 0:B4 * BW], B4 * BW)
        wg, wu, wd, xr, y_b = ([wroom.take(*sh) for _ in range(2)] for sh in ((FT, DE), (FT, DE), (2, D), (D,), (D,)))
        broom = Room(flat[:, B4 * BW:], 3 * FT * BW)
        xT, hid, gate_s = ([broom.take(*sh) for _ in range(2)] for sh in ((FT, BLK), (2, BLK), (2, BLK)))
        gain_rows = broom.take(D)
        ITER = NBLK // 2

        def owner_of(sp, i, s):
            return sp.value_load(owner[0:1, bass.ds(i * 2 + s, 1)], min_val=0, max_val=EXPERTS - 1)

        def load_x(sp, i, s):
            sp.wait_ge(S[f"m_turned{s}"], i + 1)
            sp.dma_start(xr[s][0:BLK], x_slots[bass.ds(i * (2 * BLK) + s * BLK, BLK), :]).then_inc(S[f"m_x{s}_in"], 16)

        def load_gate_up(sp, i, s):
            e = owner_of(sp, i, s)
            sp.wait_ge(S[f"m_gu{s}"], i + 1)
            for dst, w in ((wg[s], I["expert_w_gate"]), (wu[s], I["expert_w_up"])):
                sp.dma_start(dst, w[0][bass.ds(e, 1)].rearrange("e (k p) n -> p (e k) n", p=P)).then_inc(S[f"m_gu{s}_in"], 16)

        def load_down(sp, i, s):
            e = owner_of(sp, i, s)
            sp.wait_ge(S[f"m_down{s}"], i + 1)
            sp.dma_start(wd[s], I["expert_w_down"][0][bass.ds(e, 1)].rearrange("e (k p) n -> p (e k) n", p=P)).then_inc(S[f"m_d{s}_in"], 16)

        def turn_x(pe, i, s):
            pe.wait_ge(S[f"m_x{s}_in"], i * 16 + 16)
            pe.wait_ge(S["m_xT"], i * 2 + (s + 1))
            for f in range(FT):
                mm = pe.transpose(ps[:, f // 4, (f % 4) * P:(f % 4) * P + BLK], xr[s][0:BLK, f * P:(f + 1) * P], ident[0:BLK, 0:BLK])
            mm.then_inc(S[f"m_turned{s}"], 1)

        def gate_up(pe, i, s):
            pe.wait_ge(S[f"m_gu{s}_in"], i * 32 + 32)
            pe.wait_ge(S["m_xT"], i * 2 + (s + 2))
            pe.wait_ge(S["m_hid"], i * 2 + (s + 1))
            for w, c in ((wg[s], 0), (wu[s], 2)):
                for o in range(2):
                    for f in range(FT):
                        mm = pe.matmul(bank[2 + s][:, (c + o) * P:(c + o) * P + BLK], w[:, f, o * P:(o + 1) * P], xT[s][:, f, :],
                                       start=(f == 0), stop=(f == FT - 1))
            mm.then_inc(S[f"m_gu{s}"], 1)

        def down(pe, i, s):
            pe.wait_ge(S[f"m_d{s}_in"], i * 16 + 16)
            pe.wait_ge(S["m_hid"], i * 2 + (s + 3))
            pe.wait_ge(S["m_y"], i * 2 + (s + 1))
            for c in range(2):
                for f in range(2):
                    mm = pe.matmul(bank[4 + 2 * s + c][0:BLK, :], hid[s][:, f, :], wd[s][:, f, c * 512:(c + 1) * 512], start=(f == 0), stop=(f == 1))
            mm.then_inc(S[f"m_down{s}"], 1)

        def cols4(s):
            return bank[2 + s].rearrange("p (c n) -> p c n", c=4)[:, :, 0:BLK]

        def keep_x(act, i, s):
            act.wait_ge(S[f"m_turned{s}"], i + 2)
            act.copy(xT[s], ps[:, 0:2, :].rearrange("p b (f n) -> p (b f) n", f=4)[:, :, 0:BLK]).then_inc(S["m_xT"], 1)

        def silu(act, i, s):
            act.wait_ge(S[f"m_gu{s}"], i + 2)
            act.activation(gate_s[s], cols4(s)[:, 0:2, :], ACT.Silu).then_inc(S[f"m_silu{s}"], 1)

        def hidden(dve, i, s):
            dve.wait_ge(S[f"m_silu{s}"], i + 1)
            dve.tensor_tensor(hid[s], gate_s[s], cols4(s)[:, 2:4, :], ALU.mult).then_inc(S["m_hid"], 1)

        def keep_y(dve, i, s):
            dve.wait_ge(S[f"m_down{s}"], i + 2)
            dve.wait_ge(S[f"m_y{s}_free"], i + 1)
            dve.tensor_copy(y_b[s][0:BLK].rearrange("p (c n) -> p c n", c=2), ps[0:BLK, 4 + 2 * s:6 + 2 * s, :]).then_inc(S["m_y"], 1)

        with nc.Block() as block:
            @block.sync
            def _(sp):
                load_x(sp, 0, 0)
                load_x(sp, 0, 1)
                load_gate_up(sp, 0, 0)
                with sp.Fori(0, ITER - 1) as i:
                    for s in range(2):
                        load_x(sp, i + 1, s)
                        load_gate_up(sp, i + s, 1 - s)
                        load_down(sp, i, s)
                load_gate_up(sp, ITER - 1, 1)
                load_down(sp, ITER - 1, 0)
                load_down(sp, ITER - 1, 1)

            @block.gpsimd
            def _(pool):
                pool.dma_start(gain_rows, I["norm_final_g"].partition_broadcast(P)).then_inc(S["slot_gain_in"], 16)
                with pool.Fori(0, ITER) as i:
                    for s in range(2):
                        pool.wait_ge(S["m_y"], i * 2 + (s + 3))
                        pool.dma_start(y_slots[bass.ds(i * (2 * BLK) + s * BLK, BLK), :], y_b[s][0:BLK]).then_inc(S[f"m_y{s}_out"], 16)
                        pool.wait_ge(S[f"m_y{s}_out"], i * 16 + 16)
                        pool.sem_inc(S[f"m_y{s}_free"], 1)

            @block.scalar
            def _(act):
                keep_x(act, 0, 0)
                keep_x(act, 0, 1)
                silu(act, 0, 0)
                with act.Fori(0, ITER - 1) as i:
                    for s in range(2):
                        keep_x(act, i + 1, s)
                        silu(act, i + s, 1 - s)
                silu(act, ITER - 1, 1)

            @block.tensor
            def _(pe):
                for name, n in (("m_xT", 1), ("m_hid", 2), ("m_y", 2), ("m_y0_free", 1), ("m_y1_free", 1), ("m_turned0", 1),
                                ("m_turned1", 1), ("m_gu0", 1), ("m_gu1", 1), ("m_down0", 1), ("m_down1", 1)):
                    pe.sem_inc(S[name], n)
                turn_x(pe, 0, 0)
                turn_x(pe, 0, 1)
                gate_up(pe, 0, 0)
                with pe.Fori(0, ITER - 1) as i:
                    for s in range(2):
                        turn_x(pe, i + 1, s)
                        gate_up(pe, i + s, 1 - s)
                        down(pe, i, s)
                gate_up(pe, ITER - 1, 1)
                down(pe, ITER - 1, 0)
                down(pe, ITER - 1, 1)

            @block.vector
            def _(dve):
                hidden(dve, 0, 0)
                with dve.Fori(0, ITER - 1) as i:
                    for s in range(2):
                        hidden(dve, i + s, 1 - s)
                        keep_y(dve, i, s)
                hidden(dve, ITER - 1, 1)
                keep_y(dve, ITER - 1, 0)
                keep_y(dve, ITER - 1, 1)

        S.end_stage()

        froom = Room(flat[:, 0:B4 * BW], B4 * BW)
        res = [[froom.take(D) for _ in range(TOP_K)] for _ in range(TT)]
        y_sq, ss, rstd = froom.take(D), froom.take(TT), froom.take(TT)

        with nc.Block() as block:
            @block.gpsimd
            def _(pool):
                for t in range(TT):
                    for k in range(TOP_K):
                        m = tokens(t)
                        pool.indirect_dma_start(res[t][k][0:m], None, y_slots, bass.IndirectOffsetOnAxis(slot_i[k][0:m, t:t + 1], 0)).then_inc(S[f"y_in{t}"], 16)

            @block.vector
            def _(dve):
                dve.wait_ge(S["slot_gain_in"], 16)
                for t in range(TT + 1):
                    if t < TT:
                        m = tokens(t)
                        dve.wait_ge(S[f"y_in{t}"], 16 * TOP_K)
                        for k, w in enumerate((w1, w2)):
                            if k:
                                dve.wait_ge(S["y_sum"], 2 * t + 1)
                            dve.scalar_tensor_tensor(out=h_tok[0:m, t, :], in0=res[t][k][0:m], scalar=w[0:m, t:t + 1], in1=h_tok[0:m, t, :],
                                                     op0=ALU.mult, op1=ALU.add).then_inc(S["y_sum"], 1)
                    if t:
                        u = t - 1
                        m = tokens(u)
                        dve.wait_ge(S["y_rms"], u + 1)
                        dve.reciprocal(rstd[0:m, u:u + 1], rstd[0:m, u:u + 1]).then_inc(S["y_rrms"], 1)
                        dve.wait_ge(S["y_rrms"], u + 1)
                        dve.scalar_tensor_tensor(out=h_tok[0:m, u, :], in0=h_tok[0:m, u, :], scalar=rstd[0:m, u:u + 1], in1=gain_rows[0:m],
                                                 op0=ALU.mult, op1=ALU.mult).then_inc(S["y_done"], 1)

            @block.scalar
            def _(act):
                for t in range(TT):
                    m = tokens(t)
                    act.wait_ge(S["y_sum"], 2 * t + 2)
                    act.activation(y_sq[0:m], h_tok[0:m, t, :], ACT.Square, accum_out=ss[0:m, t:t + 1]).then_inc(S["y_ss"], 1)
                    act.wait_ge(S["y_ss"], t + 1)
                    act.activation(rstd[0:m, t:t + 1], ss[0:m, t:t + 1], ACT.Sqrt, bias=eps_c[0:m], scale=1.0 / D).then_inc(S["y_rms"], 1)

            @block.sync
            def _(sp):
                for t in range(TT):
                    sp.wait_ge(S["y_done"], t + 1)
                    dst = O["y_prompt"][0, t * P:(t + 1) * P, :] if t < TT - 1 else O["y_sample"][0]
                    sp.dma_start(dst, h_tok[0:tokens(t), t, :]).then_inc(S["y_out"], 16)
                sp.wait_ge(S["y_out"], 16 * TT)


_INS = ["x_prompt", "x_sample", "mem_prompt", "cache_mem_k", "cache_mem_v", "state_hgrn", "state_rwkv", "state_rwkv_shift",
        "norm_mix_g", "w_in", "hgrn_lower_bounds", "hgrn_norm_g", "rwkv_mu", "rwkv_w0", "rwkv_w2", "rwkv_a0", "rwkv_a2",
        "rwkv_g2", "rwkv_k_k", "rwkv_k_a", "rwkv_r_k", "rwkv_ln_g", "rwkv_ln_b", "w_out", "norm_x_g", "norm_mem_g",
        "wq_x", "wk_x", "wv_x", "wo_x", "norm_ffn_g", "router_group_w", "router_group_b", "router_expert_w",
        "router_expert_b", "expert_w_gate", "expert_w_up", "expert_w_down", "norm_final_g"]
_OUTS = [("y_prompt", (1, SEQ, D)), ("y_sample", (1, DEC, D)),
         ("mem_k", (1, 1, MEM, XH, D // XH)), ("mem_v", (1, 1, MEM, XH, D // XH)),
         ("hgrn_prompt", (1, 1, HEADS, P, P)), ("hgrn_sample", (1, 1, HEADS, P, P)),
         ("rwkv_prompt", (1, 1, 16, 64, 64)), ("rwkv_sample", (1, 1, 16, 64, 64)),
         ("shift_prompt", (1, 1, 1, N_RWKV)), ("shift_sample", (1, 1, 1, N_RWKV))]


def kernel(**inputs):
    import numpy as _np
    import concourse.bacc as _bacc
    from concourse.bass_utils import run_bass_kernel_spmd as _run

    nc = _bacc.Bacc("TRN2", target_bir_lowering=False, num_devices=1)
    arrays, ins, outs = {}, {}, {}
    for name in _INS:
        a = _np.ascontiguousarray(inputs[name])
        arrays[f"in_{name}"] = a
        ins[name] = nc.dram_tensor(f"in_{name}", a.shape, F32, kind="ExternalInput").ap()
    for name, shape in _OUTS:
        outs[name] = nc.dram_tensor(f"out_{name}", shape, F32, kind="ExternalOutput").ap()
    build(nc, ins, outs)
    r = _run(nc, [arrays], core_ids=[0])
    return tuple(r.results[0][f"out_{name}"] for name, _ in _OUTS)
```

```python
from contextlib import ExitStack

import concourse.bass as bass
from concourse import mybir

F32 = mybir.dt.float32
F32R = mybir.dt.float32r
ALU = mybir.AluOpType
ACT = mybir.ActivationFunctionType
AX_X = mybir.AxisListType.X

P = 128
D = 1024
FT = D // P
SEQ = 512
DEC = 32
N = SEQ + DEC
HALF = N // 2
CH = 64
NCH = SEQ // CH
BW = 1 + (NCH + 1) * CH + 1
HEADS = 8
DECAY_L, ICL_L, GATE_L = 64, 64, 160
LORA = DECAY_L + ICL_L + GATE_L
N_RWKV = 3 * D + LORA
COL_RWKV = 4 * D
COL_GATES = COL_RWKV + N_RWKV
MEM = 256
XH = 4
XSCALE = (D // XH) ** -0.5
GROUPS, PER_GROUP = 4, 8
EXPERTS = GROUPS * PER_GROUP
DE = 256
EPS = 1e-6
GN_EPS = 64e-5
UNIT = 256
TT = 5
BLK = 96
TOP_K = 2
NBLK = -(-((TOP_K * N - EXPERTS) // BLK + EXPERTS) // 2) * 2
NSLOT = NBLK * BLK
MAXB = -(-N // BLK)
U32 = mybir.dt.uint32
I32 = mybir.dt.int32
DECAY = 0.6065306597126334
LN2 = 0.6931471805599453

H, XN, B2, B3, B4, B5, B6 = (FT * i for i in range(7))


class Sems:

    def __init__(self, nc):
        self.nc, self.by_name, self.kept, self.stage = nc, {}, {}, 1

    def __getitem__(self, name):
        where = self.kept if name.startswith(("slot", "banks")) else self.by_name
        if name not in where:
            where[name] = self.nc.alloc_semaphore(name if where is self.kept else f"{name}_{self.stage}")
        return where[name]

    def end_stage(self):
        self.nc.clear_and_free_semaphores(list(self.by_name.values()))
        self.nc.all_engine_barrier()
        self.by_name = {}
        self.stage += 1


def shaped(flat, base, shape):
    n = 1
    for s in shape:
        n *= s
    v = flat[:, base:base + n]
    if len(shape) == 2:
        v = v.rearrange("p (a b) -> p a b", a=shape[0])
    if len(shape) == 3:
        v = v.rearrange("p (a b c) -> p a b c", a=shape[0], b=shape[1])
    return v


class Room:

    def __init__(self, flat, n):
        self.flat, self.n, self.at = flat, n, 0

    def take(self, *shape):
        v = shaped(self.flat, self.at, shape)
        n = 1
        for s in shape:
            n *= s
        self.at += n
        assert self.at <= self.n, (self.at, self.n)
        return v


SCR = 12800


def build(nc, I, O):
    with ExitStack() as ctx:
        def sb(name, shape):
            return ctx.enter_context(nc.sbuf_tensor(name, shape, F32))

        S = Sems(nc)
        x_slots = nc.dram_tensor("x_slots", (NSLOT, D), F32, kind="Internal").ap()
        y_slots = nc.dram_tensor("y_slots", (NSLOT, D), F32, kind="Internal").ap()
        h_kept = nc.dram_tensor("h_kept", (P, FT * BW), F32, kind="Internal").ap()
        arena = sb("arena", [P, 7 * FT, BW])
        arena_at = nc.sbuf_base - 7 * FT * BW * 4

        def rounded(name, at, *shape):
            return nc.alloc_sbuf_tensor_at(name, [P, *shape], F32R, offset=at)

        flat = arena[:, :, :].rearrange("p f n -> p (f n)")
        ring = sb("ring", [P, 2, FT, UNIT])
        ring_flat = ring[:, :, :, :].rearrange("p s k n -> p (s k n)")
        lora = sb("lora", [P, 3, BW])
        ident = sb("ident", [P, P])
        ones = sb("ones", [P, P])
        head_ones = sb("head_ones", [P, P])
        rows_a = sb("rows_a", [P, P])
        rows_b = sb("rows_b", [P, P])
        ca = sb("ca", [P, P])
        cb = sb("cb", [P, P])
        lbs = sb("lbs", [P, 2, FT])
        tiny = sb("tiny", [P, 4])
        scale_row = sb("scale_row", [P, BW])
        scr = sb("scr", [P, SCR])
        scr_at = nc.sbuf_base - SCR * 4
        ps = ctx.enter_context(nc.psum_tensor("ps", [P, 8, 512], F32))
        bank = [ps[:, b, :] for b in range(8)]
        eps_c, gn_eps_c, kk_c = tiny[:, 0:1], tiny[:, 1:2], tiny[:, 2:3]

        VEC = ["norm_mix_g", "rwkv_w0", "rwkv_a0", "rwkv_k_k", "rwkv_k_a", "rwkv_r_k", "rwkv_ln_g", "rwkv_ln_b",
               "norm_x_g", "norm_mem_g", "norm_ffn_g", "norm_final_g", "lb0", "lb1"]
        NV = len(VEC) * FT

        def col(name, f=None):
            k = VEC.index(name) * FT
            return ca[:, k:k + FT] if f is None else ca[:, k + f:k + f + 1]

        MU, HG, SHIFT, NSH = 0, 27, 28, 27

        def frames(base, a, n, f0=0, f1=FT):
            return arena[:, base + f0:base + f1, bass.ds(a + 1, n)]

        def whole(base):
            return arena[:, base:base + FT, 1:1 + N]

        def over(c, n):
            return c.unsqueeze(2).to_broadcast([P, c.shape[1], n])

        def split_heads(b):
            return b.rearrange("p (a n) -> p a n", a=8)

        def norm_stage(k, src, dst, gain, n, sq):
            parts = [(0, n)] if n <= 512 else [(0, n // 2), (n // 2, n)]
            rs = scale_row[:, 0:n]

            def on_act(act):
                for f in range(FT):
                    act.activation(sq[:, f, :], src[:, f, :], ACT.Square).then_inc(S[k + "_squares"], 1)
                act.wait_ge(S[k + "_sums"], 1)
                for h, (a, b) in enumerate(parts):
                    act.activation(rs[:, a:b], ps[:, h, 0:b - a], ACT.Sqrt, bias=eps_c, scale=1.0 / D).then_inc(S[k + "_rms"], 1)

            def on_pe(pe):
                for f in range(FT):
                    pe.wait_ge(S[k + "_squares"], f + 1)
                    for h, (a, b) in enumerate(parts):
                        mm = pe.matmul(ps[:, h, 0:b - a], ones[:, :], sq[:, f, a:b], start=(f == 0), stop=(f == FT - 1))
                mm.then_inc(S[k + "_sums"], 1)

            def on_dve(dve):
                dve.wait_ge(S[k + "_rms"], len(parts))
                dve.reciprocal(rs, rs).then_inc(S[k + "_rrms"], 1)
                dve.wait_ge(S[k + "_rrms"], 1)
                for f in range(FT):
                    dve.scalar_tensor_tensor(out=dst[:, f, :], in0=src[:, f, :], scalar=gain(f), in1=rs,
                                             op0=ALU.mult, op1=ALU.mult).then_inc(S[k + "_normed"], 1)

            return on_act, on_pe, on_dve

        used = [0]

        def linear(jobs):
            spans = []
            for job in jobs:
                spans.append((used[0], job))
                used[0] += job[3] // 2

            def on_sp(sp):
                for b0, (kind, w, c0, units, x, dst) in spans:
                    wv = w.rearrange("(k p) n -> p k n", p=P)
                    with sp.Fori(0, units // 2) as i:
                        n = sp.snap(i + (b0 + 1))
                        for s in range(2):
                            sp.wait_ge(S[f"slot{s}_free"], n)
                            sp.dma_start(ring[:, s], wv[:, :, bass.ds(i * (2 * UNIT) + (c0 + s * UNIT), UNIT)]).then_inc(S[f"slot{s}_loaded"], 16)

            def on_pe(pe):
                for b0, (kind, w, c0, units, x, dst) in spans:
                    with pe.Fori(0, units // 2) as i:
                        n = pe.snap(i + (b0 + 1))
                        n16 = pe.snap(i * 16 + (b0 + 1) * 16)
                        for s in range(2):
                            pe.wait_ge(S[f"banks{s}_free"], n)
                            pe.wait_ge(S[f"slot{s}_loaded"], n16)
                            if kind == "rows":
                                for h in range(MEM // P):
                                    for k in range(FT):
                                        mm = pe.matmul(ps[:, 4 * s + h, 0:UNIT], x[:, k, h * P:(h + 1) * P], ring[:, s, k, :],
                                                       start=(k == 0), stop=(k == FT - 1))
                            else:
                                for o in range(UNIT // P):
                                    for h in range(2):
                                        for k in range(FT):
                                            mm = pe.matmul(ps[:, 4 * s + 2 * o + h, 0:HALF], ring[:, s, k, o * P:(o + 1) * P],
                                                           arena[:, x + k, 1 + h * HALF:1 + (h + 1) * HALF],
                                                           start=(k == 0), stop=(k == FT - 1))
                            mm.then_inc(S[f"slot{s}_free"], 1)

            def leave(eng, on_dve):
                for b0, (kind, w, c0, units, x, dst) in spans:
                    if (kind == "add") != on_dve:
                        continue
                    with eng.Fori(0, units // 2) as i:
                        n = eng.snap(i + (b0 + 2))
                        for s in range(2):
                            eng.wait_ge(S[f"slot{s}_free"], n)
                            if kind == "rows":
                                last = eng.copy(dst[:, :, bass.ds(i * (2 * UNIT) + s * UNIT, UNIT)], ps[:, 4 * s:4 * s + 2, 0:UNIT])
                            else:
                                for o in range(UNIT // P):
                                    src = ps[:, 4 * s + 2 * o:4 * s + 2 * o + 2, 0:HALF]
                                    to = arena[:, bass.ds(i * 4 + (dst + 2 * s + o), 1), 1:1 + N].rearrange("p o (h n) -> p (o h) n", h=2)
                                    if kind == "keep":
                                        last = eng.copy(to, src)
                                    else:
                                        last = eng.tensor_tensor(to, to, src, ALU.add)
                            last.then_inc(S[f"banks{s}_free"], 1)

            return on_sp, on_pe, leave

        rounded_x = {x: rounded(f"rounded_{x}", arena_at + x * BW * 4, FT, BW) for x in (H, XN)}

        class Split:

            def __init__(self, name, jobs, x_hi, x_lo, parts_at):
                self.jobs, self.in_x = jobs, x_lo
                self.x_hi, self.x_lo = rounded_x[x_hi], rounded_x[x_lo]
                self.hi, self.lo = ([rounded(f"{name}_{part}{j}", scr_at + 4 * (parts_at + (2 * k + j) * FT * UNIT), FT, UNIT)[:, :, :]
                                     for j in range(2)] for k, part in enumerate(("hi", "lo")))
                self.total = sum(job[3] for job in jobs) // 2

            def spans(self):
                b0 = 0
                for job in self.jobs:
                    yield b0, job
                    b0 += job[3] // 2

            def wait_all_kept(self, eng):
                for j in range(2):
                    eng.wait_ge(S[f"w{j}_kept"], self.total + 1)

            def on_sp(self, sp):
                for b0, (kind, w, c0, units, dst) in self.spans():
                    wv = w.rearrange("(k p) n -> p k n", p=P)
                    with sp.Fori(0, units // 2) as i:
                        n = sp.snap(i + (b0 + 1))
                        for j in range(2):
                            sp.wait_ge(S[f"w{j}_lo"], n)
                            sp.dma_start(ring[:, j], wv[:, :, bass.ds(i * (2 * UNIT) + (c0 + j * UNIT), UNIT)]).then_inc(S[f"w{j}_loaded"], 16)

            def start_pe(self, pe):
                for j in range(2):
                    for name in ("lo", "used", "kept"):
                        pe.sem_inc(S[f"w{j}_{name}"], 1)

            def products(self, pe, out, hi, lo, h):
                for k in range(FT):
                    xh, xl = (x[:, k, 1 + h * HALF:1 + (h + 1) * HALF] for x in (self.x_hi, self.x_lo))
                    pe.matmul(out, hi[:, k], xh, start=(k == 0), stop=False)
                    pe.matmul(out, hi[:, k], xl, start=False, stop=False)
                    mm = pe.matmul(out, lo[:, k], xh, start=False, stop=(k == FT - 1))
                return mm

            def on_pe(self, pe):
                for b0, (kind, w, c0, units, dst) in self.spans():
                    with pe.Fori(0, units // 2) as i:
                        n, n2 = pe.snap(i + (b0 + 1)), pe.snap(i + (b0 + 2))
                        for j in range(2):
                            pe.wait_ge(S[f"w{j}_kept"], n)
                            pe.wait_ge(S[f"w{j}_lo"], n2)
                            for o in range(UNIT // P):
                                for h in range(2):
                                    mm = self.products(pe, ps[:, 4 * j + 2 * o + h, 0:HALF], self.hi[j][:, :, o * P:(o + 1) * P],
                                                       self.lo[j][:, :, o * P:(o + 1) * P], h)
                            mm.then_inc(S[f"w{j}_used"], 1)

            def make_hi(self, act, j, n):
                act.wait_ge(S[f"w{j}_used"], n)
                act.wait_ge(S[f"w{j}_loaded"], n * 16)
                act.copy(self.hi[j], ring[:, j]).then_inc(S[f"w{j}_hi"], 1)

            def make_lo(self, dve, j, n):
                dve.wait_ge(S[f"w{j}_hi"], n)
                dve.tensor_tensor(self.lo[j], ring[:, j], self.hi[j].bitcast(F32), ALU.subtract).then_inc(S[f"w{j}_lo"], 1)

            def leave(self, eng, kind, dst, i, j, n):
                eng.wait_ge(S[f"w{j}_used"], n)
                for o in range(UNIT // P):
                    src = ps[:, 4 * j + 2 * o:4 * j + 2 * o + 2, 0:HALF]
                    to = arena[:, bass.ds(i * 4 + (dst + 2 * j + o), 1), 1:1 + N].rearrange("p o (h n) -> p (o h) n", h=2)
                    last = eng.tensor_tensor(to, to, src, ALU.add) if kind == "add" else eng.activation(to, src, kind)
                last.then_inc(S[f"w{j}_kept"], 1)

            def on_parts(self, eng, make, leaves):
                make(eng, 0, 1)
                for b0, (kind, w, c0, units, dst) in self.spans():
                    def step(i, n, n2, more):
                        for j in range(2):
                            if j == 0 or more:
                                make(eng, 1 - j, n if j == 0 else n2)
                            if (kind == "add") == (leaves == "add"):
                                self.leave(eng, kind, dst, i, j, n2)

                    final = b0 + units // 2 == self.total
                    with eng.Fori(0, units // 2 - final) as i:
                        step(i, eng.snap(i + (b0 + 1)), eng.snap(i + (b0 + 2)), True)
                    if final:
                        step(units // 2 - 1, self.total, self.total + 1, False)

            def on_act(self, act):
                self.on_parts(act, self.make_hi, "kept")

            def on_dve(self, dve):
                self.on_parts(dve, self.make_lo, "add")

            def split_x_act(self, act, ready):
                for f in range(FT):
                    act.wait_ge(S[ready], f + 1)
                    act.copy(self.x_hi[:, f, 1:1 + N], arena[:, self.in_x + f, 1:1 + N]).then_inc(S["x_hi"], 1)

            def split_x_dve(self, dve):
                for f in range(FT):
                    dve.wait_ge(S["x_hi"], f + 1)
                    hi, x = self.x_hi[:, f, 1:1 + N].bitcast(F32), arena[:, self.in_x + f, 1:1 + N]
                    dve.tensor_tensor(self.x_lo[:, f, 1:1 + N], x, hi, ALU.subtract).then_inc(S["x_lo"], 1)

        x_tok = shaped(flat, B2 * BW, (TT, D))
        x_groups = []
        for t in range(TT):
            n = P if t < TT - 1 else DEC
            for f0 in (0, 4):
                x_groups.append((x_tok[0:n, t, :], n, f0, arena[:, H + f0:H + f0 + 4, 1 + t * P:1 + t * P + n]))

        with nc.Block() as block:
            @block.sync
            def _(sp):
                sp.dma_start(x_tok[:, 0:4, :], I["x_prompt"][0].rearrange("(t p) d -> p t d", p=P)).then_inc(S["x_in"], 16)
                sp.dma_start(x_tok[0:DEC, 4, :], I["x_sample"][0]).then_inc(S["x_in"], 16)

            @block.scalar
            def _(act):
                for s in range(2):
                    act.sem_inc(S[f"banks{s}_free"], 1)
                for v, name in enumerate(VEC):
                    if name == "rwkv_r_k":
                        src = I[name][0].rearrange("(f a) b -> f (a b)", f=FT)
                    elif name == "norm_final_g":
                        src = I[name].rearrange("(f p) -> f p", f=FT)
                    elif name in ("lb0", "lb1"):
                        src = I["hgrn_lower_bounds"][int(name[2])].rearrange("(f p) -> f p", f=FT)
                    else:
                        src = I[name][0].rearrange("(f p) -> f p", f=FT)
                    act.dma_start(rows_a[v * FT:(v + 1) * FT, :], src).then_inc(S["rows_a_in"], 16)
                act.wait_ge(S["rows_b_cleared"], 1)
                full = N_RWKV // P
                rest = N_RWKV - full * P
                for base, src in ((MU, I["rwkv_mu"][0]), (SHIFT, I["state_rwkv_shift"][0, 0, 0])):
                    act.dma_start(rows_b[base:base + full, :], src[0:full * P].rearrange("(f p) -> f p", p=P)).then_inc(S["rows_b_in"], 16)
                    act.dma_start(rows_b[base + full:base + full + 1, 0:rest], src[full * P:N_RWKV].unsqueeze(0)).then_inc(S["rows_b_in"], 16)
                act.dma_start(rows_b[HG:HG + 1, :], I["hgrn_norm_g"]).then_inc(S["rows_b_in"], 16)
                for i, (src, n, f0, dst) in enumerate(x_groups):
                    if i % 2:
                        act.wait_ge(S["x_turned"], i + 1)
                        act.copy(dst, ps[:, i % 8, :].rearrange("p (f n) -> p f n", f=4)[:, :, 0:n]).then_inc(S["x_kept_odd"], 1)

            @block.gpsimd
            def _(pool):
                pool.memset(rows_b[:, :], 0.0).then_inc(S["rows_b_cleared"], 1)
                pool.memset(ident[:, :], 0.0).then_inc(S["ident_zero"], 1)
                pool.memset(ones[:, :], 1.0).then_inc(S["consts"], 1)
                pool.memset(eps_c, EPS).then_inc(S["consts"], 1)
                pool.memset(gn_eps_c, GN_EPS).then_inc(S["consts"], 1)
                pool.memset(kk_c, 15.0 * LN2).then_inc(S["consts"], 1)
                pool.wait_ge(S["ident_zero"], 1)
                pool.affine_select(out=ident[:, :], in_=ident[:, :], compare_op=ALU.not_equal, fill=1.0, base=0,
                                   pattern=[[-1, P]], channel_multiplier=1).then_inc(S["ident_ready"], 1)

            @block.tensor
            def _(pe):
                for s in range(2):
                    pe.sem_inc(S[f"slot{s}_free"], 1)
                pe.wait_ge(S["ident_ready"], 1)
                pe.wait_ge(S["x_in"], 32)
                for i, (src, n, f0, dst) in enumerate(x_groups):
                    if i >= 8:
                        pe.wait_ge(S["x_kept_odd" if i % 2 else "x_kept_even"], (i - 8) // 2 + 1)
                    for f in range(4):
                        mm = pe.transpose(ps[:, i % 8, f * P:f * P + n], src[:, (f0 + f) * P:(f0 + f + 1) * P], ident[0:n, 0:n])
                    mm.then_inc(S["x_turned"], 1)
                pe.wait_ge(S["x_kept_odd"], 2)
                pe.wait_ge(S["rows_a_in"], 16 * len(VEC))
                pe.transpose(ps[:, 3, 0:NV], rows_a[0:NV, :], ident[0:NV, 0:NV]).then_inc(S["vectors_turned"], 1)
                pe.wait_ge(S["rows_b_in"], 80)
                pe.wait_ge(S["x_kept_even"], 3)
                pe.transpose(ps[:, 4, 0:P], rows_b[:, :], ident[:, :]).then_inc(S["vectors_turned"], 1)

            @block.vector
            def _(dve):
                dve.memset(arena[:, 0:B2, 1 + N:BW], 0.0).then_inc(S["pads"], 1)
                dve.memset(arena[:, 0:B2, 0:1], 0.0).then_inc(S["pads"], 1)
                dve.memset(lora[:, :, :], 0.0).then_inc(S["pads"], 1)
                dve.memset(head_ones[:, :], 0.0).then_inc(S["head_zero"], 1)
                dve.wait_ge(S["head_zero"], 1)
                dve.memset(head_ones[0:64, 0:64], 1.0).then_inc(S["consts"], 1)
                dve.memset(head_ones[64:128, 64:128], 1.0).then_inc(S["consts"], 1)
                for i, (src, n, f0, dst) in enumerate(x_groups):
                    if i % 2 == 0:
                        dve.wait_ge(S["x_turned"], i + 1)
                        dve.tensor_copy(dst, ps[:, i % 8, :].rearrange("p (f n) -> p f n", f=4)[:, :, 0:n]).then_inc(S["x_kept_even"], 1)
                dve.wait_ge(S["vectors_turned"], 1)
                dve.tensor_copy(ca[:, 0:NV], ps[:, 3, 0:NV]).then_inc(S["vectors"], 1)
                dve.wait_ge(S["vectors_turned"], 2)
                dve.tensor_copy(cb[:, :], ps[:, 4, 0:P]).then_inc(S["vectors"], 1)

        S.end_stage()

        w_in = I["w_in"][0]
        sq_all = shaped(scr[:, :], 0, (FT, N))
        n_act, n_pe, n_dve = norm_stage("mix", whole(H), whole(XN), lambda f: col("norm_mix_g", f), N, sq_all)
        lin = Split("mix", [(ACT.Silu, w_in, 0, 4, B2), (ACT.Sigmoid, w_in, D, 4, B3), (ACT.Copy, w_in, 2 * D, 4, B4),
                             (ACT.Sigmoid, w_in, COL_GATES, 4, B6), (ACT.Silu, w_in, 3 * D, 4, B5)], H, XN, FT * N)
        lb, one_m_lb = lbs[:, 0, :], lbs[:, 1, :]
        zeros = lora[:, :, :].rearrange("p t n -> p (t n)")[:, 0:1536]

        with nc.Block() as block:
            @block.gpsimd
            def _(pool):
                pool.dma_start(h_kept, flat[:, H * BW:(H + FT) * BW]).then_inc(S["h_spilled"], 16)

            @block.sync
            def _(sp):
                lin.on_sp(sp)

            @block.scalar
            def _(act):
                n_act(act)
                act.wait_ge(S["lb_diff"], 1)
                act.activation(lb, lb, ACT.Sigmoid).then_inc(S["lb_ready"], 1)
                act.wait_ge(S["h_spilled"], 16)
                lin.split_x_act(act, "mix_normed")
                lin.on_act(act)
            @block.tensor
            def _(pe):
                lin.start_pe(pe)
                n_pe(pe)
                pe.wait_ge(S["x_lo"], FT)
                pe.wait_ge(S["mix_rms"], 2)
                lin.on_pe(pe)

            @block.vector
            def _(dve):
                dve.tensor_tensor(lb, col("lb0"), col("lb1"), ALU.subtract).then_inc(S["lb_diff"], 1)
                n_dve(dve)
                lin.split_x_dve(dve)
                dve.wait_ge(S["lb_ready"], 1)
                dve.tensor_scalar(one_m_lb, lb, -1.0, 1.0, ALU.mult, ALU.add).then_inc(S["lb_ready"], 1)
                lin.on_dve(dve)
                dve.memset(arena[:, B2:B6 + FT, 1 + N:BW], 0.0).then_inc(S["pads2"], 1)
                dve.memset(arena[:, B2:B6 + FT, 0:1], 0.0).then_inc(S["pads2"], 1)
                dve.wait_ge(S["lb_ready"], 2)
                dve.wait_ge(S["pads2"], 2)
                for f in range(FT):
                    t = arena[:, B3 + f, 1:1 + N]
                    dve.tensor_scalar(t, t, one_m_lb[:, f:f + 1], lb[:, f:f + 1], ALU.mult, ALU.add).then_inc(S["f_ready"], 1)
                dve.memset(arena[:, B3:B3 + FT, 1 + N:BW], 1.0).then_inc(S["f_ready"], 1)
                lin.wait_all_kept(dve)
                dve.scalar_tensor_tensor(out=whole(B5), in0=whole(B6), scalar=cb[:, HG:HG + 1], in1=whole(B5), op0=ALU.mult, op1=ALU.mult).then_inc(S["gates"], 1)

        S.end_stage()

        room = Room(scr[:, :], SCR)
        k_s, eb, enb, q16, kinv, kh16, q32, kh32, v_s = (room.take(FT, CH) for _ in range(9))
        e32 = room.take(FT, 2)
        sc = room.take(2, 4, CH)
        k_tok, v_tok = room.take(4, P), room.take(4, P)
        state = room.take(HEADS, P)
        h_sq, h_rs = arena[:, B3:B3 + FT, 1:1 + N], arena[:, B4:B4 + FT, 1:1 + N]
        h_out = ps[:, 6:8, 0:4 * CH].rearrange("p q (a t) -> p q a t", a=4)

        def by_parity(v):
            return v.rearrange("p (a q) t -> p q a t", q=2)

        h_mask = room.take(2, 4, CH)
        h_scan = room.take((NCH + 1) * CH)

        def padded(base, f):
            return arena[:, base + f, 1:1 + (NCH + 1) * CH]


        def flat2(v):
            return v.rearrange("p a b -> p (a b)")

        def blocks(v):
            return flat2(v).rearrange("p (m e l) -> p m e l", e=2, l=16)

        def block_end(v):
            return blocks(v)[:, :, :, 15:16]

        def counts(eng, c):
            if isinstance(c, int):
                return c + 1, c + 2
            return eng.snap(c + 1), eng.snap(c + 2)

        def hgrn_act(act, c, cur, nxt):
            n, m = counts(act, c)
            if nxt:
                if cur:
                    act.wait_ge(S["h_q32"], n)
                    act.wait_ge(S["h_e32"], n)
                b_next = frames(B6, (c + 1) * CH, CH)
                act.activation(eb, b_next, ACT.Exp).then_inc(S["h_eb"], 1)
                act.activation(enb, b_next, ACT.Exp, scale=-1.0).then_inc(S["h_enb"], 1)
                if cur:
                    act.wait_ge(S["h_v_turned"], n)
                act.copy(v_s, frames(B4, (c + 1) * CH, CH)).then_inc(S["h_v"], 1)
            if cur:
                act.wait_ge(S["h_o"], n)
                act.copy(by_parity(frames(B2, c * CH, CH)), h_out).then_inc(S["h_o_kept"], 1)
            if nxt:
                if cur:
                    act.wait_ge(S["h_ds1"], n)
                act.wait_ge(S["h_v_turned"], m)
                act.copy(v_tok, bank[2].rearrange("p (a b) -> p a b", a=4)).then_inc(S["h_v_tok"], 1)
                act.wait_ge(S["h_k_turned"], m)
                act.copy(k_tok, bank[1].rearrange("p (a b) -> p a b", a=4)).then_inc(S["h_k_tok"], 1)

        def hgrn_dve(dve, c, cur, nxt):
            n, m = counts(dve, c)
            if cur:
                dve.tensor_tensor(blocks(q32)[:, :, 1, :], blocks(q16)[:, :, 1, :], block_end(eb)[:, :, 0, :].to_broadcast([P, 16, 16]), ALU.mult)
                dve.tensor_copy(blocks(q32)[:, :, 0, :], blocks(q16)[:, :, 0, :]).then_inc(S["h_q32"], 1)
                dve.wait_ge(S["h_state1"], n)
                dve.tensor_tensor(flat2(e32).rearrange("p (m o) -> p m o", o=1), block_end(eb)[:, :, 0, :], block_end(eb)[:, :, 1, :], ALU.mult).then_inc(S["h_e32"], 1)
                dve.wait_ge(S["h_scores"], n)
                dve.tensor_tensor(sc, bank[0].rearrange("p (e a b) -> p e a b", e=2, a=4), h_mask, ALU.mult).then_inc(S["h_masked"], 1)
            if nxt:
                dve.tensor_scalar(k_s, frames(B3, (c + 1) * CH, CH), -1.0, 1.0, ALU.mult, ALU.add).then_inc(S["h_k"], 1)
                if cur:
                    dve.wait_ge(S["h_q32"], n)
                dve.wait_ge(S["h_eb"], m)
                dve.tensor_tensor(q16, frames(B2, (c + 1) * CH, CH), eb, ALU.mult).then_inc(S["h_q16"], 1)
                dve.wait_ge(S["h_enb"], m)
                dve.wait_ge(S["h_k"], m)
                dve.tensor_tensor(kinv, k_s, enb, ALU.mult).then_inc(S["h_kinv"], 1)
                dve.wait_ge(S["h_kinv"], m)
                dve.tensor_tensor(blocks(kh16), blocks(kinv), block_end(eb).to_broadcast([P, 16, 2, 16]), ALU.mult).then_inc(S["h_kh16"], 1)
                if cur:
                    dve.wait_ge(S["h_k_turned"], n)
                dve.wait_ge(S["h_kh16"], m)
                dve.tensor_tensor(blocks(kh32)[:, :, 0, :], blocks(kh16)[:, :, 0, :], block_end(eb)[:, :, 1, :].to_broadcast([P, 16, 16]), ALU.mult)
                dve.tensor_copy(blocks(kh32)[:, :, 1, :], blocks(kh16)[:, :, 1, :]).then_inc(S["h_kh32"], 1)
                dve.wait_ge(S["h_q16"], m)
            if cur:
                dve.wait_ge(S["h_e32"], n)
                for k in range(2):
                    dve.wait_ge(S[f"h_ds{k}"], n)
                    for h in range(HEADS):
                        up = dve.scalar_tensor_tensor(out=state[:, h, :], in0=state[:, h, :], scalar=e32[:, h, k:k + 1],
                                                      in1=ps[:, 4 + h % 2, (h // 2) * P:(h // 2 + 1) * P], op0=ALU.mult, op1=ALU.add)
                    up.then_inc(S[f"h_state{k}"], 1)

        def hgrn_pe(pe, c, cur, nxt):
            n, m = counts(pe, c)

            def half(h):
                return slice(64 * (h % 2), 64 * (h % 2) + 64)

            def state_half(k):
                for h in range(HEADS):
                    at = (h // 2) * CH + 32 * k
                    mm = pe.matmul(bank[6 + h % 2][:, at:at + 32], state[:, h, :], q32[:, h, 32 * k:32 * k + 32],
                                   start=False, stop=(k == 1 and h >= HEADS - 2), skip_group_check=True)
                if k:
                    mm.then_inc(S["h_o"], 1)
                for h in range(HEADS):
                    part = slice(64 * (h % 2) + 32 * k, 64 * (h % 2) + 32 * k + 32)
                    mm = pe.matmul(ps[:, 4 + h % 2, (h // 2) * P:(h // 2 + 1) * P], k_tok[part, h // 2, :], v_tok[part, h // 2, :],
                                   start=True, stop=True)
                mm.then_inc(S[f"h_ds{k}"], 1)

            if nxt:
                pe.wait_ge(S["h_v"], m)
                if cur:
                    pe.wait_ge(S["h_v_tok"], n)
                for h in range(HEADS):
                    mm = pe.matmul(bank[2][half(h), (h // 2) * P:(h // 2 + 1) * P], v_s[:, h, :], ident[:, :], start=True, stop=True)
                mm.then_inc(S["h_v_turned"], 1)
            if cur:
                pe.wait_ge(S["h_ready"], 1)
                pe.wait_ge(S["h_q32"], n)
                pe.wait_ge(S["h_masked"], n)
                pe.wait_ge(S["h_k_tok"], n)
                pe.wait_ge(S["h_o_kept"], n)
                pe.wait_ge(S["h_state1"], n)
                for h in range(HEADS):
                    for e in range(2):
                        pe.matmul(bank[6 + h % 2][:, (h // 2) * CH:(h // 2 + 1) * CH], v_tok[half(h), h // 2, :], sc[half(h), e, h // 2, :],
                                  start=(h < 2 and e == 0), stop=False, skip_group_check=True)
                state_half(0)
                pe.wait_ge(S["h_state0"], n)
                state_half(1)
            if nxt:
                pe.wait_ge(S["h_kinv"], m)
                pe.wait_ge(S["h_q16"], m)
                for h in range(HEADS):
                    pe.matmul(bank[0][half(h), (h // 2) * CH:(h // 2 + 1) * CH], kinv[:, h, :], q16[:, h, :], start=True, stop=True)
                pe.wait_ge(S["h_kh16"], m)
                for h in range(HEADS):
                    mm = pe.matmul(bank[0][half(h), 256 + (h // 2) * CH:256 + (h // 2 + 1) * CH], kh16[:, h, :], q16[:, h, :], start=True, stop=True)
                mm.then_inc(S["h_scores"], 1)
                pe.wait_ge(S["h_kh32"], m)
                for h in range(HEADS):
                    mm = pe.matmul(bank[1][half(h), (h // 2) * P:(h // 2 + 1) * P], kh32[:, h, :], ident[:, :], start=True, stop=True)
                mm.then_inc(S["h_k_turned"], 1)

        with nc.Block() as block:
            @block.gpsimd
            def _(pool):
                pool.memset(h_mask[:, :, :, :], 1.0).then_inc(S["h_mask_ones"], 1)
                pool.memset(h_scan, 1.0).then_inc(S["h_scan_ones"], 1)
                pool.memset(state[:, :, :], 0.0).then_inc(S["h_state_zero"], 1)
                pool.wait_ge(S["h_scan_ones"], 1)
                pool.memset(h_scan.rearrange("p (m l) -> p m l", l=16)[:, :, 0:1], 0.0).then_inc(S["h_masks"], 1)
                pool.wait_ge(S["h_mask_ones"], 1)
                pool.wait_ge(S["h_masks"], 1)
                k = 0
                for q in range(2):
                    r = slice(64 * q, 64 * q + 64)
                    a = h_mask[r, 0, :, :].rearrange("p a (b l) -> p a b l", l=16)
                    z = h_mask[r, 1, :, :].rearrange("p a (b e l) -> p a b e l", e=2, l=16)
                    pool.memset(z[:, :, :, 0, :], 0.0).then_inc(S["h_mask_cut"], 1)
                    k += 1
                    pool.wait_ge(S["h_mask_cut"], k)
                    for view, pattern, base, mult in (
                            (a, [[0, 4], [16, 4], [1, 16]], 0, -1),
                            (a, [[0, 4], [-16, 4], [0, 16]], 0, 1),
                            (z[:, :, :, 1, :], [[0, 4], [-32, 2], [0, 16]], 0, 1),
                            (z[:, :, :, 1, :], [[0, 4], [32, 2], [0, 16]], 15, -1)):
                        k += 1
                        pool.affine_select(out=view, in_=view, compare_op=ALU.is_ge, fill=0.0, base=base,
                                           pattern=pattern, channel_multiplier=mult).then_inc(S["h_mask_cut"], 1)
                        pool.wait_ge(S["h_mask_cut"], k)
                pool.wait_ge(S["h_state_zero"], 1)
                for name in ("h_state1", "h_o_kept", "h_ready"):
                    pool.sem_inc(S[name], 1)
                rows = NSLOT * D // P // 1536
                pool.dma_start(x_slots.rearrange("(p a) d -> p (a d)", p=P).rearrange("p (r c) -> p r c", r=rows),
                               zeros.unsqueeze(1).to_broadcast([P, rows, 1536])).then_inc(S["slots_zeroed"], 16)

            @block.sync
            def _(sp):
                heads = "h k v -> k h v"
                sp.wait_ge(S["h_state1"], NCH + 1)
                sp.dma_start(O["hgrn_prompt"][0, 0].rearrange(heads, h=HEADS), state[:, :, :]).then_inc(S["h_state_out"], 16)
                sp.wait_ge(S["h_state_out"], 16)
                sp.dma_start(state[:, :, :], I["state_hgrn"][0, 0].rearrange(heads, h=HEADS)).then_inc(S["h_state_in"], 16)
                sp.wait_ge(S["h_state1"], NCH + 2)
                sp.dma_start(O["hgrn_sample"][0, 0].rearrange(heads, h=HEADS), state[:, :, :]).then_inc(S["h_state_out"], 16)
                sp.wait_ge(S["h_state_out"], 32)
                sp.wait_ge(S["slots_zeroed"], 16)

            @block.scalar
            def _(act):
                for f in range(FT):
                    act.activation(padded(B6, f), padded(B3, f), ACT.Ln).then_inc(S["h_g"], 1)
                act.wait_ge(S["h_b"], FT)
                hgrn_act(act, -1, False, True)
                with act.Fori(0, NCH - 1) as c:
                    hgrn_act(act, c, True, True)
                hgrn_act(act, NCH - 1, True, True)
                hgrn_act(act, NCH, True, False)
                act.wait_ge(S["h_o_kept"], NCH + 2)
                for f in range(FT):
                    act.activation(h_sq[:, f, :], arena[:, B2 + f, 1:1 + N], ACT.Square).then_inc(S["h_o_sq"], 1)
                for f in range(FT):
                    act.wait_ge(S["h_ms"], f + 1)
                    at = (f % 4) * 2
                    act.activation(h_rs[:, f, :].rearrange("p (h n) -> p h n", h=2), ps[:, at:at + 2, 0:HALF], ACT.Ln, bias=eps_c,
                                   scale=1.0 / P).then_inc(S["h_ln_ms"], 1)
                act.wait_ge(S["h_ln_ms"], FT)
                for f in range(FT):
                    act.activation(h_rs[:, f, :], h_rs[:, f, :], ACT.Exp, scale=-0.5).then_inc(S["h_rs"], 1)

            @block.vector
            def _(dve):
                dve.wait_ge(S["h_masks"], 1)
                for f in range(FT):
                    dve.wait_ge(S["h_g"], f + 1)
                    dve.tensor_tensor_scan(padded(B6, f), h_scan, padded(B6, f), 0.0, ALU.mult, ALU.add).then_inc(S["h_b"], 1)
                dve.wait_ge(S["h_ready"], 1)
                hgrn_dve(dve, -1, False, True)
                with dve.Fori(0, NCH - 1) as c:
                    hgrn_dve(dve, c, True, True)
                hgrn_dve(dve, NCH - 1, True, True)
                dve.wait_ge(S["h_state_in"], 16)
                hgrn_dve(dve, NCH, True, False)
                for f in range(FT):
                    dve.wait_ge(S["h_rs"], f + 1)
                    o, gate = arena[:, B2 + f, 1:1 + N], arena[:, B5 + f, 1:1 + N]
                    dve.tensor_tensor(gate, gate, h_rs[:, f, :], ALU.mult).then_inc(S["h_normed"], 1)
                    dve.wait_ge(S["h_normed"], f + 1)
                    dve.tensor_tensor(gate, gate, o, ALU.mult).then_inc(S["h_out"], 1)

            @block.tensor
            def _(pe):
                hgrn_pe(pe, -1, False, True)
                with pe.Fori(0, NCH - 1) as c:
                    hgrn_pe(pe, c, True, True)
                hgrn_pe(pe, NCH - 1, True, True)
                pe.wait_ge(S["h_state_in"], 16)
                hgrn_pe(pe, NCH, True, False)
                pe.wait_ge(S["h_o_kept"], NCH + 2)
                pe.wait_ge(S["h_state1"], NCH + 2)
                for f in range(FT):
                    pe.wait_ge(S["h_o_sq"], f + 1)
                    if f >= 4:
                        pe.wait_ge(S["h_ln_ms"], f - 3)
                    for h in range(2):
                        mm = pe.matmul(ps[:, (f % 4) * 2 + h, 0:HALF], ones[:, :], h_sq[:, f, h * HALF:(h + 1) * HALF], start=True, stop=True)
                    mm.then_inc(S["h_ms"], 1)

        S.end_stage()

        lin = Split("rwkv", [(ACT.Copy, w_in, COL_RWKV, 12, B2), (ACT.Sigmoid, w_in, COL_GATES + D, 4, B6)], H, XN, 0)
        lora_tiles = -(-LORA // P)
        w_lora = shaped(scr[:, :], 4 * FT * UNIT, (FT, lora_tiles * P))
        lora_hi, lora_lo = (rounded(f"lora_{part}", scr_at + 4 * k * FT * lora_tiles * P, FT, lora_tiles * P)[:, :, :] for k, part in enumerate(("hi", "lo")))

        with nc.Block() as block:
            @block.sync
            def _(sp):
                sp.dma_start(w_lora[:, :, 0:LORA], w_in.rearrange("(k p) n -> p k n", p=P)[:, :, COL_RWKV + 3 * D:COL_RWKV + N_RWKV]).then_inc(S["w_lora_in"], 16)
                lin.on_sp(sp)

            @block.scalar
            def _(act):
                lin.on_act(act)
                act.wait_ge(S["w_lora_in"], 16)
                act.wait_ge(S["w_lora_pad"], 1)
                act.copy(lora_hi, w_lora).then_inc(S["lora_hi"], 1)
                act.wait_ge(S["lora_done"], 1)
                for t in range(lora_tiles):
                    m = min(P, LORA - t * P)
                    act.copy(lora[0:m, t, 1:1 + N].rearrange("p (h n) -> p h n", h=2), ps[0:m, 2 * t:2 * t + 2, 0:HALF]).then_inc(S["lora_kept"], 1)

            @block.tensor
            def _(pe):
                lin.start_pe(pe)
                lin.on_pe(pe)
                pe.wait_ge(S["lora_lo"], 1)
                lin.wait_all_kept(pe)
                for t in range(lora_tiles):
                    for h in range(2):
                        mm = lin.products(pe, ps[:, 2 * t + h, 0:HALF], lora_hi[:, :, t * P:(t + 1) * P], lora_lo[:, :, t * P:(t + 1) * P], h)
                mm.then_inc(S["lora_done"], 1)

            @block.vector
            def _(dve):
                dve.memset(w_lora[:, :, LORA:lora_tiles * P], 0.0).then_inc(S["w_lora_pad"], 1)
                lin.on_dve(dve)
                dve.wait_ge(S["lora_hi"], 1)
                dve.tensor_tensor(lora_lo, w_lora, lora_hi.bitcast(F32), ALU.subtract).then_inc(S["lora_lo"], 1)

        S.end_stage()

        hroom = Room(flat[:, H * BW:(H + FT) * BW], FT * BW)
        xroom = Room(flat[:, XN * BW:(XN + FT) * BW], FT * BW)
        rroom = Room(ring_flat, 2 * FT * UNIT)
        room = Room(scr[:, :], SCR)
        wa2, g2a, g2b = room.take(D), room.take(D), room.take(D)
        d16low, d16up, offlow, strictup, inclup, eye = (room.take(CH) for _ in range(6))
        r_scan = room.take(FT * CH)
        v_d, l_d, l_s, l_a = room.take(FT, CH), room.take(3, CH), room.take(3, CH), room.take(3, CH)
        sa = room.take(2, FT, CH)
        sg_s, a_s = sa[:, 0], sa[:, 1]
        rb_s = room.take(FT, CH)
        w_dec = room.take(FT, CH + 2)
        iw = room.take(FT, CH)
        bh, kh = room.take(FT, CH), room.take(FT, CH)
        r_s, k_s2, v_s2 = xroom.take(FT, CH), xroom.take(FT, CH), xroom.take(FT, CH)
        d_r, d_k = xroom.take(FT, CH), xroom.take(FT, CH)
        kk, kmod, bka, rn = (xroom.take(FT, CH) for _ in range(4))
        rk_s = v_d
        g_raw = hroom.take(FT, CH)
        ar = room.take(FT, 2, CH)
        bonus, gg = room.take(FT, CH), room.take(FT, CH)
        t1, a1, n_low = room.take(FT, CH), room.take(FT, CH), room.take(FT, CH)
        st = room.take(FT, CH)
        b_tok, k_tok2, v_tok2 = (rroom.take(FT, CH) for _ in range(3))
        takT, trbT, trkT = (rroom.take(FT, CH) for _ in range(3))
        z_s, u_s = rroom.take(FT, CH), rroom.take(FT, CH)
        a2t2 = hroom.take(2, FT, CH)
        a4, t4, t8, qt, gt = (hroom.take(FT, CH) for _ in range(5))
        o_c = hroom.take(FT, CH)
        w_end = hroom.take(FT)
        u0_s, y_s = a4, t4
        o_q, o_r = bka, iw
        st_vk = z_s
        st_in = u_s
        w_prev, w_cur = w_dec[:, :, 0:CH], w_dec[:, :, 1:CH + 1]

        def pairs(m):
            return m.unsqueeze(1).to_broadcast([P, FT, CH])

        def q_half(q):
            return slice(64 * q, 64 * q + 64)

        def b_cols(b, a):
            return bank[b][:, a * CH:(a + 1) * CH]

        mu = cb[:, MU:MU + 27]

        def per_head(pe, b, lhsT, rhs, start=True, stop=True):
            for a in range(FT):
                for q in range(2):
                    r = q_half(q)
                    mm = pe.matmul(bank[b][r, a * CH:(a + 1) * CH], lhsT[r, a, :], rhs[r, a, :], start=start, stop=stop)
            return mm

        eye2 = [ident[q_half(q), q_half(q)] for q in range(2)]

        def turn_heads(pe, b, x):
            for a in range(FT):
                for q in range(2):
                    mm = pe.matmul(bank[b][q_half(q), a * CH:(a + 1) * CH], x[q_half(q), a, :], eye2[q], start=True, stop=True)
            return mm

        def frames_of_next(base, c, back=0):
            return frames(base, (c + 1) * CH - back, CH)

        def rwkv_pool(pool, c, cur, nxt):
            n, m = counts(pool, c)

            def const():
                pool.wait_ge(S["r_masks"], 1)

            if nxt:
                const()
                if cur:
                    pool.wait_ge(S["r_trk"], n)
                now, prev = lora[:, :, bass.ds((c + 1) * CH + 1, CH)], lora[:, :, bass.ds((c + 1) * CH, CH)]
                pool.tensor_tensor(l_d, prev, now, ALU.subtract).then_inc(S["r_ld"], 1)
                pool.wait_ge(S["r_ld"], m)
                pool.tensor_tensor(l_d, l_d, over(mu[:, 24:27], CH), ALU.mult).then_inc(S["r_lm"], 1)
                const()
                pool.wait_ge(S["r_lm"], m)
                pool.tensor_tensor(l_s, l_d, now, ALU.add).then_inc(S["r_l"], 1)
            if cur:
                const()
                pool.wait_ge(S["r_rks"], n)
                pool.wait_ge(S["r_chunk_done"], n)
                pool.tensor_tensor(bonus, rk_s, v_s2, ALU.mult).then_inc(S["r_bonus"], 1)
                const()
                pool.wait_ge(S["r_g"], n)
                pool.tensor_tensor(gg, g_raw, frames(B6, c * CH, CH), ALU.mult).then_inc(S["r_gg"], 1)
            if nxt:
                now, prev = frames_of_next(B4, c), frames_of_next(B4, c, 1)
                const()
                if cur:
                    pool.wait_ge(S["r_bonus"], n)
                    pool.wait_ge(S["r_v_turned"], n)
                pool.tensor_tensor(v_d, prev, now, ALU.subtract).then_inc(S["r_vd"], 1)
                pool.wait_ge(S["r_vd"], m)
                pool.tensor_tensor(v_d, v_d, over(mu[:, 16:24], CH), ALU.mult).then_inc(S["r_vm"], 1)
                const()
                pool.wait_ge(S["r_vm"], m)
                pool.tensor_tensor(v_s2, v_d, now, ALU.add).then_inc(S["r_v"], 1)
                pool.wait_ge(S["r_v"], m)
                pool.wait_ge(S["r_kmod"], m)
                pool.tensor_tensor(rk_s, r_s, kmod, ALU.mult).then_inc(S["r_rk0"], 1)
                pool.wait_ge(S["r_rk0"], m)
                pool.tensor_tensor(rk_s, rk_s, over(col("rwkv_r_k"), CH), ALU.mult).then_inc(S["r_rk"], 1)

        def rwkv_act(act, c, cur, nxt):
            n, m = counts(act, c)

            def keep_bank(cond, done, k, b, to, sem):
                if cond:
                    act.wait_ge(S[done], k)
                    act.copy(to, split_heads(bank[b])).then_inc(S[sem], 1)

            if cur:
                act.wait_ge(S["r_sq2"], n)
                act.copy(a2t2, ps[:, 5:7, :].rearrange("p e (a b) -> p e a b", a=8)).then_inc(S["r_a2t2"], 1)
            if nxt:
                act.wait_ge(S["r_l"], m)
                act.activation(l_a[0:64, 0, :], l_s[0:64, 0, :], ACT.Sigmoid, scale=2.0)
                act.activation(l_a[:, 1:3, :], l_s[:, 1:3, :], ACT.Sigmoid).then_inc(S["r_la_sg"], 1)
                act.wait_ge(S["r_kk0"], m)
                act.activation(rn, kk, ACT.Square).then_inc(S["r_kk_sq"], 1)
            keep_bank(cur, "r_sq4", n, 6, t4, "r_t4")
            keep_bank(cur, "r_sq4", n, 5, a4, "r_a4")
            keep_bank(cur, "r_sq8", n, 5, t8, "r_t8")
            keep_bank(cur, "r_z_done", n, 0, z_s, "r_z")
            if nxt:
                act.wait_ge(S["r_pre"], m)
                act.activation(sa, sa, ACT.Sigmoid).then_inc(S["r_sa"], 1)
            keep_bank(cur, "r_gt_done", n, 6, gt, "r_gt")
            if nxt:
                if cur:
                    act.wait_ge(S["r_gg"], n)
                act.wait_ge(S["r_glora"], m)
                act.copy(g_raw, split_heads(bank[2])).then_inc(S["r_g"], 1)
                act.wait_ge(S["r_ssm"], m)
                act.activation(rn, rn, ACT.Ln, scale=2.0 ** 30).then_inc(S["r_ln_ss"], 1)
                act.wait_ge(S["r_ln_ss"], m)
                act.activation(rn, rn, ACT.Exp, scale=-0.5, bias=kk_c).then_inc(S["r_rn"], 1)
            if nxt:
                act.wait_ge(S["r_b"], m)
                act.activation(iw, rb_s, ACT.Exp, scale=DECAY).then_inc(S["r_iw"], 1)
                if cur:
                    act.wait_ge(S["r_wend"], n)
                act.activation(w_cur, rb_s, ACT.Exp, scale=-DECAY).then_inc(S["r_w"], 1)
            keep_bank(cur, "r_o_done", n, 2, o_c, "r_o")
            keep_bank(nxt, "r_rk_ss", m, 7, rk_s, "r_rks")
            if cur:
                act.wait_ge(S["r_oc"], n)
                act.activation(o_q, o_c, ACT.Square).then_inc(S["r_o_sq"], 1)
            keep_bank(nxt, "r_b_turned", m, 6, b_tok, "r_b_tok")
            if cur:
                act.wait_ge(S["r_var"], n)
                act.activation(o_r, split_heads(bank[5]), ACT.Ln, scale=1.0 / 64, bias=gn_eps_c).then_inc(S["r_ln_var"], 1)
                act.wait_ge(S["r_ln_var"], n)
                act.activation(o_r, o_r, ACT.Exp, scale=-0.5).then_inc(S["r_rstd"], 1)
            keep_bank(nxt, "r_k_turned", m, 7, k_tok2, "r_k_tok")
            keep_bank(nxt, "r_v_turned", m, 5, v_tok2, "r_v_tok")

        def rwkv_dve(dve, c, cur, nxt, last):
            n, m = counts(dve, c)
            pad = slice(DEC, CH)
            two = lambda b: ps[:, b:b + 2, :].rearrange("p b (a e t) -> p (b a) e t", a=4, e=2)

            def add_power(k, b):
                dve.wait_ge(S[f"r_q{k}_done"], n)
                dve.wait_ge(S[f"r_qt{k - 1}"], n)
                dve.tensor_tensor(qt, qt, split_heads(bank[b]), ALU.add).then_inc(S[f"r_qt{k}"], 1)

            if nxt:
                r_cur, k_cur = frames_of_next(B2, c), frames_of_next(B3, c)
                dve.tensor_tensor(d_k, frames_of_next(B3, c, 1), k_cur, ALU.subtract).then_inc(S["r_kd"], 1)
                dve.tensor_tensor(d_r, frames_of_next(B2, c, 1), r_cur, ALU.subtract).then_inc(S["r_rd"], 1)
                dve.wait_ge(S["r_kd"], m)
                dve.tensor_tensor(d_k, d_k, over(mu[:, 8:16], CH), ALU.mult).then_inc(S["r_km"], 1)
                dve.wait_ge(S["r_rd"], m)
                dve.tensor_tensor(d_r, d_r, over(mu[:, 0:8], CH), ALU.mult).then_inc(S["r_rm"], 1)
                dve.wait_ge(S["r_km"], m)
                dve.tensor_tensor(k_s2, d_k, k_cur, ALU.add).then_inc(S["r_k"], 1)
                dve.wait_ge(S["r_rm"], m)
                dve.tensor_tensor(r_s, d_r, r_cur, ALU.add).then_inc(S["r_r"], 1)
                dve.wait_ge(S["r_k"], m)
                dve.tensor_tensor(kk, k_s2, over(col("rwkv_k_k"), CH), ALU.mult).then_inc(S["r_kk0"], 1)
            if cur:
                add_power(2, 7)
            if nxt:
                dve.wait_ge(S["r_la_sg"], m)
                dve.tensor_scalar(l_a[0:64, 0, :], l_a[0:64, 0, :], 2.0, -1.0, ALU.mult, ALU.add).then_inc(S["r_la_th"], 1)
                dve.wait_ge(S["r_kk_ss"], m)
                dve.wait_ge(S["r_kk_sq"], m)
                dve.tensor_scalar(rn, split_heads(bank[3]), 1e-24, None, ALU.max).then_inc(S["r_ssm"], 1)
            if cur:
                add_power(3, 6)
            if nxt:
                dve.wait_ge(S["r_wlora"], m)
                dve.tensor_tensor(sg_s, split_heads(bank[1]), over(col("rwkv_w0"), CH), ALU.add)
                dve.tensor_tensor(a_s, split_heads(bank[4]), over(col("rwkv_a0"), CH), ALU.add).then_inc(S["r_pre"], 1)
            if cur:
                add_power(4, 7)
            if nxt:
                dve.wait_ge(S["r_sa"], m)
                if last:
                    dve.memset(sg_s[:, :, pad], 0.0).then_inc(S["r_pad"], 1)
                    dve.wait_ge(S["r_pad"], 1)
                dve.tensor_tensor_scan(flat2(rb_s), r_scan, flat2(sg_s), 0.0, ALU.mult, ALU.add).then_inc(S["r_b"], 1)
            if cur:
                dve.wait_ge(S["r_u0_done"], n)
                dve.tensor_copy(u0_s, split_heads(bank[7])).then_inc(S["r_u0"], 1)
            if nxt:
                dve.scalar_tensor_tensor(out=kmod, in0=a_s, scalar=-1.0, in1=over(col("rwkv_k_a"), CH), op0=ALU.add, op1=ALU.mult).then_inc(S["r_ka"], 1)
                dve.wait_ge(S["r_rn"], m)
                dve.tensor_tensor(kk, kk, rn, ALU.mult).then_inc(S["r_kkn"], 1)
            if cur:
                dve.wait_ge(S["r_h1_done"], n)
                dve.wait_ge(S["r_u0"], n)
                dve.tensor_tensor(y_s, u0_s, split_heads(bank[5]), ALU.add).then_inc(S["r_y1"], 1)
            if nxt:
                dve.wait_ge(S["r_ka"], m)
                dve.scalar_tensor_tensor(out=kmod, in0=kmod, scalar=1.0, in1=k_s2, op0=ALU.add, op1=ALU.mult).then_inc(S["r_kmod0"], 1)
                dve.wait_ge(S["r_kkn"], m)
                dve.tensor_tensor(bka, kk, a_s, ALU.mult).then_inc(S["r_bka"], 1)
            if cur:
                dve.wait_ge(S["r_h2_done"], n)
                dve.tensor_tensor(y_s, u0_s, split_heads(bank[6]), ALU.add).then_inc(S["r_y2"], 1)
            if nxt:
                dve.wait_ge(S["r_bka"], m)
                dve.wait_ge(S["r_kmod0"], m)
                if last:
                    dve.memset(kmod[:, :, pad], 0.0).then_inc(S["r_pad"], 1)
                    dve.memset(bka[:, :, pad], 0.0).then_inc(S["r_pad"], 1)
                    dve.wait_ge(S["r_pad"], 3)
                dve.sem_inc(S["r_kmod"], 1)
            if cur:
                dve.wait_ge(S["r_h3_done"], n)
                dve.tensor_tensor(u_s, u0_s, split_heads(bank[5]), ALU.add).then_inc(S["r_u"], 1)
            if nxt:
                dve.wait_ge(S["r_iw"], m)
                dve.tensor_tensor(bh, bka, iw, ALU.mult).then_inc(S["r_bh"], 1)
                dve.tensor_tensor(kh, kmod, iw, ALU.mult).then_inc(S["r_kh"], 1)
            if cur:
                dve.wait_ge(S["r_o_done"], n)
                dve.tensor_tensor(st, st, split_heads(bank[3]), ALU.add).then_inc(S["r_st0"], 1)
                dve.wait_ge(S["r_st0"], n)
                dve.tensor_tensor(st, st, over(w_end, CH), ALU.mult).then_inc(S["r_st"], 1)
            if nxt:
                dve.wait_ge(S["r_w"], m)
                dve.scalar_tensor_tensor(out=ar[:, :, 0, :], in0=kk, scalar=-1.0, in1=w_prev, op0=ALU.mult, op1=ALU.mult).then_inc(S["r_ah"], 1)
                dve.tensor_tensor(ar[:, :, 1, :], r_s, w_cur, ALU.mult).then_inc(S["r_rh"], 1)
            if cur:
                dve.wait_ge(S["r_mean"], n)
                dve.wait_ge(S["r_o"], n)
                dve.scalar_tensor_tensor(out=o_c, in0=split_heads(bank[4]), scalar=-1.0 / 64, in1=o_c, op0=ALU.mult, op1=ALU.add).then_inc(S["r_oc"], 1)
            if nxt:
                dve.wait_ge(S["r_t_done"], m)
                dve.tensor_tensor(t1, split_heads(bank[0]), pairs(d16low), ALU.mult).then_inc(S["r_t1"], 1)
                dve.tensor_tensor(n_low, split_heads(bank[0]), pairs(offlow), ALU.mult).then_inc(S["r_n_low"], 1)
                dve.wait_ge(S["r_tt_done"], m)
                dve.tensor_tensor(a1, two(1)[:, :, 0, :], pairs(d16up), ALU.mult).then_inc(S["r_a1"], 1)
                dve.tensor_tensor(trbT, two(1)[:, :, 1, :], pairs(inclup), ALU.mult).then_inc(S["r_trb"], 1)
                dve.wait_ge(S["r_a1"], m)
                dve.tensor_tensor(qt, a1, pairs(eye), ALU.add).then_inc(S["r_qt1"], 1)
                if cur:
                    dve.wait_ge(S["r_st"], n)
                dve.tensor_copy(w_end, w_dec[:, :, CH:CH + 1].rearrange("p f o -> p (f o)")).then_inc(S["r_wend"], 1)
            if cur:
                dve.wait_ge(S["r_rstd"], n)
                dve.tensor_tensor(o_c, o_c, o_r, ALU.mult).then_inc(S["r_e1"], 1)
            if nxt:
                dve.wait_ge(S["r_tk_done"], m)
                dve.tensor_tensor(takT, two(3)[:, :, 0, :], pairs(strictup), ALU.mult).then_inc(S["r_tak"], 1)
                dve.tensor_tensor(trkT, two(3)[:, :, 1, :], pairs(inclup), ALU.mult).then_inc(S["r_trk"], 1)
            if cur:
                dve.wait_ge(S["r_e1"], n)
                dve.tensor_tensor(o_c, o_c, over(col("rwkv_ln_g"), CH), ALU.mult).then_inc(S["r_e2"], 1)
                dve.wait_ge(S["r_e2"], n)
                dve.tensor_tensor(o_c, o_c, over(col("rwkv_ln_b"), CH), ALU.add).then_inc(S["r_e3"], 1)
                dve.wait_ge(S["r_e3"], n)
                dve.wait_ge(S["r_bonus"], n)
                dve.tensor_tensor(o_c, o_c, bonus, ALU.add).then_inc(S["r_e4"], 1)
                dve.wait_ge(S["r_e4"], n)
                dve.wait_ge(S["r_gg"], n)
                dve.tensor_tensor(o_c, o_c, gg, ALU.mult).then_inc(S["r_e5"], 1)
                dve.wait_ge(S["r_e5"], n)
                dve.tensor_tensor(frames(B5, c * CH, CH), frames(B5, c * CH, CH), o_c, ALU.add).then_inc(S["r_chunk_done"], 1)

        def rwkv_pe(pe, c, cur, nxt):
            n, m = counts(pe, c)

            def const():
                pe.wait_ge(S["r_masks"], 1)

            def both(b, x):
                for a in range(FT):
                    for q in range(2):
                        mm = pe.matmul(bank[b + a // 4][q_half(q), (a % 4) * 2 * CH:(a % 4 + 1) * 2 * CH], x[q_half(q), a, :],
                                       ar[q_half(q), a, :, :], start=True, stop=True)
                return mm

            if cur:
                pe.wait_ge(S["r_v_tok"], n)
                pe.sem_inc(S["r_core_begun"], 1)
                const()
                pe.wait_ge(S["r_b_tok"], n)
                pe.wait_ge(S["r_t1"], n)
                pe.wait_ge(S["r_a1"], n)
                per_head(pe, 5, t1, a1)
                per_head(pe, 6, a1, t1).then_inc(S["r_sq2"], 1)
                const()
                pe.wait_ge(S["r_a2t2"], n)
                per_head(pe, 5, a2t2[:, 1], a2t2[:, 0])
                per_head(pe, 6, a2t2[:, 0], a2t2[:, 1]).then_inc(S["r_sq4"], 1)
                const()
                pe.wait_ge(S["r_k_tok"], n)
                pe.wait_ge(S["r_qt1"], n)
                per_head(pe, 7, a2t2[:, 1], qt).then_inc(S["r_q2_done"], 1)
            if nxt:
                if cur:
                    pe.wait_ge(S["r_trk"], n)
                pe.wait_ge(S["r_kk_sq"], m)
                pe.matmul(bank[3], head_ones[:, :], flat2(rn), start=True, stop=True).then_inc(S["r_kk_ss"], 1)
            if cur:
                const()
                pe.wait_ge(S["r_a4"], n)
                per_head(pe, 5, a4, t4).then_inc(S["r_sq8"], 1)
                const()
                pe.wait_ge(S["r_qt2"], n)
                per_head(pe, 6, t4, qt).then_inc(S["r_q3_done"], 1)
            if nxt:
                const()
                pe.wait_ge(S["r_l"], m)
                for f in range(FT):
                    pe.matmul(b_cols(4, f), wa2[64:128, f * P:(f + 1) * P], l_s[64:128, 0, :], start=True, stop=True)
                pe.wait_ge(S["r_la_th"], m)
                for f in range(FT):
                    mm = pe.matmul(b_cols(1, f), wa2[0:64, f * P:(f + 1) * P], l_a[0:64, 0, :], start=True, stop=True)
                mm.then_inc(S["r_wlora"], 1)
            if cur:
                const()
                pe.wait_ge(S["r_tak"], n)
                for a in range(FT):
                    for q in range(2):
                        r = q_half(q)
                        pe.matmul(bank[0][r, a * CH:(a + 1) * CH], takT[r, a, :], v_tok2[r, a, :], start=True, stop=False)
                        mm = pe.matmul(bank[0][r, a * CH:(a + 1) * CH], ar[r, a, 0, :], st[r, a, :], start=False, stop=True)
                mm.then_inc(S["r_z_done"], 1)
                const()
                pe.wait_ge(S["r_t8"], n)
                pe.wait_ge(S["r_qt3"], n)
                per_head(pe, 7, t8, qt).then_inc(S["r_q4_done"], 1)
            if nxt:
                pe.wait_ge(S["r_la_sg"], m)
                for f in range(FT):
                    pe.matmul(b_cols(2, f), g2a[:, f * P:(f + 1) * P], l_a[:, 1, :], start=True, stop=False)
                    mm = pe.matmul(b_cols(2, f), g2b[0:32, f * P:(f + 1) * P], l_a[0:32, 2, :], start=False, stop=True)
                mm.then_inc(S["r_glora"], 1)
            if cur:
                const()
                pe.wait_ge(S["r_n_low"], n)
                pe.wait_ge(S["r_qt4"], n)
                per_head(pe, 6, n_low, qt).then_inc(S["r_gt_done"], 1)
                const()
                pe.wait_ge(S["r_z"], n)
                per_head(pe, 7, qt, z_s).then_inc(S["r_u0_done"], 1)
                const()
                pe.wait_ge(S["r_gt"], n)
                pe.wait_ge(S["r_u0"], n)
                per_head(pe, 5, gt, u0_s).then_inc(S["r_h1_done"], 1)
                const()
                pe.wait_ge(S["r_y1"], n)
                per_head(pe, 6, gt, y_s).then_inc(S["r_h2_done"], 1)
                const()
                pe.wait_ge(S["r_y2"], n)
                per_head(pe, 5, gt, y_s).then_inc(S["r_h3_done"], 1)
                if nxt:
                    const()
                    pe.wait_ge(S["r_pre"], m)
                const()
                pe.wait_ge(S["r_u"], n)
                for a in range(FT):
                    for q in range(2):
                        r = q_half(q)
                        out = bank[3][r, a * CH:(a + 1) * CH]
                        pe.matmul(out, b_tok[r, a, :], u_s[r, a, :], start=True, stop=False)
                        pe.matmul(out, k_tok2[r, a, :], v_tok2[r, a, :], start=False, stop=True)
                if nxt:
                    const()
                    pe.wait_ge(S["r_g"], m)
                const()
                pe.wait_ge(S["r_trk"], n)
                for a in range(FT):
                    for q in range(2):
                        r = q_half(q)
                        out = bank[2][r, a * CH:(a + 1) * CH]
                        pe.matmul(out, st[r, a, :], ar[r, a, 1, :], start=True, stop=False)
                        pe.matmul(out, u_s[r, a, :], trbT[r, a, :], start=False, stop=False)
                        mm = pe.matmul(out, v_tok2[r, a, :], trkT[r, a, :], start=False, stop=True)
                mm.then_inc(S["r_o_done"], 1)
            if nxt:
                pe.wait_ge(S["r_rk"], m)
                pe.matmul(bank[7], head_ones[:, :], flat2(rk_s), start=True, stop=True).then_inc(S["r_rk_ss"], 1)
                const()
                pe.wait_ge(S["r_bh"], m)
                pe.wait_ge(S["r_ah"], m)
                per_head(pe, 0, ar[:, :, 0, :], bh).then_inc(S["r_t_done"], 1)
            if cur:
                pe.wait_ge(S["r_o"], n)
                pe.matmul(bank[4], head_ones[:, :], flat2(o_c), start=True, stop=True).then_inc(S["r_mean"], 1)
            if nxt:
                const()
                pe.wait_ge(S["r_rh"], m)
                both(1, bh).then_inc(S["r_tt_done"], 1)
                turn_heads(pe, 6, bh).then_inc(S["r_b_turned"], 1)
            if cur:
                pe.wait_ge(S["r_o_sq"], n)
                pe.matmul(bank[5], head_ones[:, :], flat2(o_q), start=True, stop=True).then_inc(S["r_var"], 1)
            if nxt:
                const()
                pe.wait_ge(S["r_rks"], m)
                pe.wait_ge(S["r_kh"], m)
                turn_heads(pe, 7, kh).then_inc(S["r_k_turned"], 1)
                const()
                if cur:
                    pe.wait_ge(S["r_oc"], n)
                    pe.wait_ge(S["r_st0"], n)
                both(3, kh).then_inc(S["r_tk_done"], 1)
                const()
                pe.wait_ge(S["r_v"], m)
                if cur:
                    pe.wait_ge(S["r_ln_var"], n)
                turn_heads(pe, 5, v_s2).then_inc(S["r_v_turned"], 1)

        ends = ((0, SEQ), (32, N))
        shift_cols = rows_a
        shift_rows = rows_b
        full = N_RWKV // P
        rest = N_RWKV - full * P

        with nc.Block() as block:
            @block.gpsimd
            def _(pool):
                for m in (d16low, d16up, offlow, strictup, inclup, eye):
                    pool.memset(m, 1.0).then_inc(S["r_mask_ones"], 1)
                pool.memset(r_scan, 1.0).then_inc(S["r_mask_ones"], 1)
                pool.memset(st, 0.0).then_inc(S["r_mask_ones"], 1)
                pool.memset(w_dec[:, :, 0:1], 1.0).then_inc(S["r_mask_ones"], 1)
                pool.wait_ge(S["r_mask_ones"], 9)
                pool.memset(r_scan.rearrange("p (m l) -> p m l", l=CH)[:, :, 0:1], 0.0).then_inc(S["r_scan_ready"], 1)
                pool.wait_ge(S["r_scan_ready"], 1)
                k = 0

                def cut(m, pattern, base, mult, op=ALU.is_ge):
                    pool.affine_select(out=m, in_=m, compare_op=op, fill=0.0, base=base, pattern=pattern,
                                       channel_multiplier=mult).then_inc(S["r_mask_cut"], 1)

                for q in range(2):
                    r = q_half(q)
                    b16 = lambda m: m[r].rearrange("p (b l) -> p b l", l=16)
                    steps = [
                        [(d16low[r], [[-1, CH]], -1, 1), (d16up[r], [[1, CH]], -1, -1), (strictup[r], [[1, CH]], -1, -1),
                         (inclup[r], [[1, CH]], 0, -1), (b16(offlow), [[-16, 4], [0, 16]], -16, 1)],
                        [(b16(d16low), [[16, 4], [0, 16]], 15, -1), (b16(d16up), [[-16, 4], [0, 16]], 0, 1)],
                    ]
                    for step in steps:
                        for m, pattern, base, mult in step:
                            cut(m, pattern, base, mult)
                            k += 1
                            pool.wait_ge(S["r_mask_cut"], k)
                    cut(eye[r], [[1, CH]], 0, -1, ALU.is_equal)
                    k += 1
                    pool.wait_ge(S["r_mask_cut"], k)
                pool.wait_ge(S["r_lora_in"], 64)
                pool.wait_ge(S["r_ends_kept"], 1)
                pool.sem_inc(S["r_masks"], 1)
                pool.sem_inc(S["r_chunk_done"], 1)
                rwkv_pool(pool, -1, False, True)
                with pool.Fori(0, NCH - 1) as c:
                    rwkv_pool(pool, c, True, True)
                pool.wait_ge(S["r_shift_swapped"], 4)
                rwkv_pool(pool, NCH - 1, True, True)
                rwkv_pool(pool, NCH, True, False)

            @block.sync
            def _(sp):
                sp.dma_start(wa2[0:64, :], I["rwkv_w2"][0]).then_inc(S["r_lora_in"], 16)
                sp.dma_start(wa2[64:128, :], I["rwkv_a2"][0]).then_inc(S["r_lora_in"], 16)
                sp.dma_start(g2a, I["rwkv_g2"][0][0:P, :]).then_inc(S["r_lora_in"], 16)
                sp.dma_start(g2b[0:32, :], I["rwkv_g2"][0][P:GATE_L, :]).then_inc(S["r_lora_in"], 16)
                sp.wait_ge(S["r_ends_kept"], 1)
                for (r0, _), name in zip(ends, ("shift_prompt", "shift_sample")):
                    out = O[name][0, 0, 0]
                    sp.dma_start(out[0:full * P].rearrange("(f p) -> f p", p=P), shift_rows[r0:r0 + full, :]).then_inc(S["r_shift_out"], 16)
                    sp.dma_start(out[full * P:N_RWKV].unsqueeze(0), shift_rows[r0 + full:r0 + full + 1, 0:rest]).then_inc(S["r_shift_out"], 16)
                rows = "(a q) v k -> (q v) a k"
                sp.wait_ge(S["r_state_turned"], 1)
                sp.dma_start(O["rwkv_prompt"][0, 0].rearrange(rows, q=2), st_vk).then_inc(S["r_state_out"], 16)
                sp.dma_start(st_in, I["state_rwkv"][0, 0].rearrange(rows, q=2)).then_inc(S["r_state_in"], 16)
                sp.wait_ge(S["r_state_turned"], 2)
                sp.dma_start(O["rwkv_sample"][0, 0].rearrange(rows, q=2), st_vk).then_inc(S["r_state_out"], 16)
                sp.wait_ge(S["r_state_out"], 32)
                sp.wait_ge(S["r_shift_out"], 64)

            @block.scalar
            def _(act):
                rwkv_act(act, -1, False, True)
                with act.Fori(0, NCH - 1) as c:
                    rwkv_act(act, c, True, True)
                rwkv_act(act, NCH - 1, True, True)
                act.wait_ge(S["r_end_turned"], 1)
                act.copy(st_vk, split_heads(bank[6])).then_inc(S["r_state_turned"], 1)
                act.wait_ge(S["r_state_out"], 16)
                rwkv_act(act, NCH, True, False)
                act.wait_ge(S["r_end_turned"], 2)
                act.copy(st_vk, split_heads(bank[6])).then_inc(S["r_state_turned"], 1)

            @block.vector
            def _(dve):
                dve.memset(shift_cols[:, :], 0.0).then_inc(S["r_ends_zero"], 1)
                dve.wait_ge(S["r_ends_zero"], 1)
                for r0, at in ends:
                    for g, base in enumerate((B2, B3, B4)):
                        dve.tensor_copy(shift_cols[:, r0 + 8 * g:r0 + 8 * g + 8].unsqueeze(2), arena[:, base:base + FT, at:at + 1])
                    cp = dve.tensor_copy(shift_cols[:, r0 + 24:r0 + 27].unsqueeze(2), lora[:, :, at:at + 1])
                cp.then_inc(S["r_ends"], 1)
                dve.wait_ge(S["r_ends_turned"], 1)
                dve.tensor_copy(shift_rows[:, :], bank[0][:, 0:P]).then_inc(S["r_ends_kept"], 1)
                dve.wait_ge(S["r_masks"], 1)
                rwkv_dve(dve, -1, False, True, False)
                with dve.Fori(0, NCH - 1) as c:
                    rwkv_dve(dve, c, True, True, False)
                dve.wait_ge(S["r_l"], NCH)
                dve.wait_ge(S["r_v"], NCH)
                for g, base in enumerate((B2, B3, B4)):
                    dve.tensor_copy(arena[:, base:base + FT, SEQ:SEQ + 1], cb[:, SHIFT + 8 * g:SHIFT + 8 * g + 8].unsqueeze(2)).then_inc(S["r_shift_swapped"], 1)
                dve.tensor_copy(lora[:, :, SEQ:SEQ + 1], cb[:, SHIFT + 24:SHIFT + 27].unsqueeze(2)).then_inc(S["r_shift_swapped"], 1)
                dve.wait_ge(S["r_shift_swapped"], 4)
                rwkv_dve(dve, NCH - 1, True, True, True)
                dve.wait_ge(S["r_start_turned"], 1)
                dve.tensor_copy(st, split_heads(bank[7])).then_inc(S["r_swapped"], 1)
                rwkv_dve(dve, NCH, True, False, False)

            @block.tensor
            def _(pe):
                pe.wait_ge(S["r_ends"], 1)
                pe.transpose(bank[0][:, 0:P], shift_cols[:, :], ident[:, :]).then_inc(S["r_ends_turned"], 1)
                pe.wait_ge(S["r_ends_kept"], 1)
                pe.wait_ge(S["r_masks"], 1)
                rwkv_pe(pe, -1, False, True)
                with pe.Fori(0, NCH - 1) as c:
                    rwkv_pe(pe, c, True, True)
                rwkv_pe(pe, NCH - 1, True, True)
                pe.wait_ge(S["r_st"], NCH)
                pe.wait_ge(S["r_b_tok"], NCH + 1)
                pe.wait_ge(S["r_k_tok"], NCH + 1)
                turn_heads(pe, 6, st).then_inc(S["r_end_turned"], 1)
                pe.wait_ge(S["r_state_in"], 16)
                turn_heads(pe, 7, st_in).then_inc(S["r_start_turned"], 1)
                pe.wait_ge(S["r_swapped"], 1)
                rwkv_pe(pe, NCH, True, False)
                pe.wait_ge(S["r_chunk_done"], NCH + 2)
                turn_heads(pe, 6, st).then_inc(S["r_end_turned"], 1)

        S.end_stage()

        mroom = Room(flat[:, B2 * BW:B5 * BW], 3 * FT * BW)
        memT, mem_n, mem_sq = (mroom.take(FT, MEM) for _ in range(3))
        mem_tok = mroom.take(2, D)
        aroom = Room(scr[:, :], SCR)
        kT = [aroom.take(FT, MEM) for _ in range(2)]
        v_mem = [aroom.take(2, D) for _ in range(2)]
        k_mem = [mroom.take(2, D) for _ in range(2)]
        a_sq_base = aroom.at

        l_sp, l_pe, l_leave = linear([("add", I["w_out"][0], 0, 4, B5, H)])
        out_units = used[0]
        m_sp, m_rows_pe, m_leave = linear([("rows", I["wk_x"][0], 0, 4, mem_n, k_mem[0]), ("rows", I["wv_x"][0], 0, 4, mem_n, v_mem[0])])
        m_act, m_pe, m_dve = norm_stage("mem", memT, mem_n, lambda f: col("norm_mem_g", f), MEM, mem_sq)

        def turn_rows(pe, src, j, b):
            for f in range(4):
                mm = pe.transpose(bank[b][:, f * P:(f + 1) * P], src[:, j // 2, ((j % 2) * 4 + f) * P:((j % 2) * 4 + f + 1) * P], ident[:, :])
            return mm

        def turned(dst, j):
            return dst[:, (j % 2) * 4:(j % 2) * 4 + 4, (j // 2) * P:(j // 2 + 1) * P]

        def quarters(b):
            return bank[b].rearrange("p (f n) -> p f n", f=4)

        with nc.Block() as block:
            @block.sync
            def _(sp):
                sp.dma_start(mem_tok, I["mem_prompt"][0].rearrange("(t p) d -> p t d", p=P)).then_inc(S["mem_in"], 16)
                l_sp(sp)
                m_sp(sp)
                rows = "(t p) h d -> p t (h d)"
                sp.wait_ge(S["banks0_free"], used[0] + 1)
                sp.wait_ge(S["banks1_free"], used[0] + 1)
                sp.dma_start(O["mem_k"][0, 0].rearrange(rows, p=P), k_mem[0]).then_inc(S["mem_out"], 16)
                sp.dma_start(O["mem_v"][0, 0].rearrange(rows, p=P), v_mem[0]).then_inc(S["mem_out"], 16)
                sp.wait_ge(S["mem_out"], 32)

            @block.gpsimd
            def _(pool):
                pool.dma_start(k_mem[1], I["cache_mem_k"][0, 0].rearrange("(t p) h d -> p t (h d)", p=P)).then_inc(S["cache_k_in"], 16)
                pool.dma_start(flat[:, H * BW:(H + FT) * BW], h_kept).then_inc(S["h_back"], 16)
                pool.dma_start(v_mem[1], I["cache_mem_v"][0, 0].rearrange("(t p) h d -> p t (h d)", p=P)).then_inc(S["cache_v_in"], 16)
                pool.wait_ge(S["cache_v_in"], 16)

            @block.scalar
            def _(act):
                act.wait_ge(S["memT"], 4)
                m_act(act)
                m_leave(act, False)

            @block.tensor
            def _(pe):
                pe.wait_ge(S["mem_in"], 16)
                for j in range(4):
                    mm = turn_rows(pe, mem_tok, j, j)
                mm.then_inc(S["mem_turned"], 1)
                pe.wait_ge(S["cache_k_in"], 16)
                for j in range(4):
                    mm = turn_rows(pe, k_mem[1], j, 4 + j)
                mm.then_inc(S["cache_turned"], 1)
                pe.wait_ge(S["memT"], 4)
                pe.wait_ge(S["cacheT"], 4)
                l_pe(pe)
                for s in range(2):
                    pe.wait_ge(S[f"banks{s}_free"], out_units + 1)
                m_pe(pe)
                pe.wait_ge(S["mem_normed"], FT)
                m_rows_pe(pe)
                pe.wait_ge(S["banks0_free"], used[0] + 1)
                pe.wait_ge(S["banks1_free"], used[0] + 1)
                for j in range(4):
                    mm = turn_rows(pe, k_mem[0], j, j)
                mm.then_inc(S["keys_turned"], 1)

            @block.vector
            def _(dve):
                dve.wait_ge(S["mem_turned"], 1)
                for j in range(4):
                    dve.tensor_copy(turned(memT, j), quarters(j)).then_inc(S["memT"], 1)
                dve.wait_ge(S["cache_turned"], 1)
                for j in range(4):
                    dve.tensor_copy(turned(kT[1], j), quarters(4 + j)).then_inc(S["cacheT"], 1)
                dve.wait_ge(S["h_back"], 16)
                l_leave(dve, True)
                m_dve(dve)
                dve.wait_ge(S["keys_turned"], 1)
                for j in range(4):
                    dve.tensor_copy(turned(kT[0], j), quarters(j)).then_inc(S["keysT"], 1)

        S.end_stage()

        sq_b = shaped(flat, B4 * BW, (FT, N))
        n_act, n_pe, n_dve = norm_stage("x", whole(H), whole(XN), lambda f: col("norm_x_g", f), N, sq_b)
        l_sp, l_pe, l_leave = linear([("keep", I["wq_x"][0], 0, 4, XN, B2)])

        with nc.Block() as block:
            @block.sync
            def _(sp):
                l_sp(sp)

            @block.scalar
            def _(act):
                n_act(act)
                l_leave(act, False)

            @block.tensor
            def _(pe):
                n_pe(pe)
                pe.wait_ge(S["x_normed"], FT)
                pe.wait_ge(S["x_rms"], 2)
                l_pe(pe)

            @block.vector
            def _(dve):
                n_dve(dve)

        S.end_stage()

        q_s, p_s, pT = aroom.take(FT, P), aroom.take(XH, MEM), aroom.take(FT, P)
        mx, sm = aroom.take(XH), aroom.take(XH)

        def attention_act(act, t, cur, nxt):
            n, m = counts(act, t)
            if nxt:
                if cur:
                    act.wait_ge(S["a_scores"], n)
                act.copy(q_s[:, :, 0:nxt], frames(B2, (t + 1) * P, nxt)).then_inc(S["a_q"], 1)
            if cur:
                act.wait_ge(S["a_shifted"], n)
                act.activation(p_s[0:cur], p_s[0:cur], ACT.Exp, scale=XSCALE).then_inc(S["a_exp"], 1)
                act.wait_ge(S["a_turned"], n)
                act.copy(pT[:, :, 0:cur], ps[:, 2:4, :].rearrange("p b (f n) -> p (b f) n", f=4)[:, :, 0:cur]).then_inc(S["a_pT"], 1)
                act.wait_ge(S["a_o"], n)
                act.copy(frames(B3, t * P, cur), ps[:, 4:6, :].rearrange("p b (f n) -> p (b f) n", f=4)[:, :, 0:cur]).then_inc(S["a_tile_done"], 1)

        def attention_dve(dve, t, cur, nxt):
            n, m = counts(dve, t)
            if cur:
                dve.wait_ge(S["a_exp"], n)
                dve.tensor_reduce(sm[0:cur], p_s[0:cur], AX_X, ALU.add).then_inc(S["a_sum"], 1)
                dve.wait_ge(S["a_sum"], n)
                dve.reciprocal(sm[0:cur], sm[0:cur]).then_inc(S["a_rsum"], 1)
                dve.wait_ge(S["a_rsum"], n)
                dve.tensor_tensor(p_s[0:cur], p_s[0:cur], sm[0:cur].unsqueeze(2).to_broadcast([cur, XH, MEM]), ALU.mult).then_inc(S["a_p"], 1)
            if nxt:
                scores = ps[0:nxt, 0:2, :].rearrange("p b (h k) -> p (b h) k", h=2)
                dve.wait_ge(S["a_scores"], m)
                dve.tensor_reduce(mx[0:nxt], scores, AX_X, ALU.max).then_inc(S["a_max"], 1)
                dve.wait_ge(S["a_max"], m)
                if cur:
                    dve.wait_ge(S["a_turned"], n)
                dve.tensor_tensor(p_s[0:nxt], scores, mx[0:nxt].unsqueeze(2).to_broadcast([nxt, XH, MEM]), ALU.subtract).then_inc(S["a_shifted"], 1)

        def attention_pe(pe, t, cur, nxt, group, next_group):
            n, m = counts(pe, t)
            if nxt:
                pe.wait_ge(S["a_q"], m)
                if cur:
                    pe.wait_ge(S["a_shifted"], n)
                for h in range(XH):
                    for k in range(2):
                        mm = pe.matmul(ps[0:nxt, h // 2, (h % 2) * MEM:(h % 2 + 1) * MEM], q_s[:, 2 * h + k, 0:nxt], kT[next_group][:, 2 * h + k, :],
                                       start=(k == 0), stop=(k == 1))
                mm.then_inc(S["a_scores"], 1)
            if cur:
                pe.wait_ge(S["a_p"], n)
                for h in range(XH):
                    for j in range(2):
                        b = 2 * h + j
                        mm = pe.transpose(ps[:, 2 + b // 4, (b % 4) * P:(b % 4) * P + cur], p_s[0:cur, h, j * P:(j + 1) * P], ident[0:cur, 0:cur])
                mm.then_inc(S["a_turned"], 1)
                pe.wait_ge(S["a_pT"], n)
                pe.wait_ge(S["a_tile_done"], n)
                for b in range(FT):
                    for j in range(2):
                        mm = pe.matmul(ps[:, 4 + b // 4, (b % 4) * P:(b % 4) * P + cur], v_mem[group][:, j, b * P:(b + 1) * P], pT[:, 2 * (b // 2) + j, 0:cur],
                                       start=(j == 0), stop=(j == 1))
                mm.then_inc(S["a_o"], 1)

        tiles = SEQ // P
        with nc.Block() as block:
            @block.gpsimd
            def _(pool):
                pool.sem_inc(S["a_tile_done"], 1)

            @block.scalar
            def _(act):
                attention_act(act, -1, 0, P)
                with act.Fori(0, tiles - 1) as t:
                    attention_act(act, t, P, P)
                attention_act(act, tiles - 1, P, DEC)
                attention_act(act, tiles, DEC, 0)

            @block.vector
            def _(dve):
                attention_dve(dve, -1, 0, P)
                with dve.Fori(0, tiles - 1) as t:
                    attention_dve(dve, t, P, P)
                attention_dve(dve, tiles - 1, P, DEC)
                attention_dve(dve, tiles, DEC, 0)

            @block.tensor
            def _(pe):
                attention_pe(pe, -1, 0, P, 0, 0)
                with pe.Fori(0, tiles - 1) as t:
                    attention_pe(pe, t, P, P, 0, 0)
                attention_pe(pe, tiles - 1, P, DEC, 0, 1)
                attention_pe(pe, tiles, DEC, 0, 1, 1)

        S.end_stage()

        l_sp, l_pe, l_leave = linear([("add", I["wo_x"][0], 0, 4, B3, H)])
        n_act, n_pe, n_dve = norm_stage("ffn", whole(H), whole(XN), lambda f: col("norm_ffn_g", f), N, sq_b)
        eroom = Room(scr[:, :], SCR)
        NR = GROUPS + EXPERTS
        h_tok = eroom.take(TT, D)
        w_route = eroom.take(FT, NR)
        b_route = eroom.take(NR)
        lg = eroom.take(TT, NR)
        gmax, gsum, m1, m2, e2, wsum, w1, w2 = (eroom.take(TT) for _ in range(8))
        slot_f = [eroom.take(TT) for _ in range(TOP_K)]
        ge, oh_g, seen_g, one_g = (eroom.take(TT, GROUPS) for _ in range(4))
        le4 = eroom.take(TT * GROUPS, PER_GROUP)
        lec, o1, o2, seen = (eroom.take(TT, PER_GROUP) for _ in range(4))
        one_e = eroom.take(TT, PER_GROUP)
        pick = [eroom.take(TT, EXPERTS) for _ in range(TOP_K)]
        both, slot_e = eroom.take(TT, EXPERTS), eroom.take(TT, EXPERTS)
        count, blocks_e, ends_e, base_e = (eroom.take(EXPERTS) for _ in range(4))
        before = eroom.take(P)
        blk_no = eroom.take(NBLK)
        over_e = eroom.take(NBLK, EXPERTS)
        owner_f = eroom.take(NBLK)
        x_rows = shaped(flat, B4 * BW, (TT, D))
        slot_i = [ctx.enter_context(nc.sbuf_tensor(f"slot_i{k}", [P, TT], U32)) for k in range(TOP_K)]
        owner = ctx.enter_context(nc.sbuf_tensor("owner", [1, NBLK], I32))
        blk_int = ctx.enter_context(nc.sbuf_tensor("blk_int", [1, NBLK], I32))
        exp_l = lg[:, :, GROUPS:NR]

        def wide(v, n):
            return v.unsqueeze(2).to_broadcast([P, v.shape[1], n])

        def first_of(dve, name, eq, scan_mask, seen_):
            dve.wait_ge(S[name + "_eq"], 1)
            dve.tensor_tensor_scan(flat2(seen_), flat2(scan_mask), flat2(eq), 0.0, ALU.mult, ALU.add).then_inc(S[name + "_seen"], 1)
            dve.wait_ge(S[name + "_seen"], 1)
            dve.scalar_tensor_tensor(out=eq, in0=seen_, scalar=1.0, in1=eq, op0=ALU.is_equal, op1=ALU.mult).then_inc(S[name], 1)
            dve.wait_ge(S[name], 1)

        def tokens(t):
            return P if t < TT - 1 else DEC

        def count_tokens(pe):
            pe.wait_ge(S["picks"], 1)
            pe.wait_ge(S["before"], 1)
            for t in range(TT):
                m = tokens(t)
                pe.matmul(bank[3][:, 0:EXPERTS], ones[0:m, :], both[0:m, t, :], start=(t == 0), stop=(t == TT - 1))
            for t in range(TT):
                m = tokens(t)
                out = bank[3][0:m, (t + 1) * EXPERTS:(t + 2) * EXPERTS]
                for u in range(t):
                    pe.matmul(out, ones[:, 0:m], both[:, u, :], start=(u == 0), stop=False)
                mm = pe.matmul(out, before[0:m, 0:m], both[0:m, t, :], start=(t == 0), stop=True)
            mm.then_inc(S["counted"], 1)

        turns = [(XN, x_rows, j) for j in range(2 * TT)] + [(H, h_tok, j) for j in range(2 * TT)]

        with nc.Block() as block:
            @block.sync
            def _(sp):
                sp.dma_start(w_route[:, :, 0:GROUPS], I["router_group_w"][0].rearrange("(k p) n -> p k n", p=P)).then_inc(S["route_in"], 16)
                sp.dma_start(w_route[:, :, GROUPS:NR], I["router_expert_w"][0].rearrange("(k p) n -> p k n", p=P)).then_inc(S["route_in"], 16)
                sp.dma_start(b_route[0:1, 0:GROUPS], I["router_group_b"]).then_inc(S["route_in"], 16)
                sp.dma_start(b_route[0:1, GROUPS:NR], I["router_expert_b"].rearrange("a g e -> a (g e)")).then_inc(S["route_in"], 16)
                l_sp(sp)

            @block.scalar
            def _(act):
                act.wait_ge(S["banks0_free"], used[0] + 1)
                act.wait_ge(S["banks1_free"], used[0] + 1)
                n_act(act)
                for i, (base, dst, j) in enumerate(turns):
                    act.wait_ge(S["rows_turned"], i + 1)
                    m = tokens(j // 2)
                    act.copy(dst[0:m, j // 2, (j % 2) * 512:(j % 2 + 1) * 512], ps[0:m, 4 + i % 4, :]).then_inc(S["rows_kept"], 1)
                    if i == 9:
                        act.wait_ge(S["g_shifted"], 1)
                        act.activation(ge, ge, ACT.Exp).then_inc(S["g_exp"], 1)
                    if i == 12:
                        act.wait_ge(S["e_shifted"], 1)
                        act.activation(e2, e2, ACT.Exp).then_inc(S["e_exp"], 1)

            @block.gpsimd
            def _(pool):
                pool.memset(one_g, 1.0).then_inc(S["scan_ones"], 1)
                pool.memset(one_e, 1.0).then_inc(S["scan_ones"], 1)
                pool.memset(lg, 0.0).then_inc(S["lg_zero"], 1)
                pool.memset(before, 1.0).then_inc(S["scan_ones"], 1)
                pool.iota(blk_int[:, :], pattern=[[1, NBLK]], base=0, channel_multiplier=0).then_inc(S["blk_int"], 1)
                pool.wait_ge(S["scan_ones"], 3)
                pool.memset(one_g[:, :, 0:1], 0.0).then_inc(S["scan_masks"], 1)
                pool.memset(one_e[:, :, 0:1], 0.0).then_inc(S["scan_masks"], 1)
                pool.affine_select(out=before, in_=before, compare_op=ALU.is_ge, fill=0.0, base=-1,
                                   pattern=[[1, P]], channel_multiplier=-1).then_inc(S["before"], 1)
                pool.wait_ge(S["rows_kept"], 2 * TT)
                pool.wait_ge(S["slots_known"], TOP_K)
                for t in range(TT):
                    for k in range(TOP_K):
                        m = tokens(t)
                        pool.indirect_dma_start(x_slots, bass.IndirectOffsetOnAxis(slot_i[k][0:m, t:t + 1], 0), x_rows[0:m, t, :], None).then_inc(S["scattered"], 16)
                pool.wait_ge(S["scattered"], 16 * TT * TOP_K)

            @block.tensor
            def _(pe):
                l_pe(pe)
                n_pe(pe)
                pe.wait_ge(S["ffn_normed"], FT)
                pe.wait_ge(S["route_in"], 64)
                for t in range(TT):
                    m = tokens(t)
                    out = bank[2][0:m, t * NR:(t + 1) * NR]
                    for k in range(FT):
                        pe.matmul(out, arena[:, XN + k, 1 + t * P:1 + t * P + m], w_route[:, k, :], start=(k == 0), stop=False)
                    mm = pe.matmul(out, ones[0:1, 0:m], b_route[0:1, :], start=False, stop=True)
                mm.then_inc(S["logits"], 1)
                for i, (base, dst, j) in enumerate(turns):
                    m = tokens(j // 2)
                    if i >= 4:
                        pe.wait_ge(S["rows_kept"], i - 3)
                    if i == 2 * TT:
                        count_tokens(pe)
                    for f in range(4):
                        mm = pe.transpose(ps[0:m, 4 + i % 4, f * P:(f + 1) * P],
                                          arena[:, base + (j % 2) * 4 + f, 1 + (j // 2) * P:1 + (j // 2) * P + m], ident[:, :])
                    mm.then_inc(S["rows_turned"], 1)

            @block.vector
            def _(dve):
                l_leave(dve, True)
                n_dve(dve)
                dve.wait_ge(S["logits"], 1)
                dve.wait_ge(S["lg_zero"], 1)
                dve.tensor_copy(lg[:, 0:TT - 1, :], bank[2][:, 0:(TT - 1) * NR].rearrange("p (t n) -> p t n", t=TT - 1)).then_inc(S["lg"], 1)
                dve.tensor_copy(lg[0:DEC, TT - 1, :], bank[2][0:DEC, (TT - 1) * NR:TT * NR]).then_inc(S["lg"], 1)
                dve.wait_ge(S["lg"], 2)
                dve.tensor_reduce(gmax, lg[:, :, 0:GROUPS], AX_X, ALU.max).then_inc(S["gmax"], 1)
                dve.wait_ge(S["gmax"], 1)
                dve.tensor_tensor(ge, lg[:, :, 0:GROUPS], wide(gmax, GROUPS), ALU.subtract).then_inc(S["g_shifted"], 1)
                dve.tensor_tensor(oh_g, lg[:, :, 0:GROUPS], wide(gmax, GROUPS), ALU.is_equal).then_inc(S["group_eq"], 1)
                dve.wait_ge(S["scan_masks"], 2)
                first_of(dve, "group", oh_g, one_g, seen_g)
                oh_ge = flat2(oh_g).unsqueeze(2).to_broadcast([P, TT * GROUPS, PER_GROUP])
                by_group = "p (t g) e -> p t g e"
                dve.tensor_tensor(le4.rearrange(by_group, t=TT), exp_l.rearrange("p t (g e) -> p t g e", g=GROUPS),
                                  oh_ge.rearrange(by_group, t=TT), ALU.mult).then_inc(S["le4"], 1)
                dve.wait_ge(S["le4"], 1)
                dve.tensor_reduce(lec, le4.rearrange("p (t g) e -> p t e g", t=TT), AX_X, ALU.add).then_inc(S["lec"], 1)
                dve.wait_ge(S["lec"], 1)
                dve.tensor_reduce(m1, lec, AX_X, ALU.max).then_inc(S["m1"], 1)
                dve.wait_ge(S["m1"], 1)
                dve.tensor_tensor(o1, lec, wide(m1, PER_GROUP), ALU.is_equal).then_inc(S["top1_eq"], 1)
                first_of(dve, "top1", o1, one_e, seen)
                dve.scalar_tensor_tensor(out=lec, in0=o1, scalar=-1e30, in1=lec, op0=ALU.mult, op1=ALU.add).then_inc(S["lec2"], 1)
                dve.wait_ge(S["lec2"], 1)
                dve.tensor_reduce(m2, lec, AX_X, ALU.max).then_inc(S["m2"], 1)
                dve.wait_ge(S["m2"], 1)
                dve.tensor_tensor(e2, m2, m1, ALU.subtract).then_inc(S["e_shifted"], 1)
                dve.tensor_tensor(o2, lec, wide(m2, PER_GROUP), ALU.is_equal).then_inc(S["top2_eq"], 1)
                first_of(dve, "top2", o2, one_e, seen)
                for k, o in enumerate((o1, o2)):
                    dve.tensor_tensor(pick[k].rearrange("p t (g e) -> p t g e", g=GROUPS), oh_ge.rearrange(by_group, t=TT),
                                      o.unsqueeze(2).to_broadcast([P, TT, GROUPS, PER_GROUP]), ALU.mult).then_inc(S["pick"], 1)
                dve.wait_ge(S["pick"], TOP_K)
                dve.tensor_tensor(both, pick[0], pick[1], ALU.add).then_inc(S["picks"], 1)
                dve.memset(blocks_e, 0.0).then_inc(S["blocks"], 1)
                dve.wait_ge(S["counted"], 1)
                dve.tensor_copy(count, bank[3][:, 0:EXPERTS]).then_inc(S["count"], 1)
                dve.wait_ge(S["count"], 1)
                for b in range(MAXB):
                    dve.wait_ge(S["blocks"], b + 1)
                    dve.scalar_tensor_tensor(out=blocks_e, in0=count, scalar=float(b * BLK), in1=blocks_e, op0=ALU.is_gt, op1=ALU.add).then_inc(S["blocks"], 1)
                dve.wait_ge(S["blocks"], MAXB + 1)
                dve.tensor_tensor_scan(ends_e, ones[:, 0:EXPERTS], blocks_e, 0.0, ALU.mult, ALU.add).then_inc(S["ends"], 1)
                dve.wait_ge(S["ends"], 1)
                dve.tensor_tensor(base_e, ends_e, blocks_e, ALU.subtract).then_inc(S["base"], 1)
                dve.wait_ge(S["base"], 1)
                for t in range(TT):
                    m = tokens(t)
                    dve.scalar_tensor_tensor(out=slot_e[0:m, t, :], in0=base_e[0:m], scalar=float(BLK), in1=bank[3][0:m, (t + 1) * EXPERTS:(t + 2) * EXPERTS],
                                             op0=ALU.mult, op1=ALU.add).then_inc(S["slot_e"], 1)
                dve.memset(slot_e[DEC:2 * DEC, TT - 1, :], 0.0).then_inc(S["slot_e"], 1)
                dve.memset(slot_e[2 * DEC:P, TT - 1, :], 0.0).then_inc(S["slot_e"], 1)
                dve.wait_ge(S["slot_e"], TT + 2)
                for k in range(TOP_K):
                    dve.tensor_tensor(pick[k], pick[k], slot_e, ALU.mult).then_inc(S["slot_k"], 1)
                    dve.wait_ge(S["slot_k"], 2 * k + 1)
                    dve.tensor_reduce(slot_f[k], pick[k], AX_X, ALU.add).then_inc(S["slot_k"], 1)
                    dve.wait_ge(S["slot_k"], 2 * k + 2)
                    dve.tensor_copy(slot_i[k][:, :], slot_f[k]).then_inc(S["slots_known"], 1)
                dve.wait_ge(S["blk_int"], 1)
                dve.tensor_copy(blk_no[0:1], blk_int[:, :]).then_inc(S["blk_no"], 1)
                dve.wait_ge(S["blk_no"], 1)
                dve.tensor_tensor(over_e[0:1], ends_e[0:1].unsqueeze(1).to_broadcast([1, NBLK, EXPERTS]),
                                  blk_no[0:1].unsqueeze(2).to_broadcast([1, NBLK, EXPERTS]), ALU.is_le).then_inc(S["over_e"], 1)
                dve.wait_ge(S["over_e"], 1)
                dve.tensor_reduce(owner_f[0:1], over_e[0:1], AX_X, ALU.add).then_inc(S["owner_f"], 1)
                dve.wait_ge(S["owner_f"], 1)
                dve.tensor_scalar(owner[:, :], owner_f[0:1], float(EXPERTS - 1), None, ALU.min).then_inc(S["owner"], 1)
                dve.wait_ge(S["g_exp"], 1)
                dve.tensor_reduce(gsum, ge, AX_X, ALU.add).then_inc(S["gsum"], 1)
                dve.wait_ge(S["e_exp"], 1)
                dve.wait_ge(S["gsum"], 1)
                dve.scalar_tensor_tensor(out=wsum, in0=e2, scalar=1.0, in1=gsum, op0=ALU.add, op1=ALU.mult).then_inc(S["wsum"], 1)
                dve.wait_ge(S["wsum"], 1)
                dve.reciprocal(w1, wsum).then_inc(S["w1"], 1)
                dve.wait_ge(S["w1"], 1)
                dve.tensor_tensor(w2, w1, e2, ALU.mult).then_inc(S["w2"], 1)

        S.end_stage()

        wroom = Room(flat[:, 0:B4 * BW], B4 * BW)
        wg, wu, wd, xr, y_b = ([wroom.take(*sh) for _ in range(2)] for sh in ((FT, DE), (FT, DE), (2, D), (D,), (D,)))
        broom = Room(flat[:, B4 * BW:], 3 * FT * BW)
        xT, hid, gate_s = ([broom.take(*sh) for _ in range(2)] for sh in ((FT, BLK), (2, BLK), (2, BLK)))
        gain_rows = broom.take(D)
        ITER = NBLK // 2

        def owner_of(sp, i, s):
            return sp.value_load(owner[0:1, bass.ds(i * 2 + s, 1)], min_val=0, max_val=EXPERTS - 1)

        def load_x(sp, i, s):
            sp.wait_ge(S[f"m_turned{s}"], i + 1)
            sp.dma_start(xr[s][0:BLK], x_slots[bass.ds(i * (2 * BLK) + s * BLK, BLK), :]).then_inc(S[f"m_x{s}_in"], 16)

        def load_gate_up(sp, i, s):
            e = owner_of(sp, i, s)
            sp.wait_ge(S[f"m_gu{s}"], i + 1)
            for dst, w in ((wg[s], I["expert_w_gate"]), (wu[s], I["expert_w_up"])):
                sp.dma_start(dst, w[0][bass.ds(e, 1)].rearrange("e (k p) n -> p (e k) n", p=P)).then_inc(S[f"m_gu{s}_in"], 16)

        def load_down(sp, i, s):
            e = owner_of(sp, i, s)
            sp.wait_ge(S[f"m_down{s}"], i + 1)
            sp.dma_start(wd[s], I["expert_w_down"][0][bass.ds(e, 1)].rearrange("e (k p) n -> p (e k) n", p=P)).then_inc(S[f"m_d{s}_in"], 16)

        def turn_x(pe, i, s):
            pe.wait_ge(S[f"m_x{s}_in"], i * 16 + 16)
            pe.wait_ge(S["m_xT"], i * 2 + (s + 1))
            for f in range(FT):
                mm = pe.transpose(ps[:, f // 4, (f % 4) * P:(f % 4) * P + BLK], xr[s][0:BLK, f * P:(f + 1) * P], ident[0:BLK, 0:BLK])
            mm.then_inc(S[f"m_turned{s}"], 1)

        def gate_up(pe, i, s):
            pe.wait_ge(S[f"m_gu{s}_in"], i * 32 + 32)
            pe.wait_ge(S["m_xT"], i * 2 + (s + 2))
            pe.wait_ge(S["m_hid"], i * 2 + (s + 1))
            for w, c in ((wg[s], 0), (wu[s], 2)):
                for o in range(2):
                    for f in range(FT):
                        mm = pe.matmul(bank[2 + s][:, (c + o) * P:(c + o) * P + BLK], w[:, f, o * P:(o + 1) * P], xT[s][:, f, :],
                                       start=(f == 0), stop=(f == FT - 1))
            mm.then_inc(S[f"m_gu{s}"], 1)

        def down(pe, i, s):
            pe.wait_ge(S[f"m_d{s}_in"], i * 16 + 16)
            pe.wait_ge(S["m_hid"], i * 2 + (s + 3))
            pe.wait_ge(S["m_y"], i * 2 + (s + 1))
            for c in range(2):
                for f in range(2):
                    mm = pe.matmul(bank[4 + 2 * s + c][0:BLK, :], hid[s][:, f, :], wd[s][:, f, c * 512:(c + 1) * 512], start=(f == 0), stop=(f == 1))
            mm.then_inc(S[f"m_down{s}"], 1)

        def cols4(s):
            return bank[2 + s].rearrange("p (c n) -> p c n", c=4)[:, :, 0:BLK]

        def keep_x(act, i, s):
            act.wait_ge(S[f"m_turned{s}"], i + 2)
            act.copy(xT[s], ps[:, 0:2, :].rearrange("p b (f n) -> p (b f) n", f=4)[:, :, 0:BLK]).then_inc(S["m_xT"], 1)

        def silu(act, i, s):
            act.wait_ge(S[f"m_gu{s}"], i + 2)
            act.activation(gate_s[s], cols4(s)[:, 0:2, :], ACT.Silu).then_inc(S[f"m_silu{s}"], 1)

        def hidden(dve, i, s):
            dve.wait_ge(S[f"m_silu{s}"], i + 1)
            dve.tensor_tensor(hid[s], gate_s[s], cols4(s)[:, 2:4, :], ALU.mult).then_inc(S["m_hid"], 1)

        def keep_y(dve, i, s):
            dve.wait_ge(S[f"m_down{s}"], i + 2)
            dve.wait_ge(S[f"m_y{s}_free"], i + 1)
            dve.tensor_copy(y_b[s][0:BLK].rearrange("p (c n) -> p c n", c=2), ps[0:BLK, 4 + 2 * s:6 + 2 * s, :]).then_inc(S["m_y"], 1)

        with nc.Block() as block:
            @block.sync
            def _(sp):
                load_x(sp, 0, 0)
                load_x(sp, 0, 1)
                load_gate_up(sp, 0, 0)
                with sp.Fori(0, ITER - 1) as i:
                    for s in range(2):
                        load_x(sp, i + 1, s)
                        load_gate_up(sp, i + s, 1 - s)
                        load_down(sp, i, s)
                load_gate_up(sp, ITER - 1, 1)
                load_down(sp, ITER - 1, 0)
                load_down(sp, ITER - 1, 1)

            @block.gpsimd
            def _(pool):
                pool.dma_start(gain_rows, I["norm_final_g"].partition_broadcast(P)).then_inc(S["slot_gain_in"], 16)
                with pool.Fori(0, ITER) as i:
                    for s in range(2):
                        pool.wait_ge(S["m_y"], i * 2 + (s + 3))
                        pool.dma_start(y_slots[bass.ds(i * (2 * BLK) + s * BLK, BLK), :], y_b[s][0:BLK]).then_inc(S[f"m_y{s}_out"], 16)
                        pool.wait_ge(S[f"m_y{s}_out"], i * 16 + 16)
                        pool.sem_inc(S[f"m_y{s}_free"], 1)

            @block.scalar
            def _(act):
                keep_x(act, 0, 0)
                keep_x(act, 0, 1)
                silu(act, 0, 0)
                with act.Fori(0, ITER - 1) as i:
                    for s in range(2):
                        keep_x(act, i + 1, s)
                        silu(act, i + s, 1 - s)
                silu(act, ITER - 1, 1)

            @block.tensor
            def _(pe):
                for name, n in (("m_xT", 1), ("m_hid", 2), ("m_y", 2), ("m_y0_free", 1), ("m_y1_free", 1), ("m_turned0", 1),
                                ("m_turned1", 1), ("m_gu0", 1), ("m_gu1", 1), ("m_down0", 1), ("m_down1", 1)):
                    pe.sem_inc(S[name], n)
                turn_x(pe, 0, 0)
                turn_x(pe, 0, 1)
                gate_up(pe, 0, 0)
                with pe.Fori(0, ITER - 1) as i:
                    for s in range(2):
                        turn_x(pe, i + 1, s)
                        gate_up(pe, i + s, 1 - s)
                        down(pe, i, s)
                gate_up(pe, ITER - 1, 1)
                down(pe, ITER - 1, 0)
                down(pe, ITER - 1, 1)

            @block.vector
            def _(dve):
                hidden(dve, 0, 0)
                with dve.Fori(0, ITER - 1) as i:
                    for s in range(2):
                        hidden(dve, i + s, 1 - s)
                        keep_y(dve, i, s)
                hidden(dve, ITER - 1, 1)
                keep_y(dve, ITER - 1, 0)
                keep_y(dve, ITER - 1, 1)

        S.end_stage()

        froom = Room(flat[:, 0:B4 * BW], B4 * BW)
        res = [[froom.take(D) for _ in range(TOP_K)] for _ in range(TT)]
        y_sq, ss, rstd = froom.take(D), froom.take(TT), froom.take(TT)

        with nc.Block() as block:
            @block.gpsimd
            def _(pool):
                for t in range(TT):
                    for k in range(TOP_K):
                        m = tokens(t)
                        pool.indirect_dma_start(res[t][k][0:m], None, y_slots, bass.IndirectOffsetOnAxis(slot_i[k][0:m, t:t + 1], 0)).then_inc(S[f"y_in{t}"], 16)

            @block.vector
            def _(dve):
                dve.wait_ge(S["slot_gain_in"], 16)
                for t in range(TT + 1):
                    if t < TT:
                        m = tokens(t)
                        dve.wait_ge(S[f"y_in{t}"], 16 * TOP_K)
                        for k, w in enumerate((w1, w2)):
                            if k:
                                dve.wait_ge(S["y_sum"], 2 * t + 1)
                            dve.scalar_tensor_tensor(out=h_tok[0:m, t, :], in0=res[t][k][0:m], scalar=w[0:m, t:t + 1], in1=h_tok[0:m, t, :],
                                                     op0=ALU.mult, op1=ALU.add).then_inc(S["y_sum"], 1)
                    if t:
                        u = t - 1
                        m = tokens(u)
                        dve.wait_ge(S["y_rms"], u + 1)
                        dve.reciprocal(rstd[0:m, u:u + 1], rstd[0:m, u:u + 1]).then_inc(S["y_rrms"], 1)
                        dve.wait_ge(S["y_rrms"], u + 1)
                        dve.scalar_tensor_tensor(out=h_tok[0:m, u, :], in0=h_tok[0:m, u, :], scalar=rstd[0:m, u:u + 1], in1=gain_rows[0:m],
                                                 op0=ALU.mult, op1=ALU.mult).then_inc(S["y_done"], 1)

            @block.scalar
            def _(act):
                for t in range(TT):
                    m = tokens(t)
                    act.wait_ge(S["y_sum"], 2 * t + 2)
                    act.activation(y_sq[0:m], h_tok[0:m, t, :], ACT.Square, accum_out=ss[0:m, t:t + 1]).then_inc(S["y_ss"], 1)
                    act.wait_ge(S["y_ss"], t + 1)
                    act.activation(rstd[0:m, t:t + 1], ss[0:m, t:t + 1], ACT.Sqrt, bias=eps_c[0:m], scale=1.0 / D).then_inc(S["y_rms"], 1)

            @block.sync
            def _(sp):
                for t in range(TT):
                    sp.wait_ge(S["y_done"], t + 1)
                    dst = O["y_prompt"][0, t * P:(t + 1) * P, :] if t < TT - 1 else O["y_sample"][0]
                    sp.dma_start(dst, h_tok[0:tokens(t), t, :]).then_inc(S["y_out"], 16)
                sp.wait_ge(S["y_out"], 16 * TT)


_INS = ["x_prompt", "x_sample", "mem_prompt", "cache_mem_k", "cache_mem_v", "state_hgrn", "state_rwkv", "state_rwkv_shift",
        "norm_mix_g", "w_in", "hgrn_lower_bounds", "hgrn_norm_g", "rwkv_mu", "rwkv_w0", "rwkv_w2", "rwkv_a0", "rwkv_a2",
        "rwkv_g2", "rwkv_k_k", "rwkv_k_a", "rwkv_r_k", "rwkv_ln_g", "rwkv_ln_b", "w_out", "norm_x_g", "norm_mem_g",
        "wq_x", "wk_x", "wv_x", "wo_x", "norm_ffn_g", "router_group_w", "router_group_b", "router_expert_w",
        "router_expert_b", "expert_w_gate", "expert_w_up", "expert_w_down", "norm_final_g"]
_OUTS = [("y_prompt", (1, SEQ, D)), ("y_sample", (1, DEC, D)),
         ("mem_k", (1, 1, MEM, XH, D // XH)), ("mem_v", (1, 1, MEM, XH, D // XH)),
         ("hgrn_prompt", (1, 1, HEADS, P, P)), ("hgrn_sample", (1, 1, HEADS, P, P)),
         ("rwkv_prompt", (1, 1, 16, 64, 64)), ("rwkv_sample", (1, 1, 16, 64, 64)),
         ("shift_prompt", (1, 1, 1, N_RWKV)), ("shift_sample", (1, 1, 1, N_RWKV))]


def kernel(**inputs):
    import numpy as _np
    import concourse.bacc as _bacc
    from concourse.bass_utils import run_bass_kernel_spmd as _run

    nc = _bacc.Bacc("TRN2", target_bir_lowering=False, num_devices=1)
    arrays, ins, outs = {}, {}, {}
    for name in _INS:
        a = _np.ascontiguousarray(inputs[name])
        arrays[f"in_{name}"] = a
        ins[name] = nc.dram_tensor(f"in_{name}", a.shape, F32, kind="ExternalInput").ap()
    for name, shape in _OUTS:
        outs[name] = nc.dram_tensor(f"out_{name}", shape, F32, kind="ExternalOutput").ap()
    build(nc, ins, outs)
    r = _run(nc, [arrays], core_ids=[0])
    return tuple(r.results[0][f"out_{name}"] for name, _ in _OUTS)
```
